# Optimizing a Trainium2 kernel written in Bass

```python
import jax, jax.numpy as jnp
from jax import lax
import numpy as np

D_MODEL = 1024
BATCH = 1
SEQ = 512
DEPTH = 1
DEC_BATCH = 8
DEC_SEQ = 1
PAST_LEN = 4096
PAGE_SIZE = 128

SB_HEADS = 8
SB_HEAD_DIM = 64
SB_WIDTH = SB_HEADS * SB_HEAD_DIM
SB_BLOCK = 128
SB_BIAS_HI = -2.0
SB_BIAS_LO = -10.0
GLA_HEADS = 4
GLA_DK = 64
GLA_DV = 128
GLA_KW = GLA_HEADS * GLA_DK
GLA_VW = GLA_HEADS * GLA_DV
GLA_GATE_RANK = 16
GLA_GATE_TAU = 16.0
GLA_CHUNK = 64
PEER_HEADS = 8
PEER_N_KEYS = 128
PEER_N_EXPERTS = PEER_N_KEYS * PEER_N_KEYS
PEER_TOPK = 16
PEER_QDIM = 256
PEER_HALF = PEER_QDIM // 2
PEER_BLOCK = 256
PLE_DIM = 256
RMS_EPS = 1e-6

_IN_SIZES = (SB_WIDTH, SB_WIDTH, SB_WIDTH,
             GLA_KW, GLA_KW, GLA_VW, GLA_VW,
             GLA_GATE_RANK,
             D_MODEL, D_MODEL)
IN_COLS = sum(_IN_SIZES)
_IN_SPLITS = tuple(int(s) for s in np.cumsum(_IN_SIZES)[:-1])

kernel_name = 'hybrid_stickbreak_gla_peer_step'

def rmsnorm(x, g):
    xf = x.astype(jnp.float32)
    y = xf * lax.rsqrt(jnp.mean(xf * xf, axis=-1, keepdims=True) + RMS_EPS)
    return (y * g.astype(jnp.float32)).astype(x.dtype)

def sb_attend(q, k_segs, v_segs, q_off, k_pos, bias):
    b, tq, h, d = q.shape
    qb = min(SB_BLOCK, tq)
    nq = -(-tq // qb)
    qp = jnp.pad(q, ((0, 0), (0, nq * qb - tq), (0, 0), (0, 0)))
    q_blocks = qp.reshape(b, nq, qb, h, d).transpose(1, 0, 2, 3, 4)
    pos_blocks = (q_off + jnp.arange(nq * qb)).reshape(nq, qb)
    split_pts = [int(s) for s in np.cumsum([kk.shape[1] for kk in k_segs])[:-1]]
    scale = d ** -0.5
    bias_f = bias.astype(jnp.float32)[None, :, None, None]

    def one_block(args):
        qblk, pblk = args
        z = jnp.concatenate([jnp.einsum('bqhd,bkhd->bhqk', qblk, kk) for kk in k_segs],
                            axis=-1).astype(jnp.float32) * scale + bias_f
        mask = k_pos[None, :] < pblk[:, None]
        log_beta = jax.nn.log_sigmoid(z)
        log_keep = jnp.where(mask, jax.nn.log_sigmoid(-z), 0.0)
        later = lax.cumsum(log_keep, axis=3, reverse=True) - log_keep
        w = jnp.where(mask, jnp.exp(log_beta + later), 0.0).astype(qblk.dtype)
        ws = jnp.split(w, split_pts, axis=-1)
        return sum(jnp.einsum('bhqk,bkhd->bqhd', wi, vi) for wi, vi in zip(ws, v_segs))

    out = lax.map(one_block, (q_blocks, pos_blocks))
    return out.transpose(1, 0, 2, 3, 4).reshape(b, nq * qb, h, d)[:, :tq]

def gla_scan(q, k, v, log_a, s0):
    b, t, h, dk = q.shape
    dv = v.shape[-1]
    c = min(GLA_CHUNK, t)
    n = -(-t // c)
    pad = ((0, 0), (0, n * c - t), (0, 0), (0, 0))

    def blocks(a):
        a = jnp.pad(a.astype(jnp.float32), pad)
        return a.reshape(b, n, c, h, a.shape[-1]).transpose(1, 0, 3, 2, 4)

    causal = jnp.tril(jnp.ones((c, c), dtype=bool))

    def step(s, inp):
        qc, kc, vc, ac = inp
        cum = jnp.cumsum(ac, axis=2)
        o = jnp.einsum('bhtd,bhde->bhte', qc * jnp.exp(cum), s)
        diff = jnp.where(causal[:, :, None], cum[:, :, :, None, :] - cum[:, :, None, :, :], -jnp.inf)
        scores = jnp.einsum('bhtd,bhtsd,bhsd->bhts', qc, jnp.exp(diff), kc)
        o = o + jnp.einsum('bhts,bhse->bhte', scores, vc)
        last = cum[:, :, -1:, :]
        s = jnp.exp(last[:, :, 0, :])[..., None] * s + jnp.einsum('bhsd,bhse->bhde', kc * jnp.exp(last - cum), vc)
        return s, o

    s_fin, o = lax.scan(step, s0.astype(jnp.float32), (blocks(q), blocks(k), blocks(v), blocks(log_a)))
    o = o.transpose(1, 0, 3, 2, 4).reshape(b, n * c, h, dv)[:, :t]
    return o.astype(v.dtype), s_fin

def peer(x, w_q, sub_keys, expert_u, expert_v):
    t, d = x.shape
    blk = min(PEER_BLOCK, t)
    nb = -(-t // blk)
    xb = jnp.pad(x, ((0, nb * blk - t), (0, 0))).reshape(nb, blk, d)

    def one_block(xc):
        q = (xc @ w_q).reshape(blk, PEER_HEADS, 2, PEER_HALF)
        s = jnp.einsum('thcd,hcnd->thcn', q, sub_keys).astype(jnp.float32)
        s1, i1 = lax.top_k(s[:, :, 0], PEER_TOPK)
        s2, i2 = lax.top_k(s[:, :, 1], PEER_TOPK)
        cand = (s1[..., :, None] + s2[..., None, :]).reshape(blk, PEER_HEADS, PEER_TOPK * PEER_TOPK)
        top_s, top_c = lax.top_k(cand, PEER_TOPK)
        e = (jnp.take_along_axis(i1, top_c // PEER_TOPK, axis=-1) * PEER_N_KEYS
             + jnp.take_along_axis(i2, top_c % PEER_TOPK, axis=-1))
        g = jax.nn.softmax(top_s, axis=-1)
        act = jax.nn.gelu(jnp.einsum('td,thkd->thk', xc, expert_u[e]).astype(jnp.float32), approximate=False)
        return jnp.einsum('thk,thkd->td', (g * act).astype(xc.dtype), expert_v[e])

    y = lax.map(one_block, xb)
    return y.reshape(nb * blk, d)[:t]

def trunk_layer(h, p, q_off, past_k, past_v, s0, norm1_g, w_in, b_gate, qa_norm_g, ka_norm_g, sb_bias,
                w_alpha, b_alpha, ob_norm_g, w_up_a, w_up_b, w_o, norm2_g, w_peer_q, peer_sub_keys,
                expert_u, expert_v, norm3_g, w_ple, w_ple_gate):
    bsz, t, _ = h.shape
    xn = rmsnorm(h, norm1_g)
    z = xn @ w_in
    qa, ka, va, qb, kb, vb, rb, ab, gza, gzb = jnp.split(z, _IN_SPLITS, axis=-1)
    qa = rmsnorm(qa.reshape(bsz, t, SB_HEADS, SB_HEAD_DIM), qa_norm_g)
    ka = rmsnorm(ka.reshape(bsz, t, SB_HEADS, SB_HEAD_DIM), ka_norm_g)
    va = va.reshape(bsz, t, SB_HEADS, SB_HEAD_DIM)
    new_pos = q_off + jnp.arange(t)
    if past_k is None:
        k_segs, v_segs, k_pos = (ka,), (va,), new_pos
    else:
        k_segs, v_segs = (past_k, ka), (past_v, va)
        k_pos = jnp.concatenate([jnp.arange(past_k.shape[1]), new_pos])
    ya = sb_attend(qa, k_segs, v_segs, q_off, k_pos, sb_bias).reshape(bsz, t, SB_WIDTH)
    qb = qb.reshape(bsz, t, GLA_HEADS, GLA_DK) * (GLA_DK ** -0.5)
    kb = kb.reshape(bsz, t, GLA_HEADS, GLA_DK)
    vb = vb.reshape(bsz, t, GLA_HEADS, GLA_DV)
    log_a = (jax.nn.log_sigmoid((ab @ w_alpha + b_alpha).astype(jnp.float32)) / GLA_GATE_TAU
             ).reshape(bsz, t, GLA_HEADS, GLA_DK)
    ob, s_new = gla_scan(qb, kb, vb, log_a, s0)
    yb = rmsnorm(ob, ob_norm_g).reshape(bsz, t, GLA_VW) * jax.nn.silu(rb)
    ga = jax.nn.sigmoid(gza + b_gate[0])
    gb = jax.nn.sigmoid(gzb + b_gate[1])
    h = h + (ga * (ya @ w_up_a) + gb * (yb @ w_up_b)) @ w_o
    h = h + peer(rmsnorm(h, norm2_g).reshape(bsz * t, D_MODEL), w_peer_q, peer_sub_keys,
                 expert_u, expert_v).reshape(bsz, t, D_MODEL)
    h = h + (p @ w_ple) * jax.nn.sigmoid(rmsnorm(h, norm3_g) @ w_ple_gate)
    return h, ka, va, s_new

def setup_inputs(seed: int = 0) -> dict:
    key = jax.random.key(seed)
    ks = jax.random.split(key, 32)
    f = jnp.float32
    n_pages = PAST_LEN // PAGE_SIZE
    n_used = DEC_BATCH * n_pages
    n_pool = n_used + n_used // 4

    def nrm(k, shape, scale):
        return jax.random.normal(k, shape, f) * scale

    def gain(k, shape):
        return 1.0 + 0.02 * jax.random.normal(k, shape, f)

    page_table = jax.random.permutation(ks[7], n_pool)[:n_used].reshape(DEC_BATCH, n_pages).astype(jnp.int32)
    sb_bias = (jnp.linspace(SB_BIAS_HI, SB_BIAS_LO, SB_HEADS, dtype=f)[None, :]
               + nrm(ks[27], (DEPTH, SB_HEADS), 0.1))
    return {
        'x_prompt': nrm(ks[0], (BATCH, SEQ, D_MODEL), 1.0),
        'x_sample': nrm(ks[1], (DEC_BATCH, DEC_SEQ, D_MODEL), 1.0),
        'p_prompt': nrm(ks[2], (DEPTH, BATCH, SEQ, PLE_DIM), 1.0),
        'p_sample': nrm(ks[3], (DEPTH, DEC_BATCH, DEC_SEQ, PLE_DIM), 1.0),
        'cache_k': nrm(ks[4], (DEPTH, n_pool, PAGE_SIZE, SB_HEADS, SB_HEAD_DIM), 1.0),
        'cache_v': nrm(ks[5], (DEPTH, n_pool, PAGE_SIZE, SB_HEADS, SB_HEAD_DIM), 1.0),
        'state_gla': nrm(ks[6], (DEPTH, DEC_BATCH, GLA_HEADS, GLA_DK, GLA_DV), 0.3),
        'page_table': page_table,
        'norm1_g': gain(ks[8], (DEPTH, D_MODEL)),
        'w_in': nrm(ks[9], (DEPTH, D_MODEL, IN_COLS), D_MODEL ** -0.5),
        'b_gate': nrm(ks[10], (DEPTH, 2, D_MODEL), 0.1),
        'qa_norm_g': gain(ks[11], (DEPTH, SB_HEAD_DIM)),
        'ka_norm_g': gain(ks[12], (DEPTH, SB_HEAD_DIM)),
        'sb_bias': sb_bias,
        'w_alpha': nrm(ks[13], (DEPTH, GLA_GATE_RANK, GLA_KW), GLA_GATE_RANK ** -0.5),
        'b_alpha': nrm(ks[14], (DEPTH, GLA_KW), 0.1),
        'ob_norm_g': gain(ks[15], (DEPTH, GLA_DV)),
        'w_up_a': nrm(ks[16], (DEPTH, SB_WIDTH, D_MODEL), SB_WIDTH ** -0.5),
        'w_up_b': nrm(ks[17], (DEPTH, GLA_VW, D_MODEL), GLA_VW ** -0.5),
        'w_o': nrm(ks[18], (DEPTH, D_MODEL, D_MODEL), D_MODEL ** -0.5),
        'norm2_g': gain(ks[19], (DEPTH, D_MODEL)),
        'w_peer_q': nrm(ks[20], (DEPTH, D_MODEL, PEER_HEADS * PEER_QDIM), D_MODEL ** -0.5),
        'peer_sub_keys': nrm(ks[21], (DEPTH, PEER_HEADS, 2, PEER_N_KEYS, PEER_HALF), PEER_HALF ** -0.5),
        'expert_u': nrm(ks[22], (DEPTH, PEER_N_EXPERTS, D_MODEL), D_MODEL ** -0.5),
        'expert_v': nrm(ks[23], (DEPTH, PEER_N_EXPERTS, D_MODEL), 0.25),
        'norm3_g': gain(ks[24], (DEPTH, D_MODEL)),
        'w_ple': nrm(ks[25], (DEPTH, PLE_DIM, D_MODEL), PLE_DIM ** -0.5),
        'w_ple_gate': nrm(ks[26], (DEPTH, D_MODEL, D_MODEL), D_MODEL ** -0.5),
    }

def reference(x_prompt, x_sample, p_prompt, p_sample, cache_k, cache_v, state_gla, page_table,
              norm1_g, w_in, b_gate, qa_norm_g, ka_norm_g, sb_bias, w_alpha, b_alpha, ob_norm_g, w_up_a,
              w_up_b, w_o, norm2_g, w_peer_q, peer_sub_keys, expert_u, expert_v, norm3_g, w_ple, w_ple_gate):
    dec_b, n_pages = page_table.shape
    past_len = n_pages * PAGE_SIZE
    hp, hs = x_prompt, x_sample
    kp_l, vp_l, sp_l, ks_l, vs_l, ss_l = [], [], [], [], [], []
    for i in range(DEPTH):
        lw = (norm1_g[i], w_in[i], b_gate[i], qa_norm_g[i], ka_norm_g[i], sb_bias[i], w_alpha[i], b_alpha[i],
              ob_norm_g[i], w_up_a[i], w_up_b[i], w_o[i], norm2_g[i], w_peer_q[i], peer_sub_keys[i],
              expert_u[i], expert_v[i], norm3_g[i], w_ple[i], w_ple_gate[i])
        s0 = jnp.zeros((hp.shape[0], GLA_HEADS, GLA_DK, GLA_DV), jnp.float32)
        hp, kp, vp, sp = trunk_layer(hp, p_prompt[i], 0, None, None, s0, *lw)
        past_k = cache_k[i][page_table].reshape(dec_b, past_len, SB_HEADS, SB_HEAD_DIM)
        past_v = cache_v[i][page_table].reshape(dec_b, past_len, SB_HEADS, SB_HEAD_DIM)
        hs, ksn, vsn, ssn = trunk_layer(hs, p_sample[i], past_len, past_k, past_v, state_gla[i], *lw)
        kp_l.append(kp); vp_l.append(vp); sp_l.append(sp)
        ks_l.append(ksn); vs_l.append(vsn); ss_l.append(ssn)
    return (hp, hs, jnp.stack(kp_l), jnp.stack(vp_l), jnp.stack(sp_l),
            jnp.stack(ks_l), jnp.stack(vs_l), jnp.stack(ss_l))


_drawn_inputs = setup_inputs


def setup_inputs(seed=0):
    import zlib

    import numpy as np

    out = dict(_drawn_inputs(seed))
    spreads = {}
    factors = {'b_gate': 3.259,
     'qa_norm_g': 8.0,
     'ka_norm_g': 3.092,
     'ob_norm_g': 3.773,
     'norm2_g': 3.327,
     'norm3_g': 177.901}
    for name, (base, spread) in spreads.items():
        noise = np.random.default_rng([zlib.crc32(name.encode()), seed]).standard_normal(out[name].shape)
        drawn = base * np.exp(spread * noise) if base else spread * noise
        out[name] = __import__('jax').numpy.asarray(drawn.astype(out[name].dtype))
    for name, factor in factors.items():
        out[name] = (out[name] * factor).astype(out[name].dtype)
    return out
```

```python
from contextlib import ExitStack

import numpy as np

import concourse.bass as bass
from concourse import mybir

F32 = mybir.dt.float32
U32 = mybir.dt.uint32
I32 = mybir.dt.int32
ALU = mybir.AluOpType
ACT = mybir.ActivationFunctionType
AX = mybir.AxisListType

P = 128
D = 1024
KD = D // P
SEQ = 512
NB = 8
T = SEQ + NB
HALF = T // 2
HALVES = ((0, HALF), (HALF, T))
NT = SEQ // P
ROWS = [P] * NT + [NB]
H = 8
HD = 64
GH = 4
GDK, GDV = 64, 128
CHUNK = 64
NCH = SEQ // CHUNK
RANK = 16
TAU = 16.0
PAGES = 32
PAGE_ROW = H * HD
PH = 8
NKEYS = 128
TOPK = 16
SEL = PH * TOPK
PLE = 256
EPS = 1e-6
NEG = -1e30
LOWEST = -3.0e38
Y_BANKS = ((2, 3), (0, 1))

RING_K = 8
RING_V = 8
RING_W = 4
RING_G = 8

S_QA, S_KA, S_QB, S_KB, S_VA, S_VB, S_RB, S_GA, S_GB = 0, 4, 8, 10, 12, 16, 20, 24, 32
S_UP, S_WO, S_PQ, S_END = 40, 48, 56, 72

CONSTS = {}


def _consts():
    i, j = np.arange(P)[:, None], np.arange(P)[None, :]
    pieces = [
        ("ident", i == j),
        ("mean_model", np.full((P, P), 1.0 / D)),
        ("mean_head", (i // HD == j // HD) / float(HD)),
        ("mean_gdv", np.full((P, P), 1.0 / GDV)),
        ("neg_tri", -1.0 * (i >= j)),
        ("neg_ones", np.full((P, P), -1.0)),
        ("neg_mask", NEG * (i >= j)),
        ("keep_mask", i < j),
        ("gla_mask", (i <= j) & (i // CHUNK == j // CHUNK)),
        ("chunk_reset", np.broadcast_to(np.arange(SEQ) % CHUNK != 0, (P, SEQ))),
        ("page_reset", np.broadcast_to(np.arange(512) % PAGES != 0, (P, 512))),
        ("iota16", np.broadcast_to(np.arange(TOPK), (P, TOPK))),
        ("sample_of", np.arange(P)[:, None] // (P // NB) == np.arange(NB)[None, :]),
        ("zeros", np.zeros((P, NB))),
        ("eps", np.full((P, 1), EPS)),
    ]
    at = 0
    for name, a in pieces:
        CONSTS[name] = (at, at + a.shape[1])
        at += a.shape[1]
    return np.concatenate([np.asarray(a, np.float32) for _, a in pieces], axis=1)


N_CONST = _consts().shape[1]

V_G1, V_QG, V_KG, V_BA, V_BG, V_OG, N_VEC = 0, 8, 9, 10, 12, 28, 29


class Steps:

    def __init__(self, eng, own):
        self.eng, self.own, self.count, self.last = eng, own, {}, None

    def also(self, op, *args, signal=None, **kw):
        sem = signal if signal is not None else self.own
        key = sem.name
        self.count[key] = self.count.get(key, 0) + 1
        op(*args, **kw).then_inc(sem, 1)
        self.last = (sem, self.count[key])

    def settle(self):
        if self.last is not None:
            self.eng.wait_ge(*self.last)

    def then(self, op, *args, signal=None, **kw):
        self.settle()
        self.also(op, *args, signal=signal, **kw)


def lay(start, sizes):
    out = {}
    for name, n in sizes:
        out[name] = (start, start + n)
        start += n
    return out, start


def build(nc, A):
    with ExitStack() as ctx:
        COLS = 53200
        arena = ctx.enter_context(nc.sbuf_tensor("arena", [P, COLS], F32))
        bank = [ctx.enter_context(nc.psum_tensor(f"bank{i}", [P, 512], F32))[:, :] for i in range(8)]
        made = {}

        def sem(name):
            if name not in made:
                made[name] = ctx.enter_context(nc.semaphore(name))
            return made[name]

        def sems(name, n):
            return [sem(f"{name}{i}") for i in range(n)]

        kept, at = lay(0, [("consts", N_CONST), ("vecs", 32), ("wring", RING_W * 1024)])
        first, end1 = lay(at, [
            ("gates", 16 * T), ("vab", 5 * 1024), ("srb", 4 * T), ("qk", 8 * T), ("qkb", 4 * T),
            ("zs", 2048), ("vring", RING_V * PAGE_ROW), ("la", 2 * T), ("abT", T), ("rowh", H), ("pt", 256), ("abw", 8 * RANK), ("alw", 256),
            ("xn", 8 * T), ("xT", 8 * T), ("kring", RING_K * PAGE_ROW), ("prod", 2 * PAGE_ROW)])
        second, end2 = lay(first["xn"][0], [
            ("tmp", 6144), ("cum", 2 * SEQ), ("qt", 2 * SEQ), ("kt", 2 * SEQ), ("qe", 2 * SEQ), ("kd", 2 * SEQ),
            ("gsmall", 64), ("states", 2 * (NCH + 1) * GDV), ("sstate", NB * 2 * GDV), ("kdr", 2 * SEQ)])
        assert end1 <= COLS and end2 <= COLS, (end1, end2)
        at3 = first["vab"][1]
        third, end3 = lay(at3, [
            ("xn2", 5 * D), ("g2", D), ("v16", 5 * 256), ("i16", 5 * 256), ("cand", 2048), ("onehot", 2048),
            ("expert", 5 * SEL), ("gate", 5 * SEL), ("top", 10 * SEL), ("i16f", 256), ("small", 128),
            ("xn2T", 8 * T), ("sk", 16 * P), ("qp", 2 * T), ("s_all", 5 * 2048)])
        assert end3 <= COLS, end3
        fourth, end4 = lay(third["xn2T"][0], [("gring", RING_G * 2 * D)])
        assert end4 <= end3
        fifth, end5 = lay(first["gates"][0], [("wpg", KD * D)])
        assert end5 <= first["vab"][0]
        sixth, end6 = lay(end4, [("diag", RING_G * P)])
        assert end6 <= COLS, end6
        seventh, end7 = lay(kept["wring"][0], [("ple_w", 2 * D), ("xn3T", D), ("sx", D)])
        assert end7 <= kept["wring"][1]
        eighth = {"pT": (P, P + 2 * T), "g3": third["g2"], "fin": (third["onehot"][0], third["onehot"][0] + D)}
        maps = {}
        for m in (kept, first, second, third, fourth, fifth, sixth, seventh, eighth):
            maps.update(m)

        def view(name, **dims):
            a, b = maps[name]
            return arena[:, a:b]

        def cst(name):
            a, b = CONSTS[name]
            return arena[:, maps["consts"][0] + a:maps["consts"][0] + b]

        vecs = view("vecs")
        ident = cst("ident")
        wring = view("wring").rearrange("p (s c) -> p s c", s=RING_W)
        gates = view("gates").rearrange("p (m t) -> p m t", m=16)
        mixT = gates[:, 0:8]
        vab = view("vab").rearrange("p (t c) -> p t c", t=5)
        h1 = vab
        srb = view("srb").rearrange("p (m t) -> p m t", m=4)
        qk = view("qk").rearrange("p (m t) -> p m t", m=8)
        qkb = view("qkb").rearrange("p (m t) -> p m t", m=4)
        zs = view("zs")
        vring = view("vring").rearrange("p (s c) -> p s c", s=RING_V)
        la = view("la").rearrange("p (m t) -> p m t", m=2)
        abT = view("abT")
        bias_row = view("rowh")
        xn = view("xn").rearrange("p (m t) -> p m t", m=8)
        xT = view("xT").rearrange("p (m t) -> p m t", m=8)
        qbc = view("xT")[:, 0:NB * PAGE_ROW].rearrange("p (b c) -> p b c", b=NB)
        kring = view("kring").rearrange("p (s c) -> p s c", s=RING_K)
        prod = view("prod").rearrange("p (s c) -> p s c", s=2)
        tmp = view("tmp")
        cum = view("cum").rearrange("p (m t) -> p m t", m=2)
        sc_v = view("cum").rearrange("p (q a c) -> p q a c", q=2, a=4)
        qt = view("qt").rearrange("p (m t) -> p m t", m=2)
        kt = view("kt").rearrange("p (m t) -> p m t", m=2)
        qe = view("qe").rearrange("p (m t) -> p m t", m=2)
        kd = view("kd").rearrange("p (m t) -> p m t", m=2)
        a0 = maps["qt"][0]
        yaT = arena[:, a0:a0 + 4 * T].rearrange("p (m t) -> p m t", m=4)
        assert a0 + 4 * T <= maps["qe"][1]
        states = view("states").rearrange("p (c m e) -> p c m e", c=NCH + 1, m=2)
        sstate = view("sstate").rearrange("p (b m e) -> p b m e", b=NB, m=2)
        kdr = view("kdr").rearrange("p (t m c) -> p t m c", t=NT, m=2)
        page_table = view("pt").bitcast(I32)
        abw = view("abw").rearrange("p (k c) -> p k c", k=KD)
        alw = view("alw")[0:RANK]
        qk_sq = view("vring")[:, 0:2 * T].rearrange("p (u t) -> p u t", u=2)
        qk_std = view("vring")[:, 2 * T:4 * T].rearrange("p (u t) -> p u t", u=2)
        gsmall = view("gsmall")
        chunk_decay, sample_decay = gsmall[:, 0:16], gsmall[:, 16:32].rearrange("p (m b) -> p m b", m=2)
        kv = tmp[:, 0:2048].rearrange("p (b m e) -> p b m e", b=NB, m=2)
        ob = tmp[:, 2048:2048 + 4 * T].rearrange("p (m t) -> p m t", m=4)
        ob_tmp = tmp[:, 0:3 * T].rearrange("p (u t) -> p u t", u=3)
        g2, g3 = view("g2"), view("g3")
        xn2 = view("xn2").rearrange("p (t c) -> p t c", t=5)
        xn2T = view("xn2T").rearrange("p (m t) -> p m t", m=8)
        sk = view("sk").rearrange("p (j n) -> p j n", j=16)
        qp = view("qp").rearrange("p (u t) -> p u t", u=2)
        s_all = view("s_all").rearrange("p (t j n) -> p t j n", t=5, j=16)
        v16 = view("v16").rearrange("p (t j n) -> p t j n", t=5, j=16)
        i16 = view("i16").bitcast(U32).rearrange("p (t j n) -> p t j n", t=5, j=16)
        cand = view("cand").rearrange("p (h n) -> p h n", h=PH)
        onehot = view("onehot").rearrange("p (h k j) -> p h k j", h=PH, k=TOPK)
        i16f = view("i16f").rearrange("p (j n) -> p j n", j=16)
        expert = view("expert").bitcast(U32).rearrange("p (t c) -> p t c", t=5)
        gate = view("gate").rearrange("p (t c) -> p t c", t=5)
        top = view("top").rearrange("p (u h k) -> p u h k", u=10, h=PH)
        top_u = view("top").bitcast(U32).rearrange("p (u h k) -> p u h k", u=10, h=PH)
        small = view("small")
        ssq, rstd2, den = small[:, 0:10], small[:, 10:20], small[:, 20:28]
        dot, act_g, coef = small[:, 32:40], small[:, 40:48], small[:, 48:56]
        slot_idx = view("small").bitcast(U32)[:, 56:64]
        idx_guard = view("small").bitcast(U32)[:, 80:82]
        zero_u = cst("zeros")[:, 0:2].bitcast(U32)
        sidx, sgate = view("small").bitcast(U32)[:, 64:72], small[:, 72:80]
        gring = view("gring").rearrange("p (s c) -> p s c", s=RING_G)
        wpg = view("wpg").rearrange("p (k c) -> p k c", k=KD)
        pT = view("pT").rearrange("p (m t) -> p m t", m=2)
        ple_w = view("ple_w").rearrange("p (m c) -> p m c", m=2)
        xn3T = view("xn3T").rearrange("p (k t) -> p k t", k=KD)
        fin = view("fin")
        diag = view("diag").rearrange("p (s c) -> p s c", s=RING_G)
        sx = view("sx")

        scratch_e = nc.dram_tensor("scratch_expert", (NB, SEL), U32, kind="Internal").ap()
        scratch_g = nc.dram_tensor("scratch_gate", (NB, SEL), F32, kind="Internal").ap()
        scratch_x = nc.dram_tensor("scratch_x", (NB, D), F32, kind="Internal").ap()

        items = []
        ends = {}

        def tile_items(s, kind, j):
            for half in range(2):
                items.append((kind, j, half))
            ends[s] = len(items)
        for j in range(8):
            tile_items(S_QA + j, "qk", j)
        AB_ITEM = len(items)
        items += [("ab", 0, 0), ("ab", 0, 1)]
        for j in range(4):
            tile_items(S_QB + j, "qkb", j)
        ALPHA_ITEM = len(items)
        items += [("alpha", m, half) for m in range(2) for half in range(2)]
        for s, kind in ((S_VA, "va"), (S_VB, "vb")):
            items += [(kind, t, 0) for t in range(5)]
            ends[s + 3] = len(items)
        for j in range(4):
            tile_items(S_RB + j, "rb", j)
        for j in range(16):
            tile_items(S_GA + j, "gate", j)
        N_ITEMS = len(items)

        w_in_slot = sems("w_landed", RING_W)
        k_landed = sems("k_landed", RING_K)
        v_landed = sems("v_landed", RING_V)
        consts_landed, x_landed, table_landed = sem("consts_landed"), sem("x_landed"), sem("table_landed")
        wab_landed, state_landed = sem("wab_landed"), sem("state_landed")
        sq_ready, mean1, std1, xn_ready = sem("sq_ready"), sem("mean1"), sem("std1"), sem("xn_ready")
        proj_ready, proj_taken, kstep = sem("proj_ready"), sem("proj_taken"), sem("kstep")
        qksq, qkmean, qkstd, qk_done = sem("qksq"), sem("qkmean"), sem("qkstd"), sem("qk_done")
        qb_ready, qb_taken = sem("qb_ready"), sem("qb_taken")
        k_mul, k_free = sem("k_mul"), sem("k_free")
        act_steps, dve_steps, pool_steps = sem("act_steps"), sem("dve_steps"), sem("pool_steps")
        out_done = sem("out_done")
        v_free = sem("v_free")
        zb_ready, dec_l, dec_sp, dec_z, dec_arg, dec_w = (sem(n) for n in ("zb_ready", "dec_l", "dec_sp", "dec_z", "dec_arg", "dec_w"))
        la_in, la_ready, gla_d, gla_e, gla_in = (sem(n) for n in ("la_in", "la_ready", "gla_d", "gla_e", "gla_in"))
        kd_tr, kd_rows, sc_ready, sc_done, u_ready, states_done, o_ready, o_taken = (
            sem(n) for n in ("kd_tr", "kd_rows", "sc_ready", "sc_done", "u_ready", "states_done", "o_ready", "o_taken"))
        vb_ready, vb_taken, ss_ready, so_ready, ob_sq, ob_mean, ob_std, yb_ready = (
            sem(n) for n in ("vb_ready", "vb_taken", "ss_ready", "so_ready", "ob_sq", "ob_mean", "ob_std", "yb_ready"))
        z_ready, att_l, att_r, att_sp, acc_ready, att_w, y_ready, y_taken, ya_ready = (
            sem(n) for n in ("z_ready", "att_l", "att_r", "att_sp", "acc_ready", "att_w", "y_ready", "y_taken", "ya_ready"))
        v_done = sem("v_done")
        up_ready, up_taken, mix_ready = sem("up_ready"), sem("up_taken"), sem("mix_ready")
        wo_ready, wo_taken, h_landed = sem("wo_ready"), sem("wo_taken"), sem("h_landed")
        rows_landed = sem("rows_landed")
        h_sq, h_std, xn2_ready, x2t_ready, x2t_taken = (sem(n) for n in ("h_sq", "h_std", "xn2_ready", "x2t_ready", "x2t_taken"))
        pq_ready, pq_taken, s_ready, s_taken, topk_done = (sem(n) for n in ("pq_ready", "pq_taken", "s_ready", "s_taken", "topk_done"))
        sel_ready, soft_in, soft_e = sem("sel_ready"), sem("soft_in"), sem("soft_e")
        g_landed = sems("g_landed", RING_G)
        dots, gel, gated, diag_ready, g_used = (sem(n) for n in ("dots", "gel", "gated", "diag_ready", "g_used"))
        idx_copied = sem("idx_copied")
        y_sum, h2_ready, h3_std, xn3_ready, x3t_ready, x3t_taken, ple_ready, ple_sig, y_out = (
            sem(n) for n in ("y_sum", "h2_ready", "h3_std", "xn3_ready", "x3t_ready", "x3t_taken", "ple_ready", "ple_sig", "y_out"))
        late_landed = sem("late_landed")
        sample_out, sample_in = sem("sample_out"), sem("sample_in")
        front_over = sem("front_over")

        def w_free(s):
            if s < S_UP:
                if s in ends:
                    return proj_ready, ends[s]
                base = {S_VA: 0, S_VB: 3}[S_VA if s < S_VB else S_VB]
                return kstep, base + (s - (S_VA if s < S_VB else S_VB)) + 1
            if s < S_WO:
                return up_ready, 4 * (s - S_UP + 1)
            if s < S_PQ:
                n = s - S_WO
                return (wo_ready, 5 * (n // 4 + 1)) if n % 4 == 3 else (kstep, 6 + 3 * (n // 4) + n % 4 + 1)
            return pq_ready, 2 * (s - S_PQ + 1)

        block = ctx.enter_context(nc.Block())

        @block.sync
        def _(sp):
            sp.dma_start(view("consts"), A["consts"]).then_inc(consts_landed, 16)
            sp.dma_start(vecs[:, 0:N_VEC], A["vecs"]).then_inc(consts_landed, 16)
            for k in range(4):
                sp.dma_start(xT[:, 2 * k:2 * k + 2], A["xT"][:, 2 * k:2 * k + 2]).then_inc(x_landed, 16)
            sp.dma_start(abw, A["w_ab"]).then_inc(wab_landed, 16)
            sp.dma_start(alw, A["w_alpha"]).then_inc(wab_landed, 16)
            sp.dma_start(bias_row, A["sb_bias"].partition_broadcast(P)).then_inc(wab_landed, 16)

            def stream(a, b):
                for s in range(a, b):
                    if s >= RING_W:
                        sp.wait_ge(*w_free(s - RING_W))
                    sp.dma_start(wring[:, s % RING_W], A["w_stream"][s]).then_inc(w_in_slot[s % RING_W], 16)

            stream(0, 8 + RING_W)
            sp.wait_ge(qk_done, 8)
            sp.dma_start(A["new_kT"].rearrange("(m p) t -> p m t", p=P), qk[:, 4:8]).then_inc(out_done, 16)
            stream(8 + RING_W, S_RB + RING_W)
            sp.wait_ge(proj_taken, ALPHA_ITEM + 4 + 5)
            sp.dma_start(A["new_v"][0:SEQ].rearrange("(t p) c -> p t c", p=P), vab[:, 0:NT, 0:512]).then_inc(out_done, 16)
            sp.dma_start(A["new_v"][SEQ:T], vab[0:NB, NT, 0:512]).then_inc(out_done, 16)
            stream(S_RB + RING_W, S_UP)
            sp.wait_ge(k_free, RING_K + NB * PAGES)
            sp.wait_ge(proj_ready, N_ITEMS)
            sp.dma_start(sstate, A["state"]).then_inc(state_landed, 16)
            stream(S_UP, S_UP + RING_W)
            sp.wait_ge(states_done, 2)
            sp.dma_start(A["gla_prompt"], states[:, NCH]).then_inc(out_done, 16)
            sp.wait_ge(ss_ready, 1)
            sp.dma_start(A["gla_sample"], sstate).then_inc(out_done, 16)
            sp.wait_ge(y_ready, 4)
            sp.wait_ge(out_done, 16 * 5)
            sp.wait_ge(v_done, 1)
            sp.dma_start(h1[:, 0:NT], A["x_rows"][0:SEQ].rearrange("(t p) c -> p t c", p=P)).then_inc(rows_landed, 16)
            sp.dma_start(h1[0:NB, NT], A["x_rows"][SEQ:T]).then_inc(rows_landed, 16)
            stream(S_UP + RING_W, S_WO)
            sp.wait_ge(mix_ready, 8)
            sp.dma_start(g2, A["norm2_g"].partition_broadcast(P)).then_inc(late_landed, 16)
            sp.dma_start(sk, A["sub_keysT"]).then_inc(late_landed, 16)
            stream(S_WO, S_PQ)
            stream(S_PQ, S_PQ + RING_W)
            sp.wait_ge(wo_ready, 10)
            sp.dma_start(wpg, A["w_ple_gate"]).then_inc(late_landed, 16)
            stream(S_PQ + RING_W, S_END)
            sp.wait_ge(xn2_ready, 5)
            sp.dma_start(scratch_x, xn2[0:NB, NT]).then_inc(sample_out, 16)
            sp.wait_ge(s_taken, 32)
            sp.wait_ge(topk_done, 1)
            sp.dma_start(pT, A["pT"]).then_inc(late_landed, 16)
            sp.dma_start(ple_w, A["w_ple"]).then_inc(late_landed, 16)
            sp.dma_start(g3, A["norm3_g"].partition_broadcast(P)).then_inc(late_landed, 16)
            sp.wait_ge(sel_ready, 1)
            sp.dma_start(scratch_e, expert[0:NB, NT]).then_inc(sample_out, 16)
            sp.dma_start(scratch_g, gate[0:NB, NT]).then_inc(sample_out, 16)
            sp.wait_ge(sample_out, 48)
            for b in range(NB):
                w = P // NB
                sp.dma_start(sx[b * w:(b + 1) * w], scratch_x[b].partition_broadcast(w)).then_inc(sample_in, 16)
            sp.dma_start(sidx, scratch_e.rearrange("b (j r) -> (b j) r", r=8)).then_inc(sample_in, 16)
            sp.dma_start(sgate, scratch_g.rearrange("b (j r) -> (b j) r", r=8)).then_inc(sample_in, 16)
            for n, t in enumerate([NT] + list(range(NT))):
                sp.wait_ge(y_out, n + 1)
                R = ROWS[t]
                sp.dma_start(A["y"][t * P:t * P + R], h1[0:R, t]).then_inc(out_done, 16)
            sp.wait_ge(out_done, 16 * 10)

        @block.gpsimd
        def _(pool):
            c = Steps(pool, pool_steps)
            pool.dma_start(page_table[0:1, :], A["page_table"]).then_inc(table_landed, 16)
            pool.wait_ge(table_landed, 16)

            def load_page(ring, cache, landed, n, s):
                page = pool.value_load(page_table[0:1, bass.ds(n, 1)], min_val=0, max_val=cache.shape[0] - 1)
                pool.dma_start(ring[:, s, :], cache[bass.ds(page, 1)].rearrange("a p n -> (a p) n")).then_inc(landed[s], 16)

            with pool.Fori(0, NB * PAGES // RING_K) as i:
                for s in range(RING_K):
                    pool.wait_ge(k_free, i * RING_K + (s + 1))
                    load_page(kring, A["cache_k"], k_landed, i * RING_K + s, s)
            with pool.Fori(0, NB * PAGES // RING_V) as i:
                for s in range(RING_V):
                    pool.wait_ge(v_free, i * RING_V + (s + 1))
                    load_page(vring, A["cache_v"], v_landed, i * RING_V + s, s)
            pool.wait_ge(topk_done, 1)
            pool.wait_ge(sample_in, 16 * (NB + 2))
            for r in range(8):
                pool.indirect_dma_start(gring[:, r, :], None, A["experts"], bass.IndirectOffsetOnAxis(ap=sidx[:, r:r + 1], axis=0)).then_inc(g_landed[r], 16)
            for t in range(NT):
                pool.wait_ge(sel_ready, t + 2)
                with pool.Fori(0, SEL // RING_G) as i:
                    for g in range(4):
                        pool.wait_ge(g_used, i * 4 + (t * 64 + g + 1))
                        pair = slot_idx[:, 2 * g:2 * g + 2]
                        rows = expert[:, t, bass.ds(i * 8 + 2 * g, 2)]
                        pool.tensor_tensor(pair, rows, zero_u, ALU.add).then_inc(idx_copied, 1)
                        pool.wait_ge(idx_copied, i * 4 + (t * 64 + g + 1))
                        pool.tensor_tensor(idx_guard, pair, zero_u, ALU.add)
                        for s in (2 * g, 2 * g + 1):
                            pool.indirect_dma_start(gring[:, s, :], None, A["experts"],
                                                    bass.IndirectOffsetOnAxis(ap=slot_idx[:, s:s + 1], axis=0)).then_inc(g_landed[s], 16)

        @block.scalar
        def _(act):
            c = Steps(act, act_steps)
            A_ = nc.scalar.activation
            act.wait_ge(consts_landed, 32)
            for k in range(KD):
                act.wait_ge(x_landed, 64)
                c.also(A_, qk[:, k], xT[:, k], ACT.Square, signal=sq_ready)
            std_row = view("zs")[:, 0:T]
            for half, (a, b) in enumerate(HALVES):
                act.wait_ge(mean1, half + 1)
                c.also(A_, std_row[:, a:b], bank[6 + half][:, 0:HALF], ACT.Sqrt, bias=cst("eps"), signal=std1)

            def take(i):
                kind, j, half = items[i]
                act.wait_ge(proj_ready, i + 1)
                a, b = HALVES[half]
                src = bank[i % 6][:, 0:HALF]
                if kind == "qk":
                    c.also(A_, qk[:, j, a:b], src, ACT.Copy, signal=proj_taken)
                elif kind == "ab":
                    c.also(A_, abT[0:RANK, a:b], src[0:RANK], ACT.Copy, signal=proj_taken)
                elif kind == "qkb":
                    c.also(A_, qkb[:, j, a:b], src, ACT.Copy, scale=(GDK ** -0.5 if j < 2 else 1.0), signal=proj_taken)
                elif kind == "alpha":
                    c.also(A_, la[:, j, a:b], src, ACT.Identity, bias=vecs[:, V_BA + j:V_BA + j + 1], signal=proj_taken)
                elif kind in ("va", "vb"):
                    o = 0 if kind == "va" else 512
                    R = ROWS[j]
                    c.also(A_, vab[0:R, j, o:o + 512], bank[i % 6][0:R, :], ACT.Copy, signal=proj_taken)
                elif kind == "rb":
                    c.also(A_, srb[:, j, a:b], src, ACT.Silu, signal=proj_taken)
                else:
                    c.also(A_, gates[:, j, a:b], src, ACT.Sigmoid, bias=vecs[:, V_BG + j:V_BG + j + 1], signal=proj_taken)

            def squares(j):
                if j >= 2:
                    act.wait_ge(qkmean, 2 * (j - 1))
                for half, (a, b) in enumerate(HALVES):
                    if half == 0:
                        c.settle()
                    c.also(A_, qk_sq[:, j % 2, a:b], qk[:, j, a:b], ACT.Square, signal=qksq)

            def roots(j):
                if j >= 2:
                    act.wait_ge(qk_done, j - 1)
                for half, (a, b) in enumerate(HALVES):
                    act.wait_ge(qkmean, 2 * j + half + 1)
                    c.also(A_, qk_std[:, j % 2, a:b], bank[6 + half][:, 0:HALF], ACT.Sqrt, bias=cst("eps"), signal=qkstd)

            act.wait_ge(xn_ready, KD)
            for j in range(8):
                take(2 * j)
                take(2 * j + 1)
                squares(j)
                if j >= 1:
                    roots(j - 1)
            take(AB_ITEM)
            take(AB_ITEM + 1)
            roots(7)
            for b in range(NB):
                act.wait_ge(qb_ready, b + 1)
                c.also(A_, qbc[:, b], bank[6 + b % 2][:, :], ACT.Copy, signal=qb_taken)
            for i in range(AB_ITEM + 2, N_ITEMS):
                take(i)

            act.wait_ge(zb_ready, 1)
            c.then(A_, tmp[:, 0:2048], tmp[:, 0:2048], ACT.Exp, scale=-1.0)
            c.then(A_, tmp[:, 0:2048], tmp[:, 0:2048], ACT.Ln, bias=1.0, signal=dec_l)
            for q in range(4):
                act.wait_ge(dec_arg, q + 1)
                c.also(A_, zs[:, 512 * q:512 * q + 512], zs[:, 512 * q:512 * q + 512], ACT.Exp, signal=dec_w)

            act.wait_ge(la_in, 1)
            c.then(A_, tmp[:, 4128:4128 + 2 * T], tmp[:, 4128:4128 + 2 * T], ACT.Exp, scale=-1.0)
            c.then(A_, tmp[:, 4128:4128 + 2 * T], tmp[:, 4128:4128 + 2 * T], ACT.Ln, bias=1.0, signal=la_ready)
            act.wait_ge(gla_d, 1)
            flat = lambda x: x.rearrange("p m t -> p (m t)")
            c.also(A_, flat(qe), flat(cum), ACT.Exp, scale=1.0 / TAU, signal=gla_e)
            c.also(A_, flat(qt), tmp[:, 0:1024], ACT.Exp, scale=1.0 / TAU, signal=gla_e)
            c.also(A_, flat(kt), tmp[:, 0:1024], ACT.Exp, scale=-1.0 / TAU, signal=gla_e)
            c.also(A_, flat(kd), tmp[:, 1024:2048], ACT.Exp, scale=1.0 / TAU, signal=gla_e)
            c.also(A_, sample_decay, la[:, :, SEQ:T], ACT.Exp, scale=1.0 / TAU, signal=gla_e)
            for m in range(2):
                act.wait_ge(kd_tr, m + 1)
                c.also(A_, kdr[:, :, m, :], bank[m].rearrange("p (t c) -> p t c", t=NT), ACT.Copy, signal=kd_rows)
            for u in range(2):
                for par in range(2):
                    act.wait_ge(o_ready, 2 * u + par + 1)
                    src = bank[2 + par].rearrange("p (tt m c) -> p m tt c", tt=2, m=2)
                    dst = ob[:, :, 256 * u:256 * u + 256].rearrange("p (m par) (tt c) -> p par m tt c", par=2, tt=2)[:, par]
                    c.also(A_, dst, src, ACT.Copy, signal=o_taken)
            for par in range(2):
                act.wait_ge(so_ready, par + 1)
                src = bank[7 if par == 0 else 1][:, 0:16].rearrange("p (m b) -> p m b", m=2)
                dst = ob[:, :, SEQ:T].rearrange("p (m par) b -> p par m b", par=2)[:, par]
                c.also(A_, dst, src, ACT.Copy, signal=o_taken)
            act.wait_ge(ss_ready, 1)
            for h in range(GH):
                c.settle()
                if h >= 2:
                    act.wait_ge(ob_mean, 2 * (h - 1))
                c.also(A_, ob_tmp[:, h % 2], ob[:, h], ACT.Square, signal=ob_sq)
                if h >= 1:
                    act.wait_ge(yb_ready, h)
                for half, (a, b) in enumerate(HALVES):
                    act.wait_ge(ob_mean, 2 * h + half + 1)
                    c.also(A_, ob_tmp[:, 2, a:b], bank[4 + half][:, 0:HALF], ACT.Sqrt, bias=cst("eps"), signal=ob_std)

            act.wait_ge(yb_ready, GH)
            for h in range(H):
                bias_h = bias_row[:, h:h + 1]
                if h >= 1:
                    act.wait_ge(att_sp, h)
                at = 0
                for n in range(NT):
                    w = SEQ - P * n
                    act.wait_ge(z_ready, NT * h + n + 1)
                    c.also(A_, tmp[:, at:at + w], bank[n][:, 0:w], ACT.Identity, bias=bias_h, signal=att_l)
                    at += w
                act.wait_ge(att_r, h + 1)
                c.then(A_, tmp[:, 1280:2560], tmp[:, 1280:2560], ACT.Exp, scale=-1.0)
                c.then(A_, tmp[:, 1280:2560], tmp[:, 1280:2560], ACT.Ln, bias=1.0, signal=att_l)
                at = 0
                for n in range(NT):
                    w = SEQ - P * n
                    act.wait_ge(acc_ready, NT * h + n + 1)
                    c.also(A_, tmp[:, 3840 + at:3840 + at + w], bank[n][:, 0:w], ACT.Exp, bias=bias_h, signal=att_w)
                    at += w
                if h % 2 == 1:
                    act.wait_ge(y_ready, h // 2 + 1)
                    c.also(A_, yaT[:, h // 2, 0:SEQ], bank[4 + h // 2 % 2][:, :], ACT.Copy, signal=y_taken)
            act.wait_ge(v_done, 1)
            acc = bank[6][:, 0:64].rearrange("p (b m u) -> p u m b", b=NB, m=4)
            for u in range(2):
                rows = slice(64 * u, 64 * u + 64)
                c.also(A_, yaT[rows, :, SEQ:T], acc[rows, u], ACT.Copy, signal=y_taken)

            act.wait_ge(late_landed, 32)
            for t in range(5):
                R = ROWS[t]
                act.wait_ge(wo_taken, 5 + t + 1)
                c.settle()
                c.also(A_, view("onehot")[0:R, 0:D], h1[0:R, t], ACT.Square, accum_out=ssq[0:R, t:t + 1])
                c.then(A_, ssq[0:R, 5 + t:6 + t], ssq[0:R, t:t + 1], ACT.Sqrt, bias=cst("eps")[0:R], scale=1.0 / D, signal=h_std)
            for t in range(5):
                for k2 in range(2 if t < NT else 1):
                    n = 2 * t + k2
                    act.wait_ge(x2t_ready, n + 1)
                    if t < NT:
                        c.also(A_, xn2T[:, 4 * k2:4 * k2 + 4, t * P:t * P + P],
                               bank[2 + n % 6].rearrange("p (k c) -> p k c", k=4), ACT.Copy, signal=x2t_taken)
                    else:
                        c.also(A_, xn2T[:, :, SEQ:T], bank[2 + n % 6][:, 0:64].rearrange("p (k c) -> p k c", k=8),
                               ACT.Copy, signal=x2t_taken)

            def take_scores(j):
                act.wait_ge(s_ready, 2 * j + 1)
                c.also(A_, s_all[:, 0:NT, j, :], bank[4 + j % 2].rearrange("p (t n) -> p t n", t=NT), ACT.Copy, signal=s_taken)
                act.wait_ge(s_ready, 2 * j + 2)
                c.also(A_, s_all[0:NB, NT, j, :], bank[6 + j % 2][0:NB, 0:P], ACT.Copy, signal=s_taken)

            for j in range(16):
                if j >= 2:
                    act.wait_ge(s_ready, 2 * (j - 1))
                for half, (a, b) in enumerate(HALVES):
                    act.wait_ge(pq_ready, 2 * j + half + 1)
                    c.also(A_, qp[:, j % 2, a:b], bank[(2 * j + half) % 4][:, 0:HALF], ACT.Copy, signal=pq_taken)
                if j >= 1:
                    take_scores(j - 1)
            take_scores(15)

            def softmax_exp(n, t):
                R = ROWS[t]
                act.wait_ge(soft_in, n + 1)
                c.also(A_, top[0:R, 1], top[0:R, 1], ACT.Exp, signal=soft_e)

            def final(n, t):
                R = ROWS[t]
                act.wait_ge(h2_ready, n + 1)
                c.also(A_, fin[0:R], h1[0:R, t], ACT.Square, accum_out=ssq[0:R, t:t + 1])
                c.then(A_, ssq[0:R, 5 + t:6 + t], ssq[0:R, t:t + 1], ACT.Sqrt, bias=cst("eps")[0:R], scale=1.0 / D, signal=h3_std)
                for c2 in range(2):
                    act.wait_ge(x3t_ready, 2 * n + c2 + 1)
                    c.also(A_, xn3T[:, 4 * c2:4 * c2 + 4, 0:R],
                           bank[4 + c2][:, 0:4 * R].rearrange("p (k c) -> p k c", k=4), ACT.Copy, signal=x3t_taken)
                c.settle()
                for c2 in range(2):
                    act.wait_ge(ple_ready, 4 * n + c2 + 1)
                    c.also(A_, fin[0:R, 512 * c2:512 * c2 + 512], bank[6 + c2][0:R, :], ACT.Sigmoid, signal=ple_sig)

            softmax_exp(0, NT)
            softmax_exp(1, 0)
            act.wait_ge(dots, 1)
            c.also(A_, act_g, dot, ACT.Gelu, signal=gel)
            act.wait_ge(gated, 1)
            for r in range(8):
                c.also(A_, diag[:, r, 0:NB], cst("sample_of"), ACT.Copy, scale=coef[:, r:r + 1], signal=diag_ready if r == 7 else None)
            final(0, NT)
            for t in range(NT):
                if t + 1 < NT:
                    softmax_exp(t + 2, t + 1)
                def diags(i, g):
                    act.wait_ge(gated, i * 4 + (t * 64 + g + 2))
                    act.wait_ge(g_used, i * 4 + (t * 64 + g + 1))
                    A_(diag[:, 2 * g], ident, ACT.Copy, scale=coef[:, 2 * g:2 * g + 1])
                    A_(diag[:, 2 * g + 1], ident, ACT.Copy, scale=coef[:, 2 * g + 1:2 * g + 2]).then_inc(diag_ready, 1)

                with act.Fori(0, SEL // RING_G) as i:
                    for g in range(4):
                        pair = slice(2 * g, 2 * g + 2)
                        act.wait_ge(dots, i * 4 + (t * 64 + g + 2))
                        A_(act_g[:, pair], dot[:, pair], ACT.Gelu).then_inc(gel, 1)
                        if g >= 1:
                            diags(i, g - 1)
                    diags(i, 3)
                final(t + 1, t)
        @block.vector
        def _(dve):
            c = Steps(dve, dve_steps)
            V = nc.vector

            def absolute(out, x):
                return V.scalar_tensor_tensor(out=out, in0=x, scalar=-1.0, in1=x, op0=ALU.mult, op1=ALU.max)

            dve.wait_ge(consts_landed, 32)
            rstd = view("zs")[:, T:2 * T]
            std_row = view("zs")[:, 0:T]
            dve.wait_ge(std1, 2)
            c.also(V.reciprocal, rstd, std_row)
            c.settle()
            for k in range(KD):
                c.also(V.scalar_tensor_tensor, out=xn[:, k], in0=xT[:, k], scalar=vecs[:, V_G1 + k:V_G1 + k + 1], in1=rstd,
                       op0=ALU.mult, op1=ALU.mult, signal=xn_ready)
            c.also(V.tensor_scalar, vecs[:, V_QG:V_QG + 1], vecs[:, V_QG:V_QG + 1], HD ** -0.5, None, ALU.mult)
            for j in range(8):
                gain = V_QG if j < 4 else V_KG
                dve.wait_ge(qkstd, 2 * (j + 1))
                c.then(V.reciprocal, qk_std[:, j % 2], qk_std[:, j % 2])
                c.then(V.scalar_tensor_tensor, out=qk[:, j], in0=qk[:, j], scalar=vecs[:, gain:gain + 1], in1=qk_std[:, j % 2],
                       op0=ALU.mult, op1=ALU.mult, signal=qk_done)
            dve.wait_ge(qb_taken, NB)
            z4 = zs.rearrange("p (b h g) -> p b g h", b=NB, h=H)
            c.settle()
            dve.sem_inc(k_free, RING_K)
            dve.sem_inc(v_free, RING_V)

            def sum_heads(b, g, s):
                V.tensor_reduce(z4[:, bass.ds(b, 1), bass.ds(g, 1), :].rearrange("p a c h -> p (a c h)"),
                                prod[:, s % 2].rearrange("p (h d) -> p h d", h=H), AX.X, ALU.add).then_inc(k_free, 1)

            with dve.Fori(0, NB) as b:
                with dve.Fori(0, PAGES // RING_K) as g:
                    for s in range(RING_K):
                        n = b * PAGES + g * RING_K
                        dve.wait_ge(k_landed[s], b * (16 * PAGES // RING_K) + g * 16 + 16)
                        dve.wait_ge(k_free, n + (s + 7 if s else 8))
                        if s:
                            dve.wait_ge(k_mul, n + s)
                        V.tensor_tensor(prod[:, s % 2], kring[:, s], qbc[:, bass.ds(b, 1), :].rearrange("p a n -> p (a n)"),
                                        ALU.mult).then_inc(k_mul, 1)
                        if s:
                            sum_heads(b, g * -RING_K + (PAGES - s), s - 1)
                    dve.wait_ge(k_mul, b * PAGES + g * RING_K + RING_K)
                    sum_heads(b, g * -RING_K + (PAGES - RING_K), RING_K - 1)
            dve.wait_ge(k_free, RING_K + NB * PAGES)

            dve.wait_ge(proj_taken, N_ITEMS)
            dve.wait_ge(proj_ready, N_ITEMS)
            zb3 = zs.rearrange("p (b h g) -> p b h g", b=NB, h=H)
            brow = bias_row.rearrange("p (b h g) -> p b h g", b=1, g=1).to_broadcast([P, NB, H, PAGES])
            c.also(V.tensor_tensor, zb3, zb3, brow, ALU.add)
            c.then(absolute, tmp[:, 0:2048], zs, signal=zb_ready)
            dve.wait_ge(dec_l, 1)
            c.also(V.scalar_tensor_tensor, out=tmp[:, 2048:4096], in0=zs, scalar=0.0, in1=tmp[:, 0:2048], op0=ALU.max, op1=ALU.add)
            c.settle()
            for q in range(4):
                o = 512 * q
                c.also(V.tensor_tensor_scan, tmp[:, 4096 + o:4608 + o], cst("page_reset"), tmp[:, 2048 + o:2560 + o], 0.0,
                       ALU.mult, ALU.add, signal=dec_sp)
            for q in range(4):
                o = 512 * q
                dve.wait_ge(dec_z, q + 1)
                c.also(V.tensor_tensor, zs[:, o:o + 512], zs[:, o:o + 512], bank[q][:, :], ALU.add, signal=dec_arg)

            laf = view("la")
            g_tmp = tmp[:, 4128:4128 + 2 * T]
            c.then(absolute, g_tmp, laf, signal=la_in)
            dve.wait_ge(la_ready, 1)
            c.also(V.scalar_tensor_tensor, out=laf, in0=laf, scalar=0.0, in1=g_tmp, op0=ALU.min, op1=ALU.subtract)
            c.settle()
            for m in range(2):
                c.also(V.tensor_tensor_scan, cum[:, m], cst("chunk_reset"), la[:, m, 0:SEQ], 0.0, ALU.mult, ALU.add)
            c.settle()
            ch = view("cum").rearrange("p (c i) -> p c i", i=CHUNK)
            t3 = lambda o: tmp[:, o:o + 1024].rearrange("p (c i) -> p c i", i=CHUNK)
            c.also(V.tensor_tensor, t3(0), ch, ch[:, :, CHUNK // 2 - 1:CHUNK // 2].to_broadcast([P, 2 * NCH, CHUNK]), ALU.subtract)
            c.also(V.tensor_tensor, t3(1024), ch[:, :, CHUNK - 1:CHUNK].to_broadcast([P, 2 * NCH, CHUNK]), ch, ALU.subtract, signal=gla_d)
            dve.wait_ge(gla_e, 5)
            c.also(V.tensor_copy, chunk_decay, view("qe").rearrange("p (c i) -> p c i", i=CHUNK)[:, :, CHUNK - 1])
            c.also(V.tensor_tensor, kd, kd, qkb[:, 2:4, 0:SEQ], ALU.mult, signal=gla_in)
            c.also(V.tensor_tensor, qt, qt, qkb[:, 0:2, 0:SEQ], ALU.mult)
            c.also(V.tensor_tensor, kt, kt, qkb[:, 2:4, 0:SEQ], ALU.mult, signal=gla_in)
            c.then(V.tensor_tensor, qe, qe, qkb[:, 0:2, 0:SEQ], ALU.mult)
            c.also(V.memset, states[:, 0], 0.0, signal=gla_in)
            mask4 = cst("gla_mask").rearrange("p (a c) -> p a c", a=1).to_broadcast([P, 4, P])
            for u in range(2):
                for par in range(2):
                    dve.wait_ge(sc_ready, 2 * u + par + 1)
                    c.also(V.tensor_tensor, sc_v[:, par], bank[2 + par].rearrange("p (a c) -> p a c", a=4), mask4, ALU.mult, signal=sc_done)
                dve.wait_ge(u_ready, u + 1)
                for ch4 in range(4):
                    cc = 4 * u + ch4
                    c.settle()
                    for m in range(2):
                        ub = (4 if u == 0 else 0) + cc % 2
                        ucol = (ch4 // 2 * 2 + m) * P
                        c.also(V.scalar_tensor_tensor, out=states[:, cc + 1, m], in0=states[:, cc, m],
                               scalar=chunk_decay[:, m * NCH + cc:m * NCH + cc + 1], in1=bank[ub][:, ucol:ucol + P],
                               op0=ALU.mult, op1=ALU.add, signal=states_done if (cc in (3, 7) and m == 1) else None)
            dve.wait_ge(state_landed, 16)
            for b in range(NB):
                dve.wait_ge(vb_ready, b + 1)
                for par in range(2):
                    rows = slice(64 * par, 64 * par + 64)
                    v_b = bank[7].rearrange("p (m q e) -> p q m e", m=2, q=2)[rows, par]
                    k_b = qkb[rows, 2:4, SEQ + b:SEQ + b + 1].to_broadcast([64, 2, GDV])
                    c.also(V.tensor_tensor, kv[rows, b], v_b, k_b, ALU.mult, signal=vb_taken if par else None)
            dec = sample_decay.rearrange("p m (b o) -> p b m o", o=1).to_broadcast([P, NB, 2, GDV])
            c.then(V.tensor_tensor, sstate, sstate, dec, ALU.mult)
            c.then(V.tensor_tensor, sstate, sstate, kv, ALU.add, signal=ss_ready)
            for h in range(GH):
                dve.wait_ge(ob_std, 2 * (h + 1))
                c.then(V.reciprocal, ob_tmp[:, 2], ob_tmp[:, 2])
                c.also(V.scalar_tensor_tensor, out=srb[:, h], in0=ob[:, h], scalar=vecs[:, V_OG:V_OG + 1], in1=srb[:, h],
                       op0=ALU.mult, op1=ALU.mult)
                c.then(V.tensor_tensor, srb[:, h], srb[:, h], ob_tmp[:, 2], ALU.mult, signal=yb_ready)

            for h in range(H):
                dve.wait_ge(att_l, 5 * h + 4)
                if h >= 1:
                    dve.wait_ge(acc_ready, NT * h)
                c.also(absolute, tmp[:, 1280:2560], tmp[:, 0:1280], signal=att_r)
                dve.wait_ge(att_l, 5 * h + 5)
                c.also(V.scalar_tensor_tensor, out=tmp[:, 2560:3840], in0=tmp[:, 0:1280], scalar=0.0, in1=tmp[:, 1280:2560],
                       op0=ALU.max, op1=ALU.add)
                at = 2560
                c.settle()
                for n in range(NT):
                    c.also(V.tensor_tensor, tmp[:, at:at + P], tmp[:, at:at + P], cst("keep_mask"), ALU.mult,
                           signal=att_sp if n == NT - 1 else None)
                    at += SEQ - P * n

            for m in range(8):
                for q in range(4):
                    i = 4 * m + q
                    a, b = HALVES[q % 2]
                    dve.wait_ge(up_ready, i + 1)
                    gm = gates[:, (m if q < 2 else 8 + m), a:b]
                    c.also(V.tensor_tensor, gm, gm, bank[i % 8][:, 0:HALF], ALU.mult, signal=up_taken)
                c.then(V.tensor_tensor, gates[:, m], gates[:, m], gates[:, 8 + m], ALU.add, signal=mix_ready)
            dve.wait_ge(rows_landed, 32)
            for i in range(10):
                t, half = i % 5, i // 5
                R = ROWS[t]
                dve.wait_ge(wo_ready, i + 1)
                hh = h1[0:R, t, 512 * half:512 * half + 512]
                c.also(V.tensor_tensor, hh, hh, bank[i % 8][0:R, :], ALU.add, signal=wo_taken)
            dve.wait_ge(late_landed, 32)
            for t in range(5):
                R = ROWS[t]
                dve.wait_ge(h_std, t + 1)
                c.also(V.reciprocal, rstd2[0:R, t:t + 1], ssq[0:R, 5 + t:6 + t])
                c.then(V.scalar_tensor_tensor, out=xn2[0:R, t], in0=h1[0:R, t], scalar=rstd2[0:R, t:t + 1], in1=g2[0:R],
                       op0=ALU.mult, op1=ALU.mult, signal=xn2_ready)

            def two_best(values, best, where, done=None):
                for part in range(2):
                    pick = slice(8 * part, 8 * part + 8)
                    c.settle()
                    for x, v, w in zip(values, best, where):
                        c.also(V.max, v[:, pick], x)
                    c.settle()
                    for n, (x, v, w) in enumerate(zip(values, best, where)):
                        c.also(V.max_index, w[:, pick], v[:, pick], x, signal=done if part and n == len(values) - 1 else None)
                    if part == 0:
                        c.settle()
                        for x, v, w in zip(values, best, where):
                            c.also(V.match_replace, x, v[:, pick], x, LOWEST)

            for j in range(16):
                dve.wait_ge(s_taken, 2 * (j + 1))
                pick = [(t, ROWS[t]) for t in range(5)]
                two_best([s_all[0:R, t, j] for t, R in pick], [v16[0:R, t, j] for t, R in pick], [i16[0:R, t, j] for t, R in pick],
                         done=topk_done if j == 15 else None)

            def select(n, t):
                R = ROWS[t]
                s4 = v16[0:R, t].rearrange("p (h c) k -> p h c k", c=2)
                c4 = cand[0:R].rearrange("p h (i j) -> p h i j", i=TOPK)
                s1 = s4[:, :, 0].rearrange("p h (k o) -> p h k o", o=1).to_broadcast([R, PH, TOPK, TOPK])
                s2 = s4[:, :, 1].rearrange("p h (o k) -> p h o k", o=1).to_broadcast([R, PH, TOPK, TOPK])
                c.then(V.tensor_tensor, c4, s1, s2, ALU.add)
                two_best([cand[0:R, h] for h in range(PH)], [top[0:R, 0, h] for h in range(PH)], [top_u[0:R, 2, h] for h in range(PH)])
                c.settle()
                best = top[0:R, 0, :, 0:1].to_broadcast([R, PH, TOPK])
                c.also(V.tensor_tensor, top[0:R, 1], top[0:R, 0], best, ALU.subtract, signal=soft_in)
                c.also(V.tensor_scalar, top_u[0:R, 3], top_u[0:R, 2], 4, None, ALU.logical_shift_right)
                c.also(V.tensor_scalar, top_u[0:R, 4], top_u[0:R, 2], 15, None, ALU.bitwise_and)
                c.also(V.tensor_copy, i16f[0:R], i16[0:R, t])
                c.settle()
                for part in range(2):
                    c.also(V.tensor_copy, top[0:R, 5 + part], top_u[0:R, 3 + part])
                iota = cst("iota16")[0:R].rearrange("p (a b j) -> p a b j", a=1, b=1).to_broadcast([R, PH, TOPK, TOPK])
                for part in range(2):
                    c.settle()
                    place = top[0:R, 5 + part].rearrange("p h (k o) -> p h k o", o=1).to_broadcast([R, PH, TOPK, TOPK])
                    keys = i16f[0:R].rearrange("p (h c) (o k) -> p h c o k", c=2, o=1)[:, :, part].to_broadcast([R, PH, TOPK, TOPK])
                    c.also(V.tensor_tensor, onehot[0:R], place, iota, ALU.is_equal)
                    c.then(V.tensor_tensor, onehot[0:R], onehot[0:R], keys, ALU.mult)
                    c.then(V.tensor_reduce, top[0:R, 7 + part], onehot[0:R], AX.X, ALU.add)
                c.settle()
                flat = lambda x: x.rearrange("p h k -> p (h k)")
                c.also(V.scalar_tensor_tensor, out=expert[0:R, t], in0=flat(top[0:R, 7]), scalar=float(NKEYS), in1=flat(top[0:R, 8]),
                       op0=ALU.mult, op1=ALU.add)
                dve.wait_ge(soft_e, n + 1)
                c.also(V.tensor_reduce, den[0:R], top[0:R, 1], AX.X, ALU.add)
                c.then(V.reciprocal, den[0:R], den[0:R])
                c.then(V.tensor_tensor, gate[0:R, t].rearrange("p (h k) -> p h k", h=PH), top[0:R, 1],
                       den[0:R].rearrange("p (h o) -> p h o", o=1).to_broadcast([R, PH, TOPK]), ALU.mult, signal=sel_ready)

            def final(n, t):
                R = ROWS[t]
                yb = Y_BANKS[n % 2]
                dve.wait_ge(y_sum, n + 1)
                c.settle()
                for c2 in range(2):
                    hh = h1[0:R, t, 512 * c2:512 * c2 + 512]
                    c.also(V.tensor_tensor, hh, hh, bank[yb[c2]][0:R, :], ALU.add, signal=h2_ready if c2 else None)
                dve.wait_ge(h3_std, n + 1)
                c.also(V.reciprocal, rstd2[0:R, 5:6], ssq[0:R, 5 + t:6 + t])
                c.then(V.scalar_tensor_tensor, out=xn2[0:R, t], in0=h1[0:R, t], scalar=rstd2[0:R, 5:6], in1=g3[0:R],
                       op0=ALU.mult, op1=ALU.mult, signal=xn3_ready)
                dve.wait_ge(ple_sig, 2 * (n + 1))
                for c2 in range(2):
                    dve.wait_ge(ple_ready, 4 * n + 3 + c2)
                    ff = fin[0:R, 512 * c2:512 * c2 + 512]
                    c.also(V.tensor_tensor, ff, ff, bank[4 + c2][0:R, :], ALU.mult)
                c.then(V.tensor_tensor, h1[0:R, t], h1[0:R, t], fin[0:R], ALU.add, signal=y_out)

            select(0, NT)
            select(1, 0)
            dve.wait_ge(late_landed, 96)
            dve.wait_ge(sample_in, 16 * (NB + 2))
            for r in range(8):
                dve.wait_ge(g_landed[r], 16)
                c.also(V.tensor_tensor_reduce, gring[:, r, 0:D], gring[:, r, 0:D], sx, 1.0, 0.0, ALU.mult, ALU.add, dot[:, r:r + 1],
                       signal=dots if r == 7 else None)
            dve.wait_ge(gel, 1)
            c.also(V.tensor_tensor, coef, act_g, sgate, ALU.mult, signal=gated)
            final(0, NT)
            for t in range(NT):
                if t + 1 < NT:
                    select(t + 2, t + 1)
                c.settle()

                def coefs(i, g):
                    dve.wait_ge(gel, i * 4 + (t * 64 + g + 2))
                    V.tensor_tensor(coef[:, 2 * g:2 * g + 2], act_g[:, 2 * g:2 * g + 2], gate[:, t, bass.ds(i * 8 + 2 * g, 2)],
                                    ALU.mult).then_inc(gated, 1)

                with dve.Fori(0, SEL // RING_G) as i:
                    for g in range(4):
                        for s in (2 * g, 2 * g + 1):
                            dve.wait_ge(g_landed[s], i * 16 + (t * 256 + 32))
                            last = V.tensor_tensor_reduce(gring[:, s, 0:D], gring[:, s, 0:D], xn2[:, t], 1.0, 0.0,
                                                          ALU.mult, ALU.add, dot[:, s:s + 1])
                        last.then_inc(dots, 1)
                        if g >= 1:
                            coefs(i, g - 1)
                    coefs(i, 3)
                final(t + 1, t)

        @block.tensor
        def _(pe):
            mm, tr = nc.tensor.matmul, nc.tensor.transpose
            pe.wait_ge(consts_landed, 32)
            mean = cst("mean_model")
            for half, (a, b) in enumerate(HALVES):
                for k in range(KD):
                    pe.wait_ge(sq_ready, k + 1)
                    last = mm(bank[6 + half][:, 0:HALF], mean, qk[:, k, a:b], start=(k == 0), stop=(k == KD - 1))
                last.then_inc(mean1, 1)

            def weights(s):
                pe.wait_ge(w_in_slot[s % RING_W], 16 * (s // RING_W + 1))
                return wring[:, s % RING_W]

            def item(i):
                if i >= 6:
                    pe.wait_ge(proj_taken, i - 5)
                return bank[i % 6]

            made_items = [0]

            def project(s):
                w = weights(s).rearrange("p (k c) -> p k c", k=KD)
                for a, b in HALVES:
                    out = item(made_items[0])[:, 0:HALF]
                    made_items[0] += 1
                    for k in range(KD):
                        last = mm(out, w[:, k], xn[:, k, a:b], start=(k == 0), stop=(k == KD - 1))
                    last.then_inc(proj_ready, 1)

            def head_means(j):
                pe.wait_ge(qksq, 2 * (j + 1))
                if j >= 1:
                    pe.wait_ge(qkstd, 2 * j)
                for half, (a, b) in enumerate(HALVES):
                    mm(bank[6 + half][:, 0:HALF], cst("mean_head"), qk_sq[:, j % 2, a:b], start=True, stop=True).then_inc(qkmean, 1)

            pe.wait_ge(xn_ready, KD)
            for j in range(8):
                project(S_QA + j)
                if j >= 1:
                    head_means(j - 1)
            pe.wait_ge(wab_landed, 48)
            for a, b in HALVES:
                out = item(made_items[0])[0:RANK, 0:HALF]
                made_items[0] += 1
                for k in range(KD):
                    last = mm(out, abw[:, k], xn[:, k, a:b], start=(k == 0), stop=(k == KD - 1))
                last.then_inc(proj_ready, 1)
            head_means(7)
            pe.wait_ge(qk_done, 4)
            pe.wait_ge(qkstd, 16)
            for b in range(NB):
                if b >= 2:
                    pe.wait_ge(qb_taken, b - 1)
                for j in range(4):
                    last = mm(bank[6 + b % 2][:, j * P:j * P + P], qk[:, j, SEQ + b:SEQ + b + 1].to_broadcast([P, P]), ident,
                              start=True, stop=True)
                last.then_inc(qb_ready, 1)
            for j in range(4):
                project(S_QB + j)
            pe.wait_ge(proj_taken, AB_ITEM + 2)
            for m in range(2):
                for a, b in HALVES:
                    mm(item(made_items[0])[:, 0:HALF], alw[:, m * P:m * P + P], abT[0:RANK, a:b], start=True, stop=True).then_inc(proj_ready, 1)
                    made_items[0] += 1
            for s0 in (S_VA, S_VB):
                for q in range(4):
                    w = weights(s0 + q).rearrange("p (k c) -> p k c", k=2)
                    for t in range(5):
                        out = (item(made_items[0] + t) if q == 0 else bank[(made_items[0] + t) % 6])[0:ROWS[t], :]
                        for kk in range(2):
                            k = 2 * q + kk
                            last = mm(out, xn[:, k, t * P:t * P + ROWS[t]], w[:, kk], start=(k == 0), stop=(k == KD - 1))
                        if q == 3:
                            last.then_inc(proj_ready, 1)
                    if q < 3:
                        last.then_inc(kstep, 1)
                made_items[0] += 5
            for j in range(4):
                project(S_RB + j)
            for j in range(16):
                project(S_GA + j)

            pe.wait_ge(dec_sp, 4)
            pe.wait_ge(proj_taken, N_ITEMS)
            for q in range(4):
                o = 512 * q
                late = lambda x: x.rearrange("p (r g) -> p r g", g=PAGES)
                mm(bank[q][:, :], cst("neg_tri"), tmp[:, 2048 + o:2560 + o], start=True, stop=True)
                mm(late(bank[q][:, :])[:, :, 1:PAGES], cst("neg_ones"), late(tmp[:, 4096 + o:4608 + o])[:, :, 0:PAGES - 1],
                   start=False, stop=True, skip_group_check=True).then_inc(dec_z, 1)

            pe.wait_ge(dec_arg, 4)
            pe.wait_ge(gla_in, 1)
            for m in range(2):
                for t in range(NT):
                    last = tr(bank[m][:, t * P:t * P + P], kd[:, m, t * P:t * P + P], ident)
                last.then_inc(kd_tr, 1)
            pe.wait_ge(gla_in, 3)
            qrow = lambda par: slice(64 * par, 64 * par + 64)
            for u in range(2):
                if u == 1:
                    pe.wait_ge(o_taken, 2)
                for par in range(2):
                    for tt in range(2):
                        for m in range(2):
                            t = slice((2 * u + tt) * P, (2 * u + tt) * P + P)
                            last = mm(bank[2 + par][:, (2 * tt + m) * P:(2 * tt + m) * P + P], kt[qrow(par), m, t], qt[qrow(par), m, t],
                                      start=True, stop=True)
                    last.then_inc(sc_ready, 1)
                pe.wait_ge(kd_rows, 2)
                for c2 in range(2):
                    for tt in range(2):
                        for m in range(2):
                            for par in range(2):
                                t = 2 * u + tt
                                h = 2 * m + par
                                rows = qrow(c2)
                                last = mm(bank[(4 if u == 0 else 0) + c2][qrow(par), (2 * tt + m) * P:(2 * tt + m) * P + P],
                                          kdr[rows, t, m, 64 * par:64 * par + 64], vab[rows, t, 512 + h * P:512 + h * P + P],
                                          start=True, stop=True)
                last.then_inc(u_ready, 1)
                pe.wait_ge(sc_done, 2 * u + 2)
                pe.wait_ge(states_done, u + 1)
                for par in range(2):
                    for tt in range(2):
                        for m in range(2):
                            t, h, col = 2 * u + tt, 2 * m + par, (2 * tt + m) * P
                            mm(bank[2 + par][:, col:col + P], vab[:, t, 512 + h * P:512 + h * P + P], sc_v[:, par, 2 * tt + m],
                               start=True, stop=True)
                            for c2 in range(2):
                                last = mm(bank[2 + par][:, col + 64 * c2:col + 64 * c2 + 64], states[qrow(par), 2 * t + c2, m],
                                          qe[qrow(par), m, t * P + 64 * c2:t * P + 64 * c2 + 64], start=False, stop=True,
                                          skip_group_check=True)
                    last.then_inc(o_ready, 1)
            for b in range(NB):
                if b >= 1:
                    pe.wait_ge(vb_taken, b)
                mm(bank[7][:, :], ident[0:NB, b:b + 1].to_broadcast([NB, P]), vab[0:NB, NT, 512:1024], start=True, stop=True).then_inc(vb_ready, 1)
            pe.wait_ge(ss_ready, 1)
            for par in range(2):
                for m in range(2):
                    for b in range(NB):
                        last = mm(bank[7 if par == 0 else 1][:, m * NB + b:m * NB + b + 1], sstate[qrow(par), b, m],
                                  qkb[qrow(par), m, SEQ + b:SEQ + b + 1], start=True, stop=True)
                last.then_inc(so_ready, 1)
            for h in range(GH):
                pe.wait_ge(ob_sq, h + 1)
                if h >= 1:
                    pe.wait_ge(ob_std, 2 * h)
                for half, (a, b) in enumerate(HALVES):
                    mm(bank[4 + half][:, 0:HALF], cst("mean_gdv"), ob_tmp[:, h % 2, a:b], start=True, stop=True).then_inc(ob_mean, 1)

            pe.wait_ge(dec_w, 4)
            pe.wait_ge(yb_ready, GH)
            w4 = zs.rearrange("p (b h g) -> p b g h", b=NB, h=H)
            for h in range(H):
                m, rows = h // 2, qrow(h % 2)
                if h >= 1:
                    pe.wait_ge(att_w, NT * h)
                for n in range(NT):
                    mm(bank[n][:, 0:SEQ - P * n], qk[rows, 4 + m, n * P:n * P + P], qk[rows, m, n * P:SEQ],
                       start=True, stop=True).then_inc(z_ready, 1)
                mm(bank[6][:, 8 * h:8 * h + 8], ident, cst("zeros"), start=True, stop=True)
                with pe.Fori(0, PAGES // RING_V) as g:
                    for s in range(RING_V):
                        pe.wait_ge(v_landed[s], g * 16 + (h * (16 * PAGES // RING_V) + 16))
                        for i in range(4):
                            last = mm(bank[6][:, 8 * h + 2 * i:8 * h + 2 * i + 2], vring[:, s, i * P:i * P + P],
                                      w4[:, h, bass.ds(g * -RING_V + (PAGES - 1 - s), 1), 2 * i:2 * i + 2].rearrange("p g h -> p (g h)"),
                                      start=False, stop=True, skip_group_check=True)
                        last.then_inc(v_free, 1)
                last = mm(bank[6][:, 8 * h:8 * h + 8], ident, cst("zeros"), start=False, stop=True, skip_group_check=True)
                if h == H - 1:
                    last.then_inc(v_done, 1)
                pe.wait_ge(att_sp, h + 1)
                at = [2560, 3072, 3456, 3712]
                for n in range(NT):
                    w = SEQ - P * n
                    mm(bank[n][:, 0:w], cst("neg_tri"), tmp[:, at[n]:at[n] + w], start=False, stop=True, skip_group_check=True)
                    for k2 in range(n + 1, NT):
                        mm(bank[n][:, P * (k2 - n):w], cst("neg_ones"), tmp[:, at[k2]:at[k2] + SEQ - P * k2],
                           start=False, stop=True, skip_group_check=True)
                    mm(bank[n][:, 0:P], ident, cst("neg_mask"), start=False, stop=True, skip_group_check=True).then_inc(acc_ready, 1)
                if m >= 2:
                    pe.wait_ge(y_taken, m - 1)
                for n in range(NT):
                    pe.wait_ge(att_w, NT * h + n + 1)
                    last = mm(bank[4 + m % 2][rows, P * n:SEQ], vab[:, n, h * HD:h * HD + HD], tmp[:, at[n] + 1280:at[n] + 1280 + SEQ - P * n],
                              start=(n == 0), stop=(n == NT - 1), skip_group_check=True)
                if h % 2 == 1:
                    last.then_inc(y_ready, 1)

            pe.wait_ge(y_taken, 6)
            for m in range(8):
                w = weights(S_UP + m).rearrange("p (u k c) -> p u k c", u=2, k=4)
                for q in range(4):
                    i = 4 * m + q
                    a, b = HALVES[q % 2]
                    if i >= 8:
                        pe.wait_ge(up_taken, i - 7)
                    src = yaT if q < 2 else srb
                    for k in range(4):
                        last = mm(bank[i % 8][:, 0:HALF], w[:, q // 2, k], src[:, k, a:b], start=(k == 0), stop=(k == 3))
                    last.then_inc(up_ready, 1)
            pe.wait_ge(mix_ready, 8)
            for half in range(2):
                for q in range(4):
                    w = weights(S_WO + 4 * half + q).rearrange("p (k c) -> p k c", k=2)
                    for t in range(5):
                        i = 5 * half + t
                        if q == 0 and i >= 8:
                            pe.wait_ge(wo_taken, i - 7)
                        for kk in range(2):
                            k = 2 * q + kk
                            last = mm(bank[i % 8][0:ROWS[t], :], mixT[:, k, t * P:t * P + ROWS[t]], w[:, kk], start=(k == 0), stop=(k == KD - 1))
                        if q == 3:
                            last.then_inc(wo_ready, 1)
                    if q < 3:
                        last.then_inc(kstep, 1)

            pe.wait_ge(wo_taken, 10)
            for t in range(5):
                R = ROWS[t]
                pe.wait_ge(xn2_ready, t + 1)
                for k in range(KD):
                    n = 2 * t + (k // 4 if t < NT else 0)
                    if k % 4 == 0 and n >= 6:
                        pe.wait_ge(x2t_taken, n - 5)
                    col = (k % 4) * P if t < NT else k * NB
                    last = tr(bank[2 + n % 6][:, col:col + R], xn2[0:R, t, k * P:k * P + P], ident[0:R, 0:R])
                    if k == KD - 1 or (k == 3 and t < NT):
                        last.then_inc(x2t_ready, 1)

            def scores(j):
                pe.wait_ge(pq_taken, 2 * (j + 1))
                if j >= 2:
                    pe.wait_ge(s_taken, 2 * (j - 1))
                for t in range(NT):
                    last = mm(bank[4 + j % 2][:, t * P:t * P + P], qp[:, j % 2, t * P:t * P + P], sk[:, j], start=True, stop=True)
                last.then_inc(s_ready, 1)
                mm(bank[6 + j % 2][0:NB, 0:P], qp[:, j % 2, SEQ:T], sk[:, j], start=True, stop=True).then_inc(s_ready, 1)

            pe.wait_ge(x2t_taken, 9)
            for j in range(16):
                w = weights(S_PQ + j).rearrange("p (k c) -> p k c", k=KD)
                for half, (a, b) in enumerate(HALVES):
                    i = 2 * j + half
                    if i >= 4:
                        pe.wait_ge(pq_taken, i - 3)
                    for k in range(KD):
                        last = mm(bank[i % 4][:, 0:HALF], w[:, k], xn2T[:, k, a:b], start=(k == 0), stop=(k == KD - 1))
                    last.then_inc(pq_ready, 1)
                if j >= 1:
                    scores(j - 1)
            scores(15)

            pe.wait_ge(s_taken, 32)
            zrow = cst("zeros")[:, 0:1].to_broadcast([P, 512])
            pe.wait_ge(late_landed, 96)

            def final(n, t):
                R = ROWS[t]
                pe.wait_ge(xn3_ready, n + 1)
                if n >= 1:
                    pe.wait_ge(y_out, n)
                for k in range(KD):
                    last = tr(bank[4 + k // 4][:, (k % 4) * R:(k % 4) * R + R], xn2[0:R, t, k * P:k * P + P], ident[0:R, 0:R])
                    if k % 4 == 3:
                        last.then_inc(x3t_ready, 1)
                for c2 in range(2):
                    if c2 == 0:
                        pe.wait_ge(x3t_taken, 2 * (n + 1))
                    for k in range(KD):
                        last = mm(bank[6 + c2][0:R, :], xn3T[:, k, 0:R], wpg[:, k, 512 * c2:512 * c2 + 512], start=(k == 0), stop=(k == KD - 1))
                    last.then_inc(ple_ready, 1)
                for c2 in range(2):
                    for k in range(2):
                        last = mm(bank[4 + c2][0:R, :], pT[:, k, t * P:t * P + R], ple_w[:, k, 512 * c2:512 * c2 + 512], start=(k == 0), stop=(k == 1))
                    last.then_inc(ple_ready, 1)

            pe.wait_ge(diag_ready, 1)
            yb = Y_BANKS[0]
            for r in range(8):
                for c2 in range(2):
                    last = mm(bank[yb[c2]][0:NB, :], diag[:, r, 0:NB], gring[:, r, D + 512 * c2:D + 512 * c2 + 512],
                              start=(r == 0), stop=(r == 7), skip_group_check=True)
                if r % 2 == 1:
                    last.then_inc(g_used, 1)
            mm(bank[yb[1]][0:NB, :], ident[:, 0:NB], zrow, start=False, stop=True, skip_group_check=True).then_inc(y_sum, 1)
            final(0, NT)
            for t in range(NT):
                yb = Y_BANKS[(t + 1) % 2]
                for c2 in range(2):
                    mm(bank[yb[c2]][:, :], ident, zrow, start=True, stop=True, skip_group_check=True)
                with pe.Fori(0, SEL // RING_G) as i:
                    for g in range(4):
                        pe.wait_ge(diag_ready, i * 4 + (t * 64 + g + 2))
                        for s in (2 * g, 2 * g + 1):
                            for c2 in range(2):
                                last = mm(bank[yb[c2]][:, :], diag[:, s], gring[:, s, D + 512 * c2:D + 512 * c2 + 512],
                                          start=False, stop=True, skip_group_check=True)
                        last.then_inc(g_used, 1)
                for c2 in range(2):
                    last = mm(bank[yb[c2]][:, :], ident, zrow, start=False, stop=True, skip_group_check=True)
                last.then_inc(y_sum, 1)
                final(t + 1, t)


def kernel(x_prompt, x_sample, p_prompt, p_sample, cache_k, cache_v, state_gla, page_table, norm1_g, w_in, b_gate,
           qa_norm_g, ka_norm_g, sb_bias, w_alpha, b_alpha, ob_norm_g, w_up_a, w_up_b, w_o, norm2_g, w_peer_q,
           peer_sub_keys, expert_u, expert_v, norm3_g, w_ple, w_ple_gate):
    import concourse.bacc as bacc
    from concourse.bass_utils import run_bass_kernel_spmd

    n = np.asarray

    def tiles(w):
        k, m = w.shape[0] // P, w.shape[1] // P
        return w.reshape(k, P, m, P).transpose(2, 1, 0, 3).reshape(m, P, k * P)

    def by_pairs(w):
        j = w.shape[1] // 512
        return w.reshape(4, 2, P, j, 512).transpose(3, 0, 2, 1, 4).reshape(4 * j, P, 1024)

    def by_feature(a):
        return a.reshape(a.shape[0], -1, P).transpose(2, 1, 0)

    wi = n(w_in)[0]
    cut = np.cumsum([512, 512, 512, 256, 256, 512, 512, 16, 1024, 1024])
    qa, ka, va, qb, kb, vb, rb, ab, gza, gzb = np.split(wi, cut[:-1], axis=1)
    up = np.stack([tiles(n(w_up_a)[0]), tiles(n(w_up_b)[0])], axis=2)
    w_stream = np.concatenate([
        tiles(qa), tiles(ka), tiles(qb), tiles(kb), by_pairs(va), by_pairs(vb), tiles(rb), tiles(gza), tiles(gzb),
        up.reshape(8, P, 1024), by_pairs(n(w_o)[0]), tiles(n(w_peer_q)[0])])
    col = lambda a: a.reshape(-1, P).T
    vecs = np.concatenate([
        col(n(norm1_g)[0]), np.tile(n(qa_norm_g)[0], 2)[:, None], np.tile(n(ka_norm_g)[0], 2)[:, None],
        col(n(b_alpha)[0]), col(n(b_gate)[0].reshape(-1)), n(ob_norm_g)[0][:, None]], axis=1)
    x = np.concatenate([n(x_prompt)[0], n(x_sample)[:, 0]])
    p = np.concatenate([n(p_prompt)[0, 0], n(p_sample)[0, :, 0]])
    feeds = {
        "consts": _consts(),
        "vecs": vecs,
        "xT": by_feature(x),
        "x_rows": x,
        "w_ab": ab.reshape(KD, P, RANK).transpose(1, 0, 2),
        "w_alpha": n(w_alpha)[0],
        "sb_bias": n(sb_bias)[0],
        "w_stream": w_stream,
        "cache_k": n(cache_k)[0].reshape(-1, P, PAGE_ROW),
        "cache_v": n(cache_v)[0].reshape(-1, P, PAGE_ROW),
        "page_table": n(page_table).reshape(1, -1),
        "state": n(state_gla)[0].reshape(NB, 2, 2 * GDK, GDV).transpose(2, 0, 1, 3),
        "norm2_g": n(norm2_g)[0],
        "norm3_g": n(norm3_g)[0],
        "sub_keysT": n(peer_sub_keys)[0].reshape(16, NKEYS, P).transpose(2, 0, 1),
        "experts": np.concatenate([n(expert_u)[0], n(expert_v)[0]], axis=1),
        "pT": by_feature(p),
        "w_ple": n(w_ple)[0].reshape(2, P, D).transpose(1, 0, 2),
        "w_ple_gate": n(w_ple_gate)[0].reshape(KD, P, D).transpose(1, 0, 2),
    }
    outs = {"y": (T, D), "new_kT": (512, T), "new_v": (T, 512), "gla_prompt": (P, 2, GDV), "gla_sample": (P, NB, 2, GDV)}
    nc = bacc.Bacc("TRN2", target_bir_lowering=False, num_devices=1)
    aps, arrays = {}, {}
    for name, a in feeds.items():
        arrays[name + "_in"] = np.ascontiguousarray(a)
        aps[name] = nc.dram_tensor(name + "_in", a.shape, mybir.dt.from_np(a.dtype), kind="ExternalInput").ap()
    for name, shape in outs.items():
        aps[name] = nc.dram_tensor(name + "_out", shape, F32, kind="ExternalOutput").ap()
    build(nc, aps)
    r = run_bass_kernel_spmd(nc, [arrays], core_ids=[0]).results[0]
    y, kT, v = r["y_out"], r["new_kT_out"], r["new_v_out"]
    k = kT.T.reshape(T, H, HD)
    v = v.reshape(T, H, HD)
    sp = r["gla_prompt_out"].reshape(2, GDK, 2, GDV).transpose(2, 0, 1, 3).reshape(1, 1, GH, GDK, GDV)
    ss = r["gla_sample_out"].reshape(2, GDK, NB, 2, GDV).transpose(2, 3, 0, 1, 4).reshape(1, NB, GH, GDK, GDV)
    return (y[None, :SEQ], y[SEQ:, None], k[None, None, :SEQ], v[None, None, :SEQ], sp,
            k[None, SEQ:, None], v[None, SEQ:, None], ss)
```

```python
from contextlib import ExitStack

import numpy as np

import concourse.bass as bass
from concourse import mybir

F32 = mybir.dt.float32
U32 = mybir.dt.uint32
I32 = mybir.dt.int32
ALU = mybir.AluOpType
ACT = mybir.ActivationFunctionType
AX = mybir.AxisListType

P = 128
D = 1024
KD = D // P
SEQ = 512
NB = 8
T = SEQ + NB
HALF = T // 2
HALVES = ((0, HALF), (HALF, T))
NT = SEQ // P
ROWS = [P] * NT + [NB]
H = 8
HD = 64
GH = 4
GDK, GDV = 64, 128
CHUNK = 64
NCH = SEQ // CHUNK
RANK = 16
TAU = 16.0
PAGES = 32
PAGE_ROW = H * HD
PH = 8
NKEYS = 128
TOPK = 16
SEL = PH * TOPK
PLE = 256
EPS = 1e-6
NEG = -1e30
LOWEST = -3.0e38
Y_BANKS = ((2, 3), (0, 1))

RING_K = 8
PRODS = 4
RING_V = 8
V_EARLY = 4
V_BANK = (4, 5, 7, 6, 6, 7, 6, 7)
FOLD_AT = {0: 4, 3: 5, 6: 6}
STD_BUF = (0, 1, 0, 1, 2, 3, 4, 0)
RING_W = 4
RING_G = 8
SEGMENTS = 8
SEG = SEL // RING_G // SEGMENTS

S_QA, S_KA, S_QB, S_KB, S_VA, S_VB, S_RB, S_GA, S_GB = 0, 4, 8, 10, 12, 16, 20, 24, 32
S_UP, S_WO, S_PQ, S_END = 40, 48, 56, 72

CONSTS = {}


def _consts():
    i, j = np.arange(P)[:, None], np.arange(P)[None, :]
    pieces = [
        ("ident", i == j),
        ("mean_model", np.full((P, P), 1.0 / D)),
        ("mean_head", (i // HD == j // HD) / float(HD)),
        ("mean_gdv", np.full((P, P), 1.0 / GDV)),
        ("neg_tri", -1.0 * (i >= j)),
        ("neg_ones", np.full((P, P), -1.0)),
        ("neg_mask", NEG * (i >= j)),
        ("keep_mask", i < j),
        ("gla_mask", (i <= j) & (i // CHUNK == j // CHUNK)),
        ("chunk_reset", np.broadcast_to(np.arange(SEQ) % CHUNK != 0, (P, SEQ))),
        ("page_reset", np.broadcast_to(np.arange(512) % PAGES != 0, (P, 512))),
        ("iota16", np.broadcast_to(np.arange(TOPK), (P, TOPK))),
        ("sample_of", np.arange(P)[:, None] // (P // NB) == np.arange(NB)[None, :]),
        ("zeros", np.zeros((P, NB))),
        ("eps", np.full((P, 1), EPS)),
        ("one", np.ones((P, 1))),
    ]
    at = 0
    for name, a in pieces:
        CONSTS[name] = (at, at + a.shape[1])
        at += a.shape[1]
    return np.concatenate([np.asarray(a, np.float32) for _, a in pieces], axis=1)


N_CONST = _consts().shape[1]

V_G1, V_QG, V_KG, V_BA, V_BG, V_OG, N_VEC = 0, 8, 9, 10, 12, 28, 29


class Steps:

    def __init__(self, eng, own):
        self.eng, self.own, self.count, self.last = eng, own, {}, None

    def also(self, op, *args, signal=None, **kw):
        sem = signal if signal is not None else self.own
        key = sem.name
        self.count[key] = self.count.get(key, 0) + 1
        op(*args, **kw).then_inc(sem, 1)
        self.last = (sem, self.count[key])

    def settle(self):
        if self.last is not None:
            self.eng.wait_ge(*self.last)

    def then(self, op, *args, signal=None, **kw):
        self.settle()
        self.also(op, *args, signal=signal, **kw)


def lay(start, sizes):
    out = {}
    for name, n in sizes:
        out[name] = (start, start + n)
        start += n
    return out, start


def build(nc, A):
    with ExitStack() as ctx:
        COLS = 53200
        arena = ctx.enter_context(nc.sbuf_tensor("arena", [P, COLS], F32))
        bank = [ctx.enter_context(nc.psum_tensor(f"bank{i}", [P, 512], F32))[:, :] for i in range(8)]
        made = {}

        def sem(name):
            if name not in made:
                made[name] = ctx.enter_context(nc.semaphore(name))
            return made[name]

        def sems(name, n):
            return [sem(f"{name}{i}") for i in range(n)]

        kept, at = lay(0, [("consts", N_CONST), ("vecs", 32), ("wring", RING_W * 1024)])
        first, end1 = lay(at, [
            ("gates", 16 * T), ("vab", 5 * 1024), ("srb", 4 * T), ("qk", 8 * T), ("qkb", 4 * T),
            ("zs", 2048), ("vring", RING_V * PAGE_ROW), ("la", 2 * T), ("abT", T), ("rowh", H), ("v_cols", 4 * NB), ("pt", 256), ("abw", 8 * RANK), ("alw", 256),
            ("xn", 8 * T), ("xT", 8 * T), ("kring", RING_K * PAGE_ROW), ("prod", PRODS * PAGE_ROW)])
        second, end2 = lay(first["xn"][0], [
            ("tmp", 6144), ("cum", 2 * SEQ), ("qt", 2 * SEQ), ("kt", 2 * SEQ), ("qe", 2 * SEQ), ("kd", 2 * SEQ),
            ("gsmall", 64), ("states", 2 * (NCH + 1) * GDV), ("sstate", NB * 2 * GDV), ("kdr", 2 * SEQ)])
        assert end1 <= COLS and end2 <= COLS, (end1, end2)
        at3 = first["vab"][1]
        third, end3 = lay(at3, [
            ("xn2", 5 * D), ("g2", D), ("v16", 5 * 256), ("i16", 5 * 256), ("cand", 2048), ("onehot", 2048),
            ("expert", 5 * SEL), ("gate", 5 * SEL), ("top", 10 * SEL), ("i16f", 256), ("small", 128),
            ("xn2T", 8 * T), ("sk", 16 * P), ("qp", 2 * T), ("s_all", 5 * 2048)])
        assert end3 <= COLS, end3
        fourth, end4 = lay(third["xn2T"][0], [("gring", RING_G * 2 * D)])
        assert end4 <= end3
        fifth, end5 = lay(first["gates"][0], [("wpg", KD * D)])
        assert end5 <= first["vab"][0]
        sixth, end6 = lay(end4, [("diag", RING_G * P)])
        assert end6 <= COLS, end6
        seventh, end7 = lay(kept["wring"][0], [("ple_w", 2 * D), ("xn3T", D), ("sx", D)])
        assert end7 <= kept["wring"][1]
        eighth = {"pT": (P, P + 2 * T), "g3": third["g2"], "fin": (third["onehot"][0], third["onehot"][0] + D)}
        maps = {}
        for m in (kept, first, second, third, fourth, fifth, sixth, seventh, eighth):
            maps.update(m)

        def view(name, **dims):
            a, b = maps[name]
            return arena[:, a:b]

        def cst(name):
            a, b = CONSTS[name]
            return arena[:, maps["consts"][0] + a:maps["consts"][0] + b]

        vecs = view("vecs")
        ident = cst("ident")
        wring = view("wring").rearrange("p (s c) -> p s c", s=RING_W)
        gates = view("gates").rearrange("p (m t) -> p m t", m=16)
        mixT = gates[:, 0:8]
        vab = view("vab").rearrange("p (t c) -> p t c", t=5)
        h1 = vab
        srb = view("srb").rearrange("p (m t) -> p m t", m=4)
        qk = view("qk").rearrange("p (m t) -> p m t", m=8)
        qkb = view("qkb").rearrange("p (m t) -> p m t", m=4)
        zs = view("zs")
        vring = view("vring").rearrange("p (s c) -> p s c", s=RING_V)
        la = view("la").rearrange("p (m t) -> p m t", m=2)
        abT = view("abT")
        bias_row = view("rowh")
        xn = view("xn").rearrange("p (m t) -> p m t", m=8)
        xT = view("xT").rearrange("p (m t) -> p m t", m=8)
        qbc = view("xT")[:, 0:NB * PAGE_ROW].rearrange("p (b c) -> p b c", b=NB)
        kring = view("kring").rearrange("p (s c) -> p s c", s=RING_K)
        prod = view("prod").rearrange("p (s c) -> p s c", s=PRODS)
        tmp = view("tmp")
        cum = view("cum").rearrange("p (m t) -> p m t", m=2)
        sc_v = view("cum").rearrange("p (q a c) -> p q a c", q=2, a=4)
        qt = view("qt").rearrange("p (m t) -> p m t", m=2)
        kt = view("kt").rearrange("p (m t) -> p m t", m=2)
        qe = view("qe").rearrange("p (m t) -> p m t", m=2)
        kd = view("kd").rearrange("p (m t) -> p m t", m=2)
        a0 = maps["qt"][0]
        yaT = arena[:, a0:a0 + 4 * T].rearrange("p (m t) -> p m t", m=4)
        assert a0 + 4 * T <= maps["qe"][1]
        states = view("states").rearrange("p (c m e) -> p c m e", c=NCH + 1, m=2)
        sstate = view("sstate").rearrange("p (b m e) -> p b m e", b=NB, m=2)
        kdr = view("kdr").rearrange("p (t m c) -> p t m c", t=NT, m=2)
        page_table = view("pt").bitcast(I32)
        abw = view("abw").rearrange("p (k c) -> p k c", k=KD)
        alw = view("alw")[0:RANK]
        qk_sq = view("vring")[:, 0:2 * T].rearrange("p (u t) -> p u t", u=2)
        qk_std = view("vring")[:, 2 * T:7 * T].rearrange("p (u t) -> p u t", u=5)
        v_own = [view("abT")[0:H, 0:512], tmp[0:H, 5168:5680]]
        v_cols = view("v_cols").rearrange("p (m b) -> p m b", m=4)
        gsmall = view("gsmall")
        chunk_decay, sample_decay = gsmall[:, 0:16], gsmall[:, 16:32].rearrange("p (m b) -> p m b", m=2)
        kv = tmp[:, 0:2048].rearrange("p (b m e) -> p b m e", b=NB, m=2)
        ob = tmp[:, 2048:2048 + 4 * T].rearrange("p (m t) -> p m t", m=4)
        ob_tmp = tmp[:, 0:3 * T].rearrange("p (u t) -> p u t", u=3)
        g2, g3 = view("g2"), view("g3")
        xn2 = view("xn2").rearrange("p (t c) -> p t c", t=5)
        xn2T = view("xn2T").rearrange("p (m t) -> p m t", m=8)
        sk = view("sk").rearrange("p (j n) -> p j n", j=16)
        qp = view("qp").rearrange("p (u t) -> p u t", u=2)
        s_all = view("s_all").rearrange("p (t j n) -> p t j n", t=5, j=16)
        v16 = view("v16").rearrange("p (t j n) -> p t j n", t=5, j=16)
        i16 = view("i16").bitcast(U32).rearrange("p (t j n) -> p t j n", t=5, j=16)
        cand = view("cand").rearrange("p (h n) -> p h n", h=PH)
        onehot = view("onehot").rearrange("p (h k j) -> p h k j", h=PH, k=TOPK)
        i16f = view("i16f").rearrange("p (j n) -> p j n", j=16)
        expert = view("expert").bitcast(U32).rearrange("p (t c) -> p t c", t=5)
        gate = view("gate").rearrange("p (t c) -> p t c", t=5)
        top = view("top").rearrange("p (u h k) -> p u h k", u=10, h=PH)
        top_u = view("top").bitcast(U32).rearrange("p (u h k) -> p u h k", u=10, h=PH)
        small = view("small")
        ssq, rstd2, den = small[:, 0:10], small[:, 10:20], small[:, 20:28]
        dot, act_g, coef = small[:, 32:40], small[:, 40:48], small[:, 48:56]
        slot_idx = view("small").bitcast(U32)[:, 56:64]
        idx_guard = view("small").bitcast(U32)[:, 80:82]
        zero_u = cst("zeros")[:, 0:2].bitcast(U32)
        sidx, sgate = view("small").bitcast(U32)[:, 64:72], small[:, 72:80]
        gring = view("gring").rearrange("p (s c) -> p s c", s=RING_G)
        wpg = view("wpg").rearrange("p (k c) -> p k c", k=KD)
        pT = view("pT").rearrange("p (m t) -> p m t", m=2)
        ple_w = view("ple_w").rearrange("p (m c) -> p m c", m=2)
        xn3T = view("xn3T").rearrange("p (k t) -> p k t", k=KD)
        fin = view("fin")
        diag = view("diag").rearrange("p (s c) -> p s c", s=RING_G)
        sx = view("sx")

        scratch_e = nc.dram_tensor("scratch_expert", (NB, SEL), U32, kind="Internal").ap()
        scratch_g = nc.dram_tensor("scratch_gate", (NB, SEL), F32, kind="Internal").ap()
        scratch_x = nc.dram_tensor("scratch_x", (NB, D), F32, kind="Internal").ap()

        items = []
        ends = {}

        def tile_items(s, kind, j):
            for half in range(2):
                items.append((kind, j, half))
            ends[s] = len(items)
        for j in range(8):
            tile_items(S_QA + j, "qk", j)
        AB_ITEM = len(items)
        items += [("ab", 0, 0), ("ab", 0, 1)]
        for j in range(4):
            tile_items(S_QB + j, "qkb", j)
        ALPHA_ITEM = len(items)
        items += [("alpha", m, half) for m in range(2) for half in range(2)]
        for s, kind in ((S_VA, "va"), (S_VB, "vb")):
            items += [(kind, t, 0) for t in range(5)]
            ends[s + 3] = len(items)
        for j in range(4):
            tile_items(S_RB + j, "rb", j)
        for j in range(16):
            tile_items(S_GA + j, "gate", j)
        N_ITEMS = len(items)

        w_in_slot = sems("w_landed", RING_W)
        k_landed = sems("k_landed", RING_K)
        v_landed = sems("v_landed", RING_V)
        v_early = sems("v_early", RING_V)
        consts_landed, x_landed, table_landed = sem("consts_landed"), sem("x_landed"), sem("table_landed")
        wab_landed, state_landed = sem("wab_landed"), sem("state_landed")
        sq_ready, mean1, std1, xn_ready = sem("sq_ready"), sem("mean1"), sem("std1"), sem("xn_ready")
        proj_ready, proj_taken, kstep = sem("proj_ready"), sem("proj_taken"), sem("kstep")
        qksq, qkmean, qkstd, qk_done = sem("qksq"), sem("qkmean"), sem("qkstd"), sem("qk_done")
        qb_ready, qb_taken = sem("qb_ready"), sem("qb_taken")
        k_mul, k_free = sem("k_mul"), sem("k_free")
        act_steps, dve_steps, pool_steps = sem("act_steps"), sem("dve_steps"), sem("pool_steps")
        out_done = sem("out_done")
        v_free = sem("v_free")
        zb_ready, dec_l, dec_sp, dec_z, dec_arg, dec_w = (sem(n) for n in ("zb_ready", "dec_l", "dec_sp", "dec_z", "dec_arg", "dec_w"))
        la_in, la_ready, gla_d, gla_e, gla_in = (sem(n) for n in ("la_in", "la_ready", "gla_d", "gla_e", "gla_in"))
        kd_tr, kd_rows, sc_ready, sc_done, u_ready, states_done, o_ready, o_taken = (
            sem(n) for n in ("kd_tr", "kd_rows", "sc_ready", "sc_done", "u_ready", "states_done", "o_ready", "o_taken"))
        vb_ready, vb_taken, ss_ready, so_ready, ob_sq, ob_mean, ob_std, yb_ready = (
            sem(n) for n in ("vb_ready", "vb_taken", "ss_ready", "so_ready", "ob_sq", "ob_mean", "ob_std", "yb_ready"))
        z_ready, att_l, att_r, att_sp, acc_ready, att_w, y_ready, y_taken, ya_ready = (
            sem(n) for n in ("z_ready", "att_l", "att_r", "att_sp", "acc_ready", "att_w", "y_ready", "y_taken", "ya_ready"))
        v_masked, v_done, v_taken = sem("v_masked"), sem("v_done"), sem("v_taken")
        up_ready, up_taken, mix_ready = sem("up_ready"), sem("up_taken"), sem("mix_ready")
        wo_ready, wo_taken, h_landed = sem("wo_ready"), sem("wo_taken"), sem("h_landed")
        rows_landed = sem("rows_landed")
        h_sq, h_std, xn2_ready, x2t_ready, x2t_taken = (sem(n) for n in ("h_sq", "h_std", "xn2_ready", "x2t_ready", "x2t_taken"))
        pq_ready, pq_taken, s_ready, s_taken, topk_done = (sem(n) for n in ("pq_ready", "pq_taken", "s_ready", "s_taken", "topk_done"))
        sel_ready, soft_in, soft_e = sem("sel_ready"), sem("soft_in"), sem("soft_e")
        g_landed = sems("g_landed", RING_G)
        dots, gel, gated, diag_ready, g_used = (sem(n) for n in ("dots", "gel", "gated", "diag_ready", "g_used"))
        idx_copied = sem("idx_copied")
        y_sum, h2_ready, h3_std, xn3_ready, x3t_ready, x3t_taken, ple_ready, ple_sig, y_out = (
            sem(n) for n in ("y_sum", "h2_ready", "h3_std", "xn3_ready", "x3t_ready", "x3t_taken", "ple_ready", "ple_sig", "y_out"))
        late_landed = sem("late_landed")
        sample_out, sample_in = sem("sample_out"), sem("sample_in")
        front_over = sem("front_over")

        def w_free(s):
            if s < S_UP:
                if s in ends:
                    return proj_ready, ends[s]
                base = {S_VA: 0, S_VB: 3}[S_VA if s < S_VB else S_VB]
                return kstep, base + (s - (S_VA if s < S_VB else S_VB)) + 1
            if s < S_WO:
                return up_ready, 4 * (s - S_UP + 1)
            if s < S_PQ:
                n = s - S_WO
                return (wo_ready, 5 * (n // 4 + 1)) if n % 4 == 3 else (kstep, 6 + 3 * (n // 4) + n % 4 + 1)
            return pq_ready, 2 * (s - S_PQ + 1)

        block = ctx.enter_context(nc.Block())

        @block.sync
        def _(sp):
            sp.dma_start(view("consts"), A["consts"]).then_inc(consts_landed, 16)
            sp.dma_start(vecs[:, 0:N_VEC], A["vecs"]).then_inc(consts_landed, 16)
            for k in range(4):
                sp.dma_start(xT[:, 2 * k:2 * k + 2], A["xT"][:, 2 * k:2 * k + 2]).then_inc(x_landed, 16)
            sp.dma_start(abw, A["w_ab"]).then_inc(wab_landed, 16)
            sp.dma_start(alw, A["w_alpha"]).then_inc(wab_landed, 16)
            sp.dma_start(bias_row, A["sb_bias"].partition_broadcast(P)).then_inc(wab_landed, 16)

            def stream(a, b):
                for s in range(a, b):
                    if s >= RING_W:
                        sp.wait_ge(*w_free(s - RING_W))
                    sp.dma_start(wring[:, s % RING_W], A["w_stream"][s]).then_inc(w_in_slot[s % RING_W], 16)

            stream(0, S_RB + RING_W)
            sp.wait_ge(qk_done, 8)
            sp.dma_start(A["new_kT"].rearrange("(m p) t -> p m t", p=P), qk[:, 4:8]).then_inc(out_done, 16)
            sp.wait_ge(proj_taken, ALPHA_ITEM + 4 + 5)
            sp.dma_start(A["new_v"][0:SEQ].rearrange("(t p) c -> p t c", p=P), vab[:, 0:NT, 0:512]).then_inc(out_done, 16)
            sp.dma_start(A["new_v"][SEQ:T], vab[0:NB, NT, 0:512]).then_inc(out_done, 16)
            stream(S_RB + RING_W, S_UP)
            sp.wait_ge(table_landed, 16)
            early_page = lambda n: sp.value_load(page_table[0:1, bass.ds(n, 1)], min_val=0, max_val=A["cache_v"].shape[0] - 1)
            with sp.Fori(0, V_EARLY * PAGES // RING_V) as i:
                pages = [early_page(i * RING_V)]
                for s in range(RING_V):
                    if s + 1 < RING_V:
                        pages.append(early_page(i * RING_V + (s + 1)))
                    sp.wait_ge(v_free, i * RING_V + (s + 1))
                    sp.dma_start(vring[:, s, :], A["cache_v"][bass.ds(pages[s], 1)].rearrange("a p n -> (a p) n")).then_inc(v_early[s], 16)
            sp.wait_ge(k_free, RING_K + NB * PAGES)
            sp.wait_ge(proj_ready, N_ITEMS)
            sp.dma_start(sstate, A["state"]).then_inc(state_landed, 16)
            stream(S_UP, S_UP + RING_W)
            sp.wait_ge(states_done, 2)
            sp.dma_start(A["gla_prompt"], states[:, NCH]).then_inc(out_done, 16)
            sp.wait_ge(ss_ready, 1)
            sp.dma_start(A["gla_sample"], sstate).then_inc(out_done, 16)
            sp.wait_ge(y_ready, 4)
            sp.wait_ge(out_done, 16 * 5)
            sp.wait_ge(v_done, NB)
            sp.dma_start(h1[:, 0:NT], A["x_rows"][0:SEQ].rearrange("(t p) c -> p t c", p=P)).then_inc(rows_landed, 16)
            sp.dma_start(h1[0:NB, NT], A["x_rows"][SEQ:T]).then_inc(rows_landed, 16)
            stream(S_UP + RING_W, S_WO)
            sp.wait_ge(mix_ready, 8)
            sp.dma_start(g2, A["norm2_g"].partition_broadcast(P)).then_inc(late_landed, 16)
            sp.dma_start(sk, A["sub_keysT"]).then_inc(late_landed, 16)
            stream(S_WO, S_PQ)
            stream(S_PQ, S_PQ + RING_W)
            sp.wait_ge(wo_ready, 10)
            sp.dma_start(wpg, A["w_ple_gate"]).then_inc(late_landed, 16)
            stream(S_PQ + RING_W, S_END)
            sp.wait_ge(xn2_ready, 5)
            sp.dma_start(scratch_x, xn2[0:NB, NT]).then_inc(sample_out, 16)
            sp.wait_ge(s_taken, 32)
            sp.wait_ge(topk_done, 1)
            sp.dma_start(pT, A["pT"]).then_inc(late_landed, 16)
            sp.dma_start(ple_w, A["w_ple"]).then_inc(late_landed, 16)
            sp.dma_start(g3, A["norm3_g"].partition_broadcast(P)).then_inc(late_landed, 16)
            sp.wait_ge(sel_ready, NT + 1)
            sp.dma_start(scratch_e, expert[0:NB, NT]).then_inc(sample_out, 16)
            sp.dma_start(scratch_g, gate[0:NB, NT]).then_inc(sample_out, 16)
            sp.wait_ge(sample_out, 48)
            for b in range(NB):
                w = P // NB
                sp.dma_start(sx[b * w:(b + 1) * w], scratch_x[b].partition_broadcast(w)).then_inc(sample_in, 16)
            sp.dma_start(sidx, scratch_e.rearrange("b (j r) -> (b j) r", r=8)).then_inc(sample_in, 16)
            sp.dma_start(sgate, scratch_g.rearrange("b (j r) -> (b j) r", r=8)).then_inc(sample_in, 16)
            for t in range(NT + 1):
                sp.wait_ge(y_out, t + 1)
                R = ROWS[t]
                sp.dma_start(A["y"][t * P:t * P + R], h1[0:R, t]).then_inc(out_done, 16)
            sp.wait_ge(out_done, 16 * 10)

        @block.gpsimd
        def _(pool):
            c = Steps(pool, pool_steps)
            pool.dma_start(page_table[0:1, :], A["page_table"]).then_inc(table_landed, 16)
            pool.wait_ge(table_landed, 16)

            def load_page(ring, cache, landed, page, s):
                pool.dma_start(ring[:, s, :], cache[bass.ds(page, 1)].rearrange("a p n -> (a p) n")).then_inc(landed[s], 16)

            page_number = lambda n: pool.value_load(page_table[0:1, bass.ds(n, 1)], min_val=0, max_val=A["cache_k"].shape[0] - 1)

            with pool.Fori(0, NB * PAGES // RING_K) as i:
                pages = [page_number(i * RING_K + s) for s in range(RING_K)]
                for s in range(RING_K):
                    pool.wait_ge(k_free, i * RING_K + (s + 1))
                    load_page(kring, A["cache_k"], k_landed, pages[s], s)
            with pool.Fori(V_EARLY * PAGES // RING_V, NB * PAGES // RING_V) as i:
                pages = [page_number(i * RING_V + s) for s in range(RING_V)]
                for s in range(RING_V):
                    pool.wait_ge(v_free, i * RING_V + (s + 1))
                    load_page(vring, A["cache_v"], v_landed, pages[s], s)
            for t in range(NT):
                pool.wait_ge(sel_ready, t + 1)
                with pool.Fori(0, SEL // RING_G) as i:
                    for g in range(4):
                        pool.wait_ge(g_used, i * 4 + (t * 64 + g + 1))
                        pair = slot_idx[:, 2 * g:2 * g + 2]
                        rows = expert[:, t, bass.ds(i * 8 + 2 * g, 2)]
                        pool.tensor_tensor(pair, rows, zero_u, ALU.add).then_inc(idx_copied, 1)
                        pool.wait_ge(idx_copied, i * 4 + (t * 64 + g + 1))
                        pool.tensor_tensor(idx_guard, pair, zero_u, ALU.add)
                        for s in (2 * g, 2 * g + 1):
                            pool.indirect_dma_start(gring[:, s, :], None, A["experts"],
                                                    bass.IndirectOffsetOnAxis(ap=slot_idx[:, s:s + 1], axis=0)).then_inc(g_landed[s], 16)
            pool.wait_ge(sample_in, 16 * (NB + 2))
            for r in range(8):
                pool.wait_ge(g_used, NT * 64 + r // 2 + 1)
                pool.indirect_dma_start(gring[:, r, :], None, A["experts"],
                                        bass.IndirectOffsetOnAxis(ap=sidx[:, r:r + 1], axis=0)).then_inc(g_landed[r], 16)

        @block.scalar
        def _(act):
            c = Steps(act, act_steps)
            A_ = nc.scalar.activation
            act.wait_ge(consts_landed, 32)
            for k in range(KD):
                act.wait_ge(x_landed, 64)
                c.also(A_, qk[:, k], xT[:, k], ACT.Square, signal=sq_ready)
            std_row = view("zs")[:, 0:T]
            for half, (a, b) in enumerate(HALVES):
                act.wait_ge(mean1, half + 1)
                c.also(A_, std_row[:, a:b], bank[6 + half][:, 0:HALF], ACT.Sqrt, bias=cst("eps"), signal=std1)

            def take(i):
                kind, j, half = items[i]
                act.wait_ge(proj_ready, i + 1)
                a, b = HALVES[half]
                src = bank[i % 6][:, 0:HALF]
                if kind == "qk":
                    c.also(A_, qk[:, j, a:b], src, ACT.Copy, signal=proj_taken)
                elif kind == "ab":
                    c.also(A_, abT[0:RANK, a:b], src[0:RANK], ACT.Copy, signal=proj_taken)
                elif kind == "qkb":
                    c.also(A_, qkb[:, j, a:b], src, ACT.Copy, scale=(GDK ** -0.5 if j < 2 else 1.0), signal=proj_taken)
                elif kind == "alpha":
                    c.also(A_, la[:, j, a:b], src, ACT.Identity, bias=vecs[:, V_BA + j:V_BA + j + 1], signal=proj_taken)
                elif kind in ("va", "vb"):
                    o = 0 if kind == "va" else 512
                    R = ROWS[j]
                    c.also(A_, vab[0:R, j, o:o + 512], bank[i % 6][0:R, :], ACT.Copy, signal=proj_taken)
                elif kind == "rb":
                    c.also(A_, srb[:, j, a:b], src, ACT.Silu, signal=proj_taken)
                else:
                    c.also(A_, gates[:, j, a:b], src, ACT.Sigmoid, bias=vecs[:, V_BG + j:V_BG + j + 1], signal=proj_taken)

            def squares(j):
                if j >= 2:
                    act.wait_ge(qkmean, 2 * (j - 1))
                for half, (a, b) in enumerate(HALVES):
                    if half == 0:
                        c.settle()
                    c.also(A_, qk_sq[:, j % 2, a:b], qk[:, j, a:b], ACT.Square, signal=qksq)

            def roots(j):
                if j in (2, 3, 7):
                    act.wait_ge(qk_done, {2: 1, 3: 2, 7: 3}[j])
                for half, (a, b) in enumerate(HALVES):
                    act.wait_ge(qkmean, 2 * j + half + 1)
                    c.also(A_, qk_std[:, STD_BUF[j], a:b], bank[6 + half][:, 0:HALF], ACT.Sqrt, bias=cst("eps"), signal=qkstd)

            act.wait_ge(xn_ready, KD)
            for j in range(8):
                take(2 * j)
                take(2 * j + 1)
                squares(j)
                if j >= 1:
                    roots(j - 1)
                if j == 5:
                    for b in range(NB):
                        act.wait_ge(qb_ready, b + 1)
                        c.also(A_, qbc[:, b], bank[6 + b % 2][:, :], ACT.Copy, signal=qb_taken)
            take(AB_ITEM)
            take(AB_ITEM + 1)
            roots(7)
            for i in range(AB_ITEM + 2, N_ITEMS):
                take(i)

            def take_v(b):
                act.wait_ge(v_done, b + 1)
                c.also(A_, v_cols[:, :, b], bank[V_BANK[b]][:, 0:4], ACT.Copy, signal=v_taken)

            for half in range(2):
                act.wait_ge(zb_ready, half + 1)
                c.then(A_, tmp[:, 0:1024], tmp[:, 0:1024], ACT.Exp, scale=-1.0)
                c.then(A_, tmp[:, 0:1024], tmp[:, 0:1024], ACT.Ln, bias=1.0, signal=dec_l)
                for q in (2 * half, 2 * half + 1):
                    act.wait_ge(dec_arg, q + 1)
                    c.also(A_, zs[:, 512 * q:512 * q + 512], zs[:, 512 * q:512 * q + 512], ACT.Exp, signal=dec_w)

            act.wait_ge(la_in, 1)
            c.then(A_, tmp[:, 4128:4128 + 2 * T], tmp[:, 4128:4128 + 2 * T], ACT.Exp, scale=-1.0)
            c.then(A_, tmp[:, 4128:4128 + 2 * T], tmp[:, 4128:4128 + 2 * T], ACT.Ln, bias=1.0, signal=la_ready)
            act.wait_ge(gla_d, 1)
            flat = lambda x: x.rearrange("p m t -> p (m t)")
            c.also(A_, flat(qe), flat(cum), ACT.Exp, scale=1.0 / TAU, signal=gla_e)
            c.also(A_, flat(qt), tmp[:, 0:1024], ACT.Exp, scale=1.0 / TAU, signal=gla_e)
            c.also(A_, flat(kt), tmp[:, 0:1024], ACT.Exp, scale=-1.0 / TAU, signal=gla_e)
            c.also(A_, flat(kd), tmp[:, 1024:2048], ACT.Exp, scale=1.0 / TAU, signal=gla_e)
            c.also(A_, sample_decay, la[:, :, SEQ:T], ACT.Exp, scale=1.0 / TAU, signal=gla_e)
            for b in range(3):
                take_v(b)
            for m in range(2):
                act.wait_ge(kd_tr, m + 1)
                c.also(A_, kdr[:, :, m, :], bank[m].rearrange("p (t c) -> p t c", t=NT), ACT.Copy, signal=kd_rows)
            for u in range(2):
                for par in range(2):
                    act.wait_ge(o_ready, 2 * u + par + 1)
                    src = bank[2 + par].rearrange("p (tt m c) -> p m tt c", tt=2, m=2)
                    dst = ob[:, :, 256 * u:256 * u + 256].rearrange("p (m par) (tt c) -> p par m tt c", par=2, tt=2)[:, par]
                    c.also(A_, dst, src, ACT.Copy, signal=o_taken)
            take_v(3)
            for par in range(2):
                act.wait_ge(so_ready, par + 1)
                src = bank[7 if par == 0 else 1][:, 0:16].rearrange("p (m b) -> p m b", m=2)
                dst = ob[:, :, SEQ:T].rearrange("p (m par) b -> p par m b", par=2)[:, par]
                c.also(A_, dst, src, ACT.Copy, signal=o_taken)
            act.wait_ge(ss_ready, 1)
            for h in range(GH):
                c.settle()
                if h >= 2:
                    act.wait_ge(ob_mean, 2 * (h - 1))
                c.also(A_, ob_tmp[:, h % 2], ob[:, h], ACT.Square, signal=ob_sq)
                if h >= 1:
                    act.wait_ge(yb_ready, h)
                for half, (a, b) in enumerate(HALVES):
                    act.wait_ge(ob_mean, 2 * h + half + 1)
                    c.also(A_, ob_tmp[:, 2, a:b], bank[4 + half][:, 0:HALF], ACT.Sqrt, bias=cst("eps"), signal=ob_std)

            act.wait_ge(yb_ready, GH)
            for h in range(H):
                if h in FOLD_AT:
                    take_v(FOLD_AT[h])
                bias_h = bias_row[:, h:h + 1]
                if h >= 1:
                    act.wait_ge(att_sp, h)
                at = 0
                for n in range(NT):
                    w = SEQ - P * n
                    act.wait_ge(z_ready, NT * h + n + 1)
                    c.also(A_, tmp[:, at:at + w], bank[n][:, 0:w], ACT.Identity, bias=bias_h, signal=att_l)
                    at += w
                act.wait_ge(att_r, h + 1)
                c.then(A_, tmp[:, 1280:2560], tmp[:, 1280:2560], ACT.Exp, scale=-1.0)
                c.then(A_, tmp[:, 1280:2560], tmp[:, 1280:2560], ACT.Ln, bias=1.0, signal=att_l)
                at = 0
                for n in range(NT):
                    w = SEQ - P * n
                    act.wait_ge(acc_ready, NT * h + n + 1)
                    c.also(A_, tmp[:, 3840 + at:3840 + at + w], bank[n][:, 0:w], ACT.Exp, bias=bias_h, signal=att_w)
                    at += w
                if h % 2 == 1:
                    act.wait_ge(y_ready, h // 2 + 1)
                    c.also(A_, yaT[:, h // 2, 0:SEQ], bank[4 + h // 2 % 2][:, :], ACT.Copy, signal=y_taken)
            take_v(NB - 1)
            c.settle()
            c.also(A_, yaT[:, :, SEQ:T], v_cols, ACT.Copy, signal=y_taken)

            act.wait_ge(late_landed, 32)
            for t in range(5):
                R = ROWS[t]
                act.wait_ge(wo_taken, 5 + t + 1)
                c.settle()
                c.also(A_, view("onehot")[0:R, 0:D], h1[0:R, t], ACT.Square, accum_out=ssq[0:R, t:t + 1])
                c.then(A_, ssq[0:R, 5 + t:6 + t], ssq[0:R, t:t + 1], ACT.Sqrt, bias=cst("eps")[0:R], scale=1.0 / D, signal=h_std)
            for t in range(5):
                for k2 in range(2 if t < NT else 1):
                    n = 2 * t + k2
                    act.wait_ge(x2t_ready, n + 1)
                    if t < NT:
                        c.also(A_, xn2T[:, 4 * k2:4 * k2 + 4, t * P:t * P + P],
                               bank[2 + n % 6].rearrange("p (k c) -> p k c", k=4), ACT.Copy, signal=x2t_taken)
                    else:
                        c.also(A_, xn2T[:, :, SEQ:T], bank[2 + n % 6][:, 0:64].rearrange("p (k c) -> p k c", k=8),
                               ACT.Copy, signal=x2t_taken)

            def take_scores(j):
                act.wait_ge(s_ready, 2 * j + 1)
                c.also(A_, s_all[:, 0:NT, j, :], bank[4 + j % 2].rearrange("p (t n) -> p t n", t=NT), ACT.Copy, signal=s_taken)
                act.wait_ge(s_ready, 2 * j + 2)
                c.also(A_, s_all[0:NB, NT, j, :], bank[6 + j % 2][0:NB, 0:P], ACT.Copy, signal=s_taken)

            for j in range(16):
                if j >= 2:
                    act.wait_ge(s_ready, 2 * (j - 1))
                for half, (a, b) in enumerate(HALVES):
                    act.wait_ge(pq_ready, 2 * j + half + 1)
                    c.also(A_, qp[:, j % 2, a:b], bank[(2 * j + half) % 4][:, 0:HALF], ACT.Copy, signal=pq_taken)
                if j >= 1:
                    take_scores(j - 1)
            take_scores(15)

            def softmax_exp(t):
                act.wait_ge(soft_in, t + 1)
                c.also(A_, top[0:ROWS[t], 1], top[0:ROWS[t], 1], ACT.Exp, signal=soft_e)

            def h2_root(t):
                R = ROWS[t]
                act.wait_ge(h2_ready, t + 1)
                c.also(A_, fin[0:R], h1[0:R, t], ACT.Square, accum_out=ssq[0:R, t:t + 1])
                c.then(A_, ssq[0:R, 5 + t:6 + t], ssq[0:R, t:t + 1], ACT.Sqrt, bias=cst("eps")[0:R], scale=1.0 / D, signal=h3_std)

            def x3_columns(t):
                R = ROWS[t]
                for c2 in range(2):
                    act.wait_ge(x3t_ready, 2 * t + c2 + 1)
                    c.also(A_, xn3T[:, 4 * c2:4 * c2 + 4, 0:R],
                           bank[4 + c2][:, 0:4 * R].rearrange("p (k c) -> p k c", k=4), ACT.Copy, signal=x3t_taken)

            def ple_sigmoid(t):
                R = ROWS[t]
                c.settle()
                for c2 in range(2):
                    act.wait_ge(ple_ready, 4 * t + c2 + 1)
                    c.also(A_, fin[0:R, 512 * c2:512 * c2 + 512], bank[6 + c2][0:R, :], ACT.Sigmoid, signal=ple_sig)

            softmax_exp(0)
            for t in range(NT):
                for k in range(SEGMENTS):
                    if t >= 1 and k == 1:
                        h2_root(t - 1)
                    elif t >= 1 and k == 3:
                        x3_columns(t - 1)
                    elif k == 5:
                        if t >= 1:
                            ple_sigmoid(t - 1)
                        softmax_exp(t + 1)
                    with act.Fori(k * SEG, (k + 1) * SEG) as i:
                        for g in range(4):
                            pair = slice(2 * g, 2 * g + 2)
                            act.wait_ge(dots, i * 4 + (t * 64 + g + 1))
                            A_(act_g[:, pair], dot[:, pair], ACT.Gelu).then_inc(gel, 1)
                            act.wait_ge(gated, i * 4 + (t * 64 + g + 1))
                            act.wait_ge(g_used, i * 4 + (t * 64 + g + 1))
                            A_(diag[:, 2 * g], ident, ACT.Copy, scale=coef[:, 2 * g:2 * g + 1])
                            A_(diag[:, 2 * g + 1], ident, ACT.Copy, scale=coef[:, 2 * g + 1:2 * g + 2]).then_inc(diag_ready, 1)
            h2_root(NT - 1)
            act.wait_ge(dots, NT * 64 + 1)
            c.also(A_, act_g, dot, ACT.Gelu, signal=gel)
            act.wait_ge(gated, NT * 64 + 1)
            act.wait_ge(g_used, NT * 64 + 4)
            for r in range(8):
                c.also(A_, diag[:, r, 0:NB], cst("sample_of"), ACT.Copy, scale=coef[:, r:r + 1], signal=diag_ready if r == 7 else None)
            x3_columns(NT - 1)
            ple_sigmoid(NT - 1)
            h2_root(NT)
            x3_columns(NT)
            ple_sigmoid(NT)
        @block.vector
        def _(dve):
            c = Steps(dve, dve_steps)
            V = nc.vector

            def absolute(out, x):
                return V.scalar_tensor_tensor(out=out, in0=x, scalar=-1.0, in1=x, op0=ALU.mult, op1=ALU.max)

            dve.wait_ge(consts_landed, 32)
            rstd = view("zs")[:, T:2 * T]
            std_row = view("zs")[:, 0:T]
            dve.wait_ge(std1, 2)
            c.also(V.reciprocal, rstd, std_row)
            c.settle()
            for k in range(KD):
                c.also(V.scalar_tensor_tensor, out=xn[:, k], in0=xT[:, k], scalar=vecs[:, V_G1 + k:V_G1 + k + 1], in1=rstd,
                       op0=ALU.mult, op1=ALU.mult, signal=xn_ready)
            c.also(V.tensor_scalar, vecs[:, V_QG:V_QG + 1], vecs[:, V_QG:V_QG + 1], HD ** -0.5, None, ALU.mult)

            def head_norm(j):
                gain = V_QG if j < 4 else V_KG
                dve.wait_ge(qkstd, 2 * (j + 1))
                std = qk_std[:, STD_BUF[j]]
                c.then(V.reciprocal, std, std)
                c.then(V.scalar_tensor_tensor, out=qk[:, j], in0=qk[:, j], scalar=vecs[:, gain:gain + 1], in1=std,
                       op0=ALU.mult, op1=ALU.mult, signal=qk_done)

            for j in range(4):
                head_norm(j)
            dve.wait_ge(qb_taken, NB)
            z4 = zs.rearrange("p (b h g) -> p b g h", b=NB, h=H)
            dve.sem_inc(k_free, RING_K)

            def sum_heads(b, g, s):
                V.tensor_reduce(z4[:, bass.ds(b, 1), bass.ds(g, 1), :].rearrange("p a c h -> p (a c h)"),
                                prod[:, s % PRODS].rearrange("p (h d) -> p h d", h=H), AX.X, ALU.add).then_inc(k_free, 1)

            def k_pages(samples, rounds):
                begin = samples[0] == 0 and rounds[0] == 0
                with dve.Fori(*samples) as b:
                    with dve.Fori(*rounds) as g:
                        for s in range(RING_K):
                            n = b * PAGES + g * RING_K
                            dve.wait_ge(k_landed[s], b * (16 * PAGES // RING_K) + g * 16 + 16)
                            dve.wait_ge(k_free, n + (RING_K if begin and s == 0 else RING_K + s + 1 - PRODS))
                            if s:
                                dve.wait_ge(k_mul, n + s)
                            V.tensor_tensor(prod[:, s % PRODS], kring[:, s], qbc[:, bass.ds(b, 1), :].rearrange("p a n -> p (a n)"),
                                            ALU.mult).then_inc(k_mul, 1)
                            if s:
                                sum_heads(b, g * -RING_K + (PAGES - s), s - 1)
                        dve.wait_ge(k_mul, b * PAGES + g * RING_K + RING_K)
                        sum_heads(b, g * -RING_K + (PAGES - RING_K), RING_K - 1)

            def scores_bias(half):
                cols = slice(1024 * half, 1024 * half + 1024)
                dve.wait_ge(k_free, RING_K + (half + 1) * 4 * PAGES)
                if half == 0:
                    dve.wait_ge(proj_ready, N_ITEMS)
                else:
                    dve.wait_ge(dec_z, 2)
                zb3 = zs[:, cols].rearrange("p (b h g) -> p b h g", b=NB // 2, h=H)
                brow = bias_row.rearrange("p (b h g) -> p b h g", b=1, g=1).to_broadcast([P, NB // 2, H, PAGES])
                c.also(V.tensor_tensor, zb3, zb3, brow, ALU.add)
                c.then(absolute, tmp[:, 0:1024], zs[:, cols], signal=zb_ready)

            def scores_softplus(half):
                dve.wait_ge(dec_l, half + 1)
                c.also(V.scalar_tensor_tensor, out=tmp[:, 1024:2048], in0=zs[:, 1024 * half:1024 * half + 1024], scalar=0.0,
                       in1=tmp[:, 0:1024], op0=ALU.max, op1=ALU.add)
                c.settle()
                for q in range(2):
                    o = 512 * q
                    c.also(V.tensor_tensor_scan, tmp[:, 2048 + o:2560 + o], cst("page_reset"), tmp[:, 1024 + o:1536 + o], 0.0,
                           ALU.mult, ALU.add, signal=dec_sp)

            def scores_argument(half):
                for q in (2 * half, 2 * half + 1):
                    dve.wait_ge(dec_z, q + 1)
                    c.also(V.tensor_tensor, zs[:, 512 * q:512 * q + 512], zs[:, 512 * q:512 * q + 512], bank[q][:, :], ALU.add,
                           signal=dec_arg)

            k_pages((0, 1), (0, 4))
            for j in range(4, 8):
                head_norm(j)
            c.settle()
            dve.sem_inc(v_free, RING_V)
            k_pages((1, 6), (0, 4))
            scores_bias(0)
            k_pages((6, 7), (0, 1))
            scores_softplus(0)
            k_pages((6, 7), (1, 2))
            scores_argument(0)
            k_pages((6, 7), (2, 4))
            k_pages((7, 8), (0, 4))
            for step in (scores_bias, scores_softplus, scores_argument):
                step(1)
            dve.wait_ge(proj_taken, N_ITEMS)


            def own_heads(b):
                dve.wait_ge(v_free, RING_V + (b + 1) * PAGES)
                if b >= 2:
                    dve.wait_ge(v_done, b - 1)
                own = ident[0:H, 0:H].rearrange("p (h o) -> p h o", o=1).to_broadcast([H, H, HD])
                by_head = lambda x: x.rearrange("p (h d) -> p h d", d=HD)
                c.also(V.tensor_tensor, by_head(v_own[b % 2]), by_head(bank[V_BANK[b]][0:H, :]), own, ALU.mult, signal=v_masked)

            laf = view("la")
            g_tmp = tmp[:, 4128:4128 + 2 * T]
            c.then(absolute, g_tmp, laf, signal=la_in)
            dve.wait_ge(la_ready, 1)
            c.also(V.scalar_tensor_tensor, out=laf, in0=laf, scalar=0.0, in1=g_tmp, op0=ALU.min, op1=ALU.subtract)
            c.settle()
            for m in range(2):
                c.also(V.tensor_tensor_scan, cum[:, m], cst("chunk_reset"), la[:, m, 0:SEQ], 0.0, ALU.mult, ALU.add)
            c.settle()
            ch = view("cum").rearrange("p (c i) -> p c i", i=CHUNK)
            t3 = lambda o: tmp[:, o:o + 1024].rearrange("p (c i) -> p c i", i=CHUNK)
            c.also(V.tensor_tensor, t3(0), ch, ch[:, :, CHUNK // 2 - 1:CHUNK // 2].to_broadcast([P, 2 * NCH, CHUNK]), ALU.subtract)
            c.also(V.tensor_tensor, t3(1024), ch[:, :, CHUNK - 1:CHUNK].to_broadcast([P, 2 * NCH, CHUNK]), ch, ALU.subtract, signal=gla_d)
            dve.wait_ge(gla_e, 5)
            c.also(V.tensor_copy, chunk_decay, view("qe").rearrange("p (c i) -> p c i", i=CHUNK)[:, :, CHUNK - 1])
            c.also(V.tensor_tensor, kd, kd, qkb[:, 2:4, 0:SEQ], ALU.mult, signal=gla_in)
            c.also(V.tensor_tensor, qt, qt, qkb[:, 0:2, 0:SEQ], ALU.mult)
            c.also(V.tensor_tensor, kt, kt, qkb[:, 2:4, 0:SEQ], ALU.mult, signal=gla_in)
            c.then(V.tensor_tensor, qe, qe, qkb[:, 0:2, 0:SEQ], ALU.mult)
            c.also(V.memset, states[:, 0], 0.0, signal=gla_in)
            for b in range(3):
                own_heads(b)
            mask4 = cst("gla_mask").rearrange("p (a c) -> p a c", a=1).to_broadcast([P, 4, P])
            for u in range(2):
                for par in range(2):
                    dve.wait_ge(sc_ready, 2 * u + par + 1)
                    c.also(V.tensor_tensor, sc_v[:, par], bank[2 + par].rearrange("p (a c) -> p a c", a=4), mask4, ALU.mult, signal=sc_done)
                dve.wait_ge(u_ready, u + 1)
                for ch4 in range(4):
                    cc = 4 * u + ch4
                    c.settle()
                    for m in range(2):
                        ub = (4 if u == 0 else 0) + cc % 2
                        ucol = (ch4 // 2 * 2 + m) * P
                        c.also(V.scalar_tensor_tensor, out=states[:, cc + 1, m], in0=states[:, cc, m],
                               scalar=chunk_decay[:, m * NCH + cc:m * NCH + cc + 1], in1=bank[ub][:, ucol:ucol + P],
                               op0=ALU.mult, op1=ALU.add, signal=states_done if (cc in (3, 7) and m == 1) else None)
            own_heads(3)
            dve.wait_ge(state_landed, 16)
            for b in range(NB):
                dve.wait_ge(vb_ready, b + 1)
                for par in range(2):
                    rows = slice(64 * par, 64 * par + 64)
                    v_b = bank[7].rearrange("p (m q e) -> p q m e", m=2, q=2)[rows, par]
                    k_b = qkb[rows, 2:4, SEQ + b:SEQ + b + 1].to_broadcast([64, 2, GDV])
                    c.also(V.tensor_tensor, kv[rows, b], v_b, k_b, ALU.mult, signal=vb_taken if par else None)
            dec = sample_decay.rearrange("p m (b o) -> p b m o", o=1).to_broadcast([P, NB, 2, GDV])
            c.then(V.tensor_tensor, sstate, sstate, dec, ALU.mult)
            c.then(V.tensor_tensor, sstate, sstate, kv, ALU.add, signal=ss_ready)
            for h in range(GH):
                dve.wait_ge(ob_std, 2 * (h + 1))
                c.then(V.reciprocal, ob_tmp[:, 2], ob_tmp[:, 2])
                c.also(V.scalar_tensor_tensor, out=srb[:, h], in0=ob[:, h], scalar=vecs[:, V_OG:V_OG + 1], in1=srb[:, h],
                       op0=ALU.mult, op1=ALU.mult)
                c.then(V.tensor_tensor, srb[:, h], srb[:, h], ob_tmp[:, 2], ALU.mult, signal=yb_ready)

            own_heads(4)
            for h in range(H):
                dve.wait_ge(att_l, 5 * h + 4)
                if h >= 1:
                    dve.wait_ge(acc_ready, NT * h)
                c.also(absolute, tmp[:, 1280:2560], tmp[:, 0:1280], signal=att_r)
                dve.wait_ge(att_l, 5 * h + 5)
                c.also(V.scalar_tensor_tensor, out=tmp[:, 2560:3840], in0=tmp[:, 0:1280], scalar=0.0, in1=tmp[:, 1280:2560],
                       op0=ALU.max, op1=ALU.add)
                at = 2560
                c.settle()
                for n in range(NT):
                    c.also(V.tensor_tensor, tmp[:, at:at + P], tmp[:, at:at + P], cst("keep_mask"), ALU.mult,
                           signal=att_sp if n == NT - 1 else None)
                    at += SEQ - P * n
                if h + 1 in FOLD_AT:
                    own_heads(FOLD_AT[h + 1])
            own_heads(NB - 1)

            for m in range(8):
                for q in range(4):
                    i = 4 * m + q
                    a, b = HALVES[q % 2]
                    dve.wait_ge(up_ready, i + 1)
                    gm = gates[:, (m if q < 2 else 8 + m), a:b]
                    c.also(V.tensor_tensor, gm, gm, bank[i % 8][:, 0:HALF], ALU.mult, signal=up_taken)
                c.then(V.tensor_tensor, gates[:, m], gates[:, m], gates[:, 8 + m], ALU.add, signal=mix_ready)
            dve.wait_ge(rows_landed, 32)
            for i in range(10):
                t, half = i % 5, i // 5
                R = ROWS[t]
                dve.wait_ge(wo_ready, i + 1)
                hh = h1[0:R, t, 512 * half:512 * half + 512]
                c.also(V.tensor_tensor, hh, hh, bank[i % 8][0:R, :], ALU.add, signal=wo_taken)
            dve.wait_ge(late_landed, 32)
            for t in range(5):
                R = ROWS[t]
                dve.wait_ge(h_std, t + 1)
                c.also(V.reciprocal, rstd2[0:R, t:t + 1], ssq[0:R, 5 + t:6 + t])
                c.then(V.scalar_tensor_tensor, out=xn2[0:R, t], in0=h1[0:R, t], scalar=rstd2[0:R, t:t + 1], in1=g2[0:R],
                       op0=ALU.mult, op1=ALU.mult, signal=xn2_ready)

            def two_best(values, best, where, done=None):
                for part in range(2):
                    pick = slice(8 * part, 8 * part + 8)
                    c.settle()
                    for x, v, w in zip(values, best, where):
                        c.also(V.max, v[:, pick], x)
                    c.settle()
                    for n, (x, v, w) in enumerate(zip(values, best, where)):
                        c.also(V.max_index, w[:, pick], v[:, pick], x, signal=done if part and n == len(values) - 1 else None)
                    if part == 0:
                        c.settle()
                        for x, v, w in zip(values, best, where):
                            c.also(V.match_replace, x, v[:, pick], x, LOWEST)

            for j in range(16):
                dve.wait_ge(s_taken, 2 * (j + 1))
                pick = [(t, ROWS[t]) for t in range(5)]
                two_best([s_all[0:R, t, j] for t, R in pick], [v16[0:R, t, j] for t, R in pick], [i16[0:R, t, j] for t, R in pick],
                         done=topk_done if j == 15 else None)

            def select_lists(t):
                R = ROWS[t]
                s4 = v16[0:R, t].rearrange("p (h c) k -> p h c k", c=2)
                c4 = cand[0:R].rearrange("p h (i j) -> p h i j", i=TOPK)
                s1 = s4[:, :, 0].rearrange("p h (k o) -> p h k o", o=1).to_broadcast([R, PH, TOPK, TOPK])
                s2 = s4[:, :, 1].rearrange("p h (o k) -> p h o k", o=1).to_broadcast([R, PH, TOPK, TOPK])
                c.then(V.tensor_tensor, c4, s1, s2, ALU.add)

            def select_best(t):
                R = ROWS[t]
                two_best([cand[0:R, h] for h in range(PH)], [top[0:R, 0, h] for h in range(PH)], [top_u[0:R, 2, h] for h in range(PH)])
                c.settle()
                best = top[0:R, 0, :, 0:1].to_broadcast([R, PH, TOPK])
                c.also(V.tensor_tensor, top[0:R, 1], top[0:R, 0], best, ALU.subtract, signal=soft_in)
                c.also(V.tensor_scalar, top_u[0:R, 3], top_u[0:R, 2], 4, None, ALU.logical_shift_right)
                c.also(V.tensor_scalar, top_u[0:R, 4], top_u[0:R, 2], 15, None, ALU.bitwise_and)
                c.also(V.tensor_copy, i16f[0:R], i16[0:R, t])
                c.settle()
                for part in range(2):
                    c.also(V.tensor_copy, top[0:R, 5 + part], top_u[0:R, 3 + part])

            def select_keys(t, part):
                R = ROWS[t]
                iota = cst("iota16")[0:R].rearrange("p (a b j) -> p a b j", a=1, b=1).to_broadcast([R, PH, TOPK, TOPK])
                c.settle()
                place = top[0:R, 5 + part].rearrange("p h (k o) -> p h k o", o=1).to_broadcast([R, PH, TOPK, TOPK])
                keys = i16f[0:R].rearrange("p (h c) (o k) -> p h c o k", c=2, o=1)[:, :, part].to_broadcast([R, PH, TOPK, TOPK])
                c.also(V.tensor_tensor, onehot[0:R], place, iota, ALU.is_equal)
                c.then(V.tensor_tensor, onehot[0:R], onehot[0:R], keys, ALU.mult)
                c.then(V.tensor_reduce, top[0:R, 7 + part], onehot[0:R], AX.X, ALU.add)

            def select_end(t):
                R = ROWS[t]
                c.settle()
                flat = lambda x: x.rearrange("p h k -> p (h k)")
                c.also(V.scalar_tensor_tensor, out=expert[0:R, t], in0=flat(top[0:R, 7]), scalar=float(NKEYS), in1=flat(top[0:R, 8]),
                       op0=ALU.mult, op1=ALU.add)
                dve.wait_ge(soft_e, t + 1)
                c.also(V.tensor_reduce, den[0:R], top[0:R, 1], AX.X, ALU.add)
                c.then(V.reciprocal, den[0:R], den[0:R])
                c.then(V.tensor_tensor, gate[0:R, t].rearrange("p (h k) -> p h k", h=PH), top[0:R, 1],
                       den[0:R].rearrange("p (h o) -> p h o", o=1).to_broadcast([R, PH, TOPK]), ALU.mult, signal=sel_ready)

            def residual(t):
                R = ROWS[t]
                dve.wait_ge(y_sum, t + 1)
                c.settle()
                for c2 in range(2):
                    hh = h1[0:R, t, 512 * c2:512 * c2 + 512]
                    c.also(V.tensor_tensor, hh, hh, bank[Y_BANKS[t % 2][c2]][0:R, :], ALU.add, signal=h2_ready if c2 else None)

            def third_norm(t):
                R = ROWS[t]
                dve.wait_ge(h3_std, t + 1)
                c.also(V.reciprocal, rstd2[0:R, 5:6], ssq[0:R, 5 + t:6 + t])
                c.then(V.scalar_tensor_tensor, out=xn2[0:R, t], in0=h1[0:R, t], scalar=rstd2[0:R, 5:6], in1=g3[0:R],
                       op0=ALU.mult, op1=ALU.mult, signal=xn3_ready)

            def embed(t):
                R = ROWS[t]
                dve.wait_ge(ple_sig, 2 * (t + 1))
                for c2 in range(2):
                    dve.wait_ge(ple_ready, 4 * t + 3 + c2)
                    ff = fin[0:R, 512 * c2:512 * c2 + 512]
                    c.also(V.tensor_tensor, ff, ff, bank[4 + c2][0:R, :], ALU.mult)
                c.then(V.tensor_tensor, h1[0:R, t], h1[0:R, t], fin[0:R], ALU.add, signal=y_out)

            select_lists(0)
            select_best(0)
            select_keys(0, 0)
            select_keys(0, 1)
            dve.sem_inc(g_used, 4)
            select_end(0)
            dve.wait_ge(late_landed, 96)
            for t in range(NT):
                for k in range(SEGMENTS):
                    if k == 1 and t >= 1:
                        residual(t - 1)
                    elif k == 2:
                        if t >= 1:
                            third_norm(t - 1)
                        select_lists(t + 1)
                    elif k == 3:
                        select_best(t + 1)
                    elif k == 5:
                        if t >= 1:
                            embed(t - 1)
                        select_keys(t + 1, 0)
                    elif k == 6:
                        select_keys(t + 1, 1)
                        select_end(t + 1)
                    c.settle()
                    with dve.Fori(k * SEG, (k + 1) * SEG) as i:
                        for g in range(4):
                            for s in (2 * g, 2 * g + 1):
                                dve.wait_ge(g_landed[s], i * 16 + (t * 256 + 16))
                                last = V.tensor_tensor_reduce(gring[:, s, 0:D], gring[:, s, 0:D], xn2[:, t], 1.0, 0.0,
                                                              ALU.mult, ALU.add, dot[:, s:s + 1])
                            last.then_inc(dots, 1)
                            dve.wait_ge(gel, i * 4 + (t * 64 + g + 1))
                            V.tensor_tensor(coef[:, 2 * g:2 * g + 2], act_g[:, 2 * g:2 * g + 2], gate[:, t, bass.ds(i * 8 + 2 * g, 2)],
                                            ALU.mult).then_inc(gated, 1)
            residual(NT - 1)
            third_norm(NT - 1)
            dve.wait_ge(sample_in, 16 * (NB + 2))
            for r in range(8):
                dve.wait_ge(g_landed[r], 16 * (NT * SEL // RING_G + 1))
                c.also(V.tensor_tensor_reduce, gring[:, r, 0:D], gring[:, r, 0:D], sx, 1.0, 0.0, ALU.mult, ALU.add, dot[:, r:r + 1],
                       signal=dots if r == 7 else None)
            dve.wait_ge(gel, NT * 64 + 1)
            c.also(V.tensor_tensor, coef, act_g, sgate, ALU.mult, signal=gated)
            embed(NT - 1)
            residual(NT)
            third_norm(NT)
            embed(NT)

        @block.tensor
        def _(pe):
            mm, tr = nc.tensor.matmul, nc.tensor.transpose
            pe.wait_ge(consts_landed, 32)
            mean = cst("mean_model")
            for half, (a, b) in enumerate(HALVES):
                for k in range(KD):
                    pe.wait_ge(sq_ready, k + 1)
                    last = mm(bank[6 + half][:, 0:HALF], mean, qk[:, k, a:b], start=(k == 0), stop=(k == KD - 1))
                last.then_inc(mean1, 1)

            def weights(s):
                pe.wait_ge(w_in_slot[s % RING_W], 16 * (s // RING_W + 1))
                return wring[:, s % RING_W]

            def item(i):
                if i >= 6:
                    pe.wait_ge(proj_taken, i - 5)
                return bank[i % 6]

            made_items = [0]

            def project(s):
                w = weights(s).rearrange("p (k c) -> p k c", k=KD)
                for a, b in HALVES:
                    out = item(made_items[0])[:, 0:HALF]
                    made_items[0] += 1
                    for k in range(KD):
                        last = mm(out, w[:, k], xn[:, k, a:b], start=(k == 0), stop=(k == KD - 1))
                    last.then_inc(proj_ready, 1)

            def head_means(j):
                pe.wait_ge(qksq, 2 * (j + 1))
                if j >= 1:
                    pe.wait_ge(qkstd, 2 * j)
                for half, (a, b) in enumerate(HALVES):
                    mm(bank[6 + half][:, 0:HALF], cst("mean_head"), qk_sq[:, j % 2, a:b], start=True, stop=True).then_inc(qkmean, 1)

            pe.wait_ge(xn_ready, KD)
            for j in range(8):
                project(S_QA + j)
                if j >= 1:
                    head_means(j - 1)
                if j == 5:
                    pe.wait_ge(qk_done, 4)
                    pe.wait_ge(qkstd, 10)
                    for b in range(NB):
                        if b >= 2:
                            pe.wait_ge(qb_taken, b - 1)
                        for m in range(4):
                            last = mm(bank[6 + b % 2][:, m * P:m * P + P], qk[:, m, SEQ + b:SEQ + b + 1].to_broadcast([P, P]), ident,
                                      start=True, stop=True)
                        last.then_inc(qb_ready, 1)
                    pe.wait_ge(qb_taken, NB)
            pe.wait_ge(wab_landed, 48)
            for a, b in HALVES:
                out = item(made_items[0])[0:RANK, 0:HALF]
                made_items[0] += 1
                for k in range(KD):
                    last = mm(out, abw[:, k], xn[:, k, a:b], start=(k == 0), stop=(k == KD - 1))
                last.then_inc(proj_ready, 1)
            head_means(7)
            for j in range(4):
                project(S_QB + j)
            pe.wait_ge(proj_taken, AB_ITEM + 2)
            for m in range(2):
                for a, b in HALVES:
                    mm(item(made_items[0])[:, 0:HALF], alw[:, m * P:m * P + P], abT[0:RANK, a:b], start=True, stop=True).then_inc(proj_ready, 1)
                    made_items[0] += 1
            for s0 in (S_VA, S_VB):
                for q in range(4):
                    w = weights(s0 + q).rearrange("p (k c) -> p k c", k=2)
                    for t in range(5):
                        out = (item(made_items[0] + t) if q == 0 else bank[(made_items[0] + t) % 6])[0:ROWS[t], :]
                        for kk in range(2):
                            k = 2 * q + kk
                            last = mm(out, xn[:, k, t * P:t * P + ROWS[t]], w[:, kk], start=(k == 0), stop=(k == KD - 1))
                        if q == 3:
                            last.then_inc(proj_ready, 1)
                    if q < 3:
                        last.then_inc(kstep, 1)
                made_items[0] += 5
            for j in range(4):
                project(S_RB + j)
            for j in range(16):
                project(S_GA + j)

            w4 = zs.rearrange("p (b h g) -> p b g h", b=NB, h=H)
            zrow = cst("zeros")[:, 0:1].to_broadcast([P, 512])
            rounds = PAGES // RING_V

            def v_rounds(b, first, end):
                out = bank[V_BANK[b]][0:H, :]
                if first == 0:
                    if b >= 4:
                        pe.wait_ge(v_taken, max(b - 1, 4))
                    mm(out, cst("zeros"), zrow, start=True, stop=True)
                for g in range(first, end):
                    for s in range(RING_V):
                        if b < V_EARLY:
                            pe.wait_ge(v_early[s], 16 * (b * rounds + g + 1))
                        else:
                            pe.wait_ge(v_landed[s], 16 * ((b - V_EARLY) * rounds + g + 1))
                        mm(out, w4[:, b, PAGES - 1 - g * RING_V - s], vring[:, s],
                           start=False, stop=True, skip_group_check=True).then_inc(v_free, 1)

            def v_fold(b):
                pe.wait_ge(v_masked, b + 1)
                for m in range(4):
                    last = mm(bank[V_BANK[b]][:, m:m + 1], v_own[b % 2][:, m * P:m * P + P], cst("one")[0:H], start=True, stop=True)
                last.then_inc(v_done, 1)

            def later_keys(half):
                for q in range(2):
                    pe.wait_ge(dec_sp, 2 * half + q + 1)
                    o = 512 * q
                    late = lambda x: x.rearrange("p (r g) -> p r g", g=PAGES)
                    out = bank[2 * half + q][:, :]
                    mm(out, cst("neg_tri"), tmp[:, 1024 + o:1536 + o], start=True, stop=True)
                    mm(late(out)[:, :, 1:PAGES], cst("neg_ones"), late(tmp[:, 2048 + o:2560 + o])[:, :, 0:PAGES - 1],
                       start=False, stop=True, skip_group_check=True).then_inc(dec_z, 1)

            pe.wait_ge(proj_taken, N_ITEMS)
            later_keys(0)
            pe.wait_ge(dec_w, 2)
            v_rounds(0, 0, 4)
            v_rounds(1, 0, 4)
            later_keys(1)
            v_rounds(2, 0, 4)
            pe.wait_ge(dec_arg, 4)
            pe.wait_ge(gla_in, 1)
            for m in range(2):
                for t in range(NT):
                    last = tr(bank[m][:, t * P:t * P + P], kd[:, m, t * P:t * P + P], ident)
                last.then_inc(kd_tr, 1)
            for b in range(3):
                v_fold(b)
            v_rounds(3, 0, 1)
            pe.wait_ge(v_taken, 3)
            pe.wait_ge(gla_in, 3)
            qrow = lambda par: slice(64 * par, 64 * par + 64)
            for u in range(2):
                if u == 1:
                    pe.wait_ge(o_taken, 2)
                for par in range(2):
                    for tt in range(2):
                        for m in range(2):
                            t = slice((2 * u + tt) * P, (2 * u + tt) * P + P)
                            last = mm(bank[2 + par][:, (2 * tt + m) * P:(2 * tt + m) * P + P], kt[qrow(par), m, t], qt[qrow(par), m, t],
                                      start=True, stop=True)
                    last.then_inc(sc_ready, 1)
                if u == 0:
                    v_rounds(3, 1, 2)
                pe.wait_ge(kd_rows, 2)
                for c2 in range(2):
                    for tt in range(2):
                        for m in range(2):
                            for par in range(2):
                                t = 2 * u + tt
                                h = 2 * m + par
                                rows = qrow(c2)
                                last = mm(bank[(4 if u == 0 else 0) + c2][qrow(par), (2 * tt + m) * P:(2 * tt + m) * P + P],
                                          kdr[rows, t, m, 64 * par:64 * par + 64], vab[rows, t, 512 + h * P:512 + h * P + P],
                                          start=True, stop=True)
                last.then_inc(u_ready, 1)
                v_rounds(3, u + 2, u + 3)
                pe.wait_ge(sc_done, 2 * u + 2)
                pe.wait_ge(states_done, u + 1)
                for par in range(2):
                    for tt in range(2):
                        for m in range(2):
                            t, h, col = 2 * u + tt, 2 * m + par, (2 * tt + m) * P
                            mm(bank[2 + par][:, col:col + P], vab[:, t, 512 + h * P:512 + h * P + P], sc_v[:, par, 2 * tt + m],
                               start=True, stop=True)
                            for c2 in range(2):
                                last = mm(bank[2 + par][:, col + 64 * c2:col + 64 * c2 + 64], states[qrow(par), 2 * t + c2, m],
                                          qe[qrow(par), m, t * P + 64 * c2:t * P + 64 * c2 + 64], start=False, stop=True,
                                          skip_group_check=True)
                    last.then_inc(o_ready, 1)
            for b in range(NB):
                if b >= 1:
                    pe.wait_ge(vb_taken, b)
                mm(bank[7][:, :], ident[0:NB, b:b + 1].to_broadcast([NB, P]), vab[0:NB, NT, 512:1024], start=True, stop=True).then_inc(vb_ready, 1)
            v_fold(3)
            pe.wait_ge(dec_w, 4)
            v_rounds(4, 0, 1)
            pe.wait_ge(ss_ready, 1)
            for par in range(2):
                for m in range(2):
                    for b in range(NB):
                        last = mm(bank[7 if par == 0 else 1][:, m * NB + b:m * NB + b + 1], sstate[qrow(par), b, m],
                                  qkb[qrow(par), m, SEQ + b:SEQ + b + 1], start=True, stop=True)
                last.then_inc(so_ready, 1)
            for h in range(GH):
                pe.wait_ge(ob_sq, h + 1)
                if h >= 1:
                    pe.wait_ge(ob_std, 2 * h)
                for half, (a, b) in enumerate(HALVES):
                    mm(bank[4 + half][:, 0:HALF], cst("mean_gdv"), ob_tmp[:, h % 2, a:b], start=True, stop=True).then_inc(ob_mean, 1)
                if h < GH - 1:
                    v_rounds(4, h + 1, h + 2)

            def v_round(r):
                v_rounds(5 + r // rounds, r % rounds, r % rounds + 1)

            pe.wait_ge(yb_ready, GH)
            for h in range(H):
                m, rows = h // 2, qrow(h % 2)
                if h >= 1:
                    pe.wait_ge(att_w, NT * h)
                if h in FOLD_AT:
                    v_fold(FOLD_AT[h])
                for n in range(NT):
                    mm(bank[n][:, 0:SEQ - P * n], qk[rows, 4 + m, n * P:n * P + P], qk[rows, m, n * P:SEQ],
                       start=True, stop=True).then_inc(z_ready, 1)
                v_round(h + h // 2)
                pe.wait_ge(att_sp, h + 1)
                at = [2560, 3072, 3456, 3712]
                for n in range(NT):
                    w = SEQ - P * n
                    mm(bank[n][:, 0:w], cst("neg_tri"), tmp[:, at[n]:at[n] + w], start=False, stop=True, skip_group_check=True)
                    for k2 in range(n + 1, NT):
                        mm(bank[n][:, P * (k2 - n):w], cst("neg_ones"), tmp[:, at[k2]:at[k2] + SEQ - P * k2],
                           start=False, stop=True, skip_group_check=True)
                    mm(bank[n][:, 0:P], ident, cst("neg_mask"), start=False, stop=True, skip_group_check=True).then_inc(acc_ready, 1)
                if h % 2 == 1:
                    v_round(h + h // 2 + 1)
                if m >= 2:
                    pe.wait_ge(y_taken, m - 1)
                for n in range(NT):
                    pe.wait_ge(att_w, NT * h + n + 1)
                    last = mm(bank[4 + m % 2][rows, P * n:SEQ], vab[:, n, h * HD:h * HD + HD], tmp[:, at[n] + 1280:at[n] + 1280 + SEQ - P * n],
                              start=(n == 0), stop=(n == NT - 1), skip_group_check=True)
                if h % 2 == 1:
                    last.then_inc(y_ready, 1)
            v_fold(NB - 1)

            pe.wait_ge(y_taken, 5)
            for m in range(8):
                w = weights(S_UP + m).rearrange("p (u k c) -> p u k c", u=2, k=4)
                for q in range(4):
                    i = 4 * m + q
                    a, b = HALVES[q % 2]
                    if i >= 8:
                        pe.wait_ge(up_taken, i - 7)
                    src = yaT if q < 2 else srb
                    for k in range(4):
                        last = mm(bank[i % 8][:, 0:HALF], w[:, q // 2, k], src[:, k, a:b], start=(k == 0), stop=(k == 3))
                    last.then_inc(up_ready, 1)
            pe.wait_ge(mix_ready, 8)
            for half in range(2):
                for q in range(4):
                    w = weights(S_WO + 4 * half + q).rearrange("p (k c) -> p k c", k=2)
                    for t in range(5):
                        i = 5 * half + t
                        if q == 0 and i >= 8:
                            pe.wait_ge(wo_taken, i - 7)
                        for kk in range(2):
                            k = 2 * q + kk
                            last = mm(bank[i % 8][0:ROWS[t], :], mixT[:, k, t * P:t * P + ROWS[t]], w[:, kk], start=(k == 0), stop=(k == KD - 1))
                        if q == 3:
                            last.then_inc(wo_ready, 1)
                    if q < 3:
                        last.then_inc(kstep, 1)

            pe.wait_ge(wo_taken, 10)
            for t in range(5):
                R = ROWS[t]
                pe.wait_ge(xn2_ready, t + 1)
                for k in range(KD):
                    n = 2 * t + (k // 4 if t < NT else 0)
                    if k % 4 == 0 and n >= 6:
                        pe.wait_ge(x2t_taken, n - 5)
                    col = (k % 4) * P if t < NT else k * NB
                    last = tr(bank[2 + n % 6][:, col:col + R], xn2[0:R, t, k * P:k * P + P], ident[0:R, 0:R])
                    if k == KD - 1 or (k == 3 and t < NT):
                        last.then_inc(x2t_ready, 1)

            def scores(j):
                pe.wait_ge(pq_taken, 2 * (j + 1))
                if j >= 2:
                    pe.wait_ge(s_taken, 2 * (j - 1))
                for t in range(NT):
                    last = mm(bank[4 + j % 2][:, t * P:t * P + P], qp[:, j % 2, t * P:t * P + P], sk[:, j], start=True, stop=True)
                last.then_inc(s_ready, 1)
                mm(bank[6 + j % 2][0:NB, 0:P], qp[:, j % 2, SEQ:T], sk[:, j], start=True, stop=True).then_inc(s_ready, 1)

            pe.wait_ge(x2t_taken, 9)
            for j in range(16):
                w = weights(S_PQ + j).rearrange("p (k c) -> p k c", k=KD)
                for half, (a, b) in enumerate(HALVES):
                    i = 2 * j + half
                    if i >= 4:
                        pe.wait_ge(pq_taken, i - 3)
                    for k in range(KD):
                        last = mm(bank[i % 4][:, 0:HALF], w[:, k], xn2T[:, k, a:b], start=(k == 0), stop=(k == KD - 1))
                    last.then_inc(pq_ready, 1)
                if j >= 1:
                    scores(j - 1)
            scores(15)

            pe.wait_ge(s_taken, 32)
            pe.wait_ge(late_landed, 96)

            def x3_columns(t):
                R = ROWS[t]
                pe.wait_ge(xn3_ready, t + 1)
                if t >= 1:
                    pe.wait_ge(y_out, t)
                for k in range(KD):
                    last = tr(bank[4 + k // 4][:, (k % 4) * R:(k % 4) * R + R], xn2[0:R, t, k * P:k * P + P], ident[0:R, 0:R])
                    if k % 4 == 3:
                        last.then_inc(x3t_ready, 1)

            def ple(t):
                R = ROWS[t]
                pe.wait_ge(x3t_taken, 2 * (t + 1))
                for c2 in range(2):
                    for k in range(KD):
                        last = mm(bank[6 + c2][0:R, :], xn3T[:, k, 0:R], wpg[:, k, 512 * c2:512 * c2 + 512], start=(k == 0), stop=(k == KD - 1))
                    last.then_inc(ple_ready, 1)
                for c2 in range(2):
                    for k in range(2):
                        last = mm(bank[4 + c2][0:R, :], pT[:, k, t * P:t * P + R], ple_w[:, k, 512 * c2:512 * c2 + 512], start=(k == 0), stop=(k == 1))
                    last.then_inc(ple_ready, 1)

            for t in range(NT):
                yb = Y_BANKS[t % 2]
                if t >= 2:
                    pe.wait_ge(h2_ready, t - 1)
                for c2 in range(2):
                    mm(bank[yb[c2]][:, :], ident, zrow, start=True, stop=True, skip_group_check=True)
                for k in range(SEGMENTS):
                    if t >= 1 and k == 3:
                        x3_columns(t - 1)
                    elif t >= 1 and k == 4:
                        ple(t - 1)
                    with pe.Fori(k * SEG, (k + 1) * SEG) as i:
                        for g in range(4):
                            pe.wait_ge(diag_ready, i * 4 + (t * 64 + g + 1))
                            for s in (2 * g, 2 * g + 1):
                                for c2 in range(2):
                                    last = mm(bank[yb[c2]][:, :], diag[:, s], gring[:, s, D + 512 * c2:D + 512 * c2 + 512],
                                              start=False, stop=True, skip_group_check=True)
                            last.then_inc(g_used, 1)
                for c2 in range(2):
                    last = mm(bank[yb[c2]][:, :], ident, zrow, start=False, stop=True, skip_group_check=True)
                last.then_inc(y_sum, 1)
            x3_columns(NT - 1)
            yb = Y_BANKS[NT % 2]
            pe.wait_ge(diag_ready, NT * 64 + 1)
            for r in range(8):
                for c2 in range(2):
                    last = mm(bank[yb[c2]][0:NB, :], diag[:, r, 0:NB], gring[:, r, D + 512 * c2:D + 512 * c2 + 512],
                              start=(r == 0), stop=(r == 7), skip_group_check=True)
            mm(bank[yb[1]][0:NB, :], ident[:, 0:NB], zrow, start=False, stop=True, skip_group_check=True).then_inc(y_sum, 1)
            ple(NT - 1)
            x3_columns(NT)
            ple(NT)


def kernel(x_prompt, x_sample, p_prompt, p_sample, cache_k, cache_v, state_gla, page_table, norm1_g, w_in, b_gate,
           qa_norm_g, ka_norm_g, sb_bias, w_alpha, b_alpha, ob_norm_g, w_up_a, w_up_b, w_o, norm2_g, w_peer_q,
           peer_sub_keys, expert_u, expert_v, norm3_g, w_ple, w_ple_gate):
    import concourse.bacc as bacc
    from concourse.bass_utils import run_bass_kernel_spmd

    n = np.asarray

    def tiles(w):
        k, m = w.shape[0] // P, w.shape[1] // P
        return w.reshape(k, P, m, P).transpose(2, 1, 0, 3).reshape(m, P, k * P)

    def by_pairs(w):
        j = w.shape[1] // 512
        return w.reshape(4, 2, P, j, 512).transpose(3, 0, 2, 1, 4).reshape(4 * j, P, 1024)

    def by_feature(a):
        return a.reshape(a.shape[0], -1, P).transpose(2, 1, 0)

    wi = n(w_in)[0]
    cut = np.cumsum([512, 512, 512, 256, 256, 512, 512, 16, 1024, 1024])
    qa, ka, va, qb, kb, vb, rb, ab, gza, gzb = np.split(wi, cut[:-1], axis=1)
    up = np.stack([tiles(n(w_up_a)[0]), tiles(n(w_up_b)[0])], axis=2)
    w_stream = np.concatenate([
        tiles(qa), tiles(ka), tiles(qb), tiles(kb), by_pairs(va), by_pairs(vb), tiles(rb), tiles(gza), tiles(gzb),
        up.reshape(8, P, 1024), by_pairs(n(w_o)[0]), tiles(n(w_peer_q)[0])])
    col = lambda a: a.reshape(-1, P).T
    vecs = np.concatenate([
        col(n(norm1_g)[0]), np.tile(n(qa_norm_g)[0], 2)[:, None], np.tile(n(ka_norm_g)[0], 2)[:, None],
        col(n(b_alpha)[0]), col(n(b_gate)[0].reshape(-1)), n(ob_norm_g)[0][:, None]], axis=1)
    x = np.concatenate([n(x_prompt)[0], n(x_sample)[:, 0]])
    p = np.concatenate([n(p_prompt)[0, 0], n(p_sample)[0, :, 0]])
    feeds = {
        "consts": _consts(),
        "vecs": vecs,
        "xT": by_feature(x),
        "x_rows": x,
        "w_ab": ab.reshape(KD, P, RANK).transpose(1, 0, 2),
        "w_alpha": n(w_alpha)[0],
        "sb_bias": n(sb_bias)[0],
        "w_stream": w_stream,
        "cache_k": n(cache_k)[0].reshape(-1, P, PAGE_ROW),
        "cache_v": n(cache_v)[0].reshape(-1, P, PAGE_ROW),
        "page_table": n(page_table).reshape(1, -1),
        "state": n(state_gla)[0].reshape(NB, 2, 2 * GDK, GDV).transpose(2, 0, 1, 3),
        "norm2_g": n(norm2_g)[0],
        "norm3_g": n(norm3_g)[0],
        "sub_keysT": n(peer_sub_keys)[0].reshape(16, NKEYS, P).transpose(2, 0, 1),
        "experts": np.concatenate([n(expert_u)[0], n(expert_v)[0]], axis=1),
        "pT": by_feature(p),
        "w_ple": n(w_ple)[0].reshape(2, P, D).transpose(1, 0, 2),
        "w_ple_gate": n(w_ple_gate)[0].reshape(KD, P, D).transpose(1, 0, 2),
    }
    outs = {"y": (T, D), "new_kT": (512, T), "new_v": (T, 512), "gla_prompt": (P, 2, GDV), "gla_sample": (P, NB, 2, GDV)}
    nc = bacc.Bacc("TRN2", target_bir_lowering=False, num_devices=1)
    aps, arrays = {}, {}
    for name, a in feeds.items():
        arrays[name + "_in"] = np.ascontiguousarray(a)
        aps[name] = nc.dram_tensor(name + "_in", a.shape, mybir.dt.from_np(a.dtype), kind="ExternalInput").ap()
    for name, shape in outs.items():
        aps[name] = nc.dram_tensor(name + "_out", shape, F32, kind="ExternalOutput").ap()
    build(nc, aps)
    r = run_bass_kernel_spmd(nc, [arrays], core_ids=[0]).results[0]
    y, kT, v = r["y_out"], r["new_kT_out"], r["new_v_out"]
    k = kT.T.reshape(T, H, HD)
    v = v.reshape(T, H, HD)
    sp = r["gla_prompt_out"].reshape(2, GDK, 2, GDV).transpose(2, 0, 1, 3).reshape(1, 1, GH, GDK, GDV)
    ss = r["gla_sample_out"].reshape(2, GDK, NB, 2, GDV).transpose(2, 3, 0, 1, 4).reshape(1, NB, GH, GDK, GDV)
    return (y[None, :SEQ], y[SEQ:, None], k[None, None, :SEQ], v[None, None, :SEQ], sp,
            k[None, SEQ:, None], v[None, SEQ:, None], ss)
```

```python
from contextlib import ExitStack

import numpy as np

import concourse.bass as bass
from concourse import mybir

F32 = mybir.dt.float32
U32 = mybir.dt.uint32
I32 = mybir.dt.int32
ALU = mybir.AluOpType
ACT = mybir.ActivationFunctionType
AX = mybir.AxisListType

P = 128
D = 1024
KD = D // P
SEQ = 512
NB = 8
T = SEQ + NB
HALF = T // 2
HALVES = ((0, HALF), (HALF, T))
NT = SEQ // P
ROWS = [P] * NT + [NB]
H = 8
HD = 64
GH = 4
GDK, GDV = 64, 128
CHUNK = 64
NCH = SEQ // CHUNK
RANK = 16
TAU = 16.0
PAGES = 32
PAGE_ROW = H * HD
PH = 8
NKEYS = 128
TOPK = 16
SEL = PH * TOPK
PLE = 256
EPS = 1e-6
NEG = -1e30
LOWEST = -3.0e38
Y_BANKS = ((2, 3), (0, 1))

RING_K = 8
PRODS = 4
RING_V = 8
KEYS_BANK = (6, 7, 0, 1)
V_EARLY = 4
V_BANK = (4, 5, 7, 6, 6, 7, 6, 7)
FOLD_AT = {0: 4, 3: 5, 6: 6}
STD_BUF = (0, 1, 0, 1, 2, 3, 4, 0)
RING_W = 4
RING_G = 8
SEGMENTS = 8
SEG = SEL // RING_G // SEGMENTS

S_QA, S_KA, S_QB, S_KB, S_VA, S_VB, S_RB, S_GA, S_GB = 0, 4, 8, 10, 12, 16, 20, 24, 32
S_UP, S_WO, S_PQ, S_END = 40, 48, 56, 72

CONSTS = {}


def _consts():
    i, j = np.arange(P)[:, None], np.arange(P)[None, :]
    pieces = [
        ("ident", i == j),
        ("mean_model", np.full((P, P), 1.0 / D)),
        ("mean_head", (i // HD == j // HD) / float(HD)),
        ("mean_gdv", np.full((P, P), 1.0 / GDV)),
        ("neg_tri", -1.0 * (i >= j)),
        ("neg_ones", np.full((P, P), -1.0)),
        ("neg_mask", NEG * (i >= j)),
        ("keep_mask", i < j),
        ("gla_mask", (i <= j) & (i // CHUNK == j // CHUNK)),
        ("chunk_reset", np.broadcast_to(np.arange(SEQ) % CHUNK != 0, (P, SEQ))),
        ("page_reset", np.broadcast_to(np.arange(512) % PAGES != 0, (P, 512))),
        ("iota16", np.broadcast_to(np.arange(TOPK), (P, TOPK))),
        ("sample_of", np.arange(P)[:, None] // (P // NB) == np.arange(NB)[None, :]),
        ("zeros", np.zeros((P, NB))),
        ("eps", np.full((P, 1), EPS)),
        ("one", np.ones((P, 1))),
    ]
    at = 0
    for name, a in pieces:
        CONSTS[name] = (at, at + a.shape[1])
        at += a.shape[1]
    return np.concatenate([np.asarray(a, np.float32) for _, a in pieces], axis=1)


N_CONST = _consts().shape[1]

V_G1, V_QG, V_KG, V_BA, V_BG, V_OG, N_VEC = 0, 8, 9, 10, 12, 28, 29


class Steps:

    def __init__(self, eng, own):
        self.eng, self.own, self.count, self.last = eng, own, {}, None

    def also(self, op, *args, signal=None, **kw):
        sem = signal if signal is not None else self.own
        key = sem.name
        self.count[key] = self.count.get(key, 0) + 1
        op(*args, **kw).then_inc(sem, 1)
        self.last = (sem, self.count[key])

    def settle(self):
        if self.last is not None:
            self.eng.wait_ge(*self.last)

    def then(self, op, *args, signal=None, **kw):
        self.settle()
        self.also(op, *args, signal=signal, **kw)


def lay(start, sizes):
    out = {}
    for name, n in sizes:
        out[name] = (start, start + n)
        start += n
    return out, start


def build(nc, A):
    with ExitStack() as ctx:
        COLS = 53200
        arena = ctx.enter_context(nc.sbuf_tensor("arena", [P, COLS], F32))
        bank = [ctx.enter_context(nc.psum_tensor(f"bank{i}", [P, 512], F32))[:, :] for i in range(8)]

        def sem(name):
            return ctx.enter_context(nc.semaphore(name))

        def sems(name, n):
            return [sem(f"{name}{i}") for i in range(n)]

        kept, at = lay(0, [("consts", N_CONST), ("vecs", 32), ("wring", RING_W * 1024)])
        first, end1 = lay(at, [
            ("gates", 16 * T), ("vab", 5 * 1024), ("srb", 4 * T), ("qk", 8 * T), ("qkb", 4 * T),
            ("zs", 2048), ("vring", RING_V * PAGE_ROW), ("la", 2 * T), ("abT", T), ("rowh", H), ("v_cols", 4 * NB),
            ("pt", NB * PAGES), ("abw", KD * RANK), ("alw", 256),
            ("xn", 8 * T), ("xT", 8 * T), ("kring", RING_K * PAGE_ROW), ("prod", PRODS * PAGE_ROW)])
        second, end2 = lay(first["xn"][0], [
            ("tmp", 6144), ("cum", 2 * SEQ), ("qt", 2 * SEQ), ("kt", 2 * SEQ), ("qe", 2 * SEQ), ("kd", 2 * SEQ),
            ("gsmall", 64), ("states", 2 * (NCH + 1) * GDV), ("sstate", NB * 2 * GDV), ("kdr", 2 * SEQ)])
        assert end1 <= COLS and end2 <= COLS, (end1, end2)
        at3 = first["vab"][1]
        third, end3 = lay(at3, [
            ("xn2", 5 * D), ("g2", D), ("v16", 5 * 256), ("i16", 5 * 256), ("cand", 2048), ("onehot", 2048),
            ("expert", 5 * SEL), ("gate", 5 * SEL), ("top", 10 * SEL), ("i16f", 256), ("small", 128),
            ("xn2T", 8 * T), ("sk", 16 * P), ("qp", 2 * T), ("s_all", 5 * 2048)])
        assert end3 <= COLS, end3
        fourth, end4 = lay(third["xn2T"][0], [("gring", RING_G * 2 * D)])
        assert end4 <= end3
        fifth, end5 = lay(first["gates"][0], [("wpg", KD * D)])
        assert end5 <= first["vab"][0]
        sixth, end6 = lay(end4, [("diag", RING_G * P)])
        lists, end_lists = lay(end6, [("s_list", NKEYS), ("v_list", TOPK), ("i_list", TOPK)])
        assert end_lists <= COLS, end_lists
        seventh, end7 = lay(kept["wring"][0], [("ple_w", 2 * D), ("xn3T", D), ("sx", D)])
        assert end7 <= kept["wring"][1]
        eighth = {"pT": (P, P + 2 * T), "g3": third["g2"], "fin": (third["cand"][0], third["cand"][0] + D)}
        maps = {}
        for m in (kept, first, second, third, fourth, fifth, sixth, seventh, eighth, lists):
            maps.update(m)

        def view(name):
            a, b = maps[name]
            return arena[:, a:b]

        def cst(name):
            a, b = CONSTS[name]
            return arena[:, maps["consts"][0] + a:maps["consts"][0] + b]

        vecs = view("vecs")
        ident = cst("ident")
        wring = view("wring").rearrange("p (s c) -> p s c", s=RING_W)
        gates = view("gates").rearrange("p (m t) -> p m t", m=16)
        mixT = gates[:, 0:8]
        vab = view("vab").rearrange("p (t c) -> p t c", t=5)
        h1 = vab
        srb = view("srb").rearrange("p (m t) -> p m t", m=4)
        qk = view("qk").rearrange("p (m t) -> p m t", m=8)
        qkb = view("qkb").rearrange("p (m t) -> p m t", m=4)
        zs = view("zs")
        vring = view("vring").rearrange("p (s c) -> p s c", s=RING_V)
        la = view("la").rearrange("p (m t) -> p m t", m=2)
        abT = view("abT")
        bias_row = view("rowh")
        xn = view("xn").rearrange("p (m t) -> p m t", m=8)
        xT = view("xT").rearrange("p (m t) -> p m t", m=8)
        qbc = view("xT")[:, 0:NB * PAGE_ROW].rearrange("p (b c) -> p b c", b=NB)
        kring = view("kring").rearrange("p (s c) -> p s c", s=RING_K)
        prod = view("prod").rearrange("p (s c) -> p s c", s=PRODS)
        tmp = view("tmp")
        part_l, part_sp, part_sum = (arena[:, end1 + 512 * i:end1 + 512 * (i + 1)] for i in range(3))
        assert end1 + 3 * 512 <= COLS
        cum = view("cum").rearrange("p (m t) -> p m t", m=2)
        sc_v = view("cum").rearrange("p (q a c) -> p q a c", q=2, a=4)
        qt = view("qt").rearrange("p (m t) -> p m t", m=2)
        kt = view("kt").rearrange("p (m t) -> p m t", m=2)
        qe = view("qe").rearrange("p (m t) -> p m t", m=2)
        kd = view("kd").rearrange("p (m t) -> p m t", m=2)
        a0 = maps["qt"][0]
        yaT = arena[:, a0:a0 + 4 * T].rearrange("p (m t) -> p m t", m=4)
        assert a0 + 4 * T <= maps["qe"][1]
        states = view("states").rearrange("p (c m e) -> p c m e", c=NCH + 1, m=2)
        sstate = view("sstate").rearrange("p (b m e) -> p b m e", b=NB, m=2)
        kdr = view("kdr").rearrange("p (t m c) -> p t m c", t=NT, m=2)
        page_table = view("pt").bitcast(I32)
        abw = view("abw").rearrange("p (k c) -> p k c", k=KD)
        alw = view("alw")[0:RANK]
        qk_sq = view("vring")[:, 0:2 * T].rearrange("p (u t) -> p u t", u=2)
        qk_std = view("vring")[:, 2 * T:7 * T].rearrange("p (u t) -> p u t", u=5)
        v_own = [view("abT")[0:H, 0:512], tmp[0:H, 5168:5680]]
        v_cols = view("v_cols").rearrange("p (m b) -> p m b", m=4)
        gsmall = view("gsmall")
        chunk_decay, sample_decay = gsmall[:, 0:16], gsmall[:, 16:32].rearrange("p (m b) -> p m b", m=2)
        kv = tmp[:, 0:2048].rearrange("p (b m e) -> p b m e", b=NB, m=2)
        ob = tmp[:, 2048:2048 + 4 * T].rearrange("p (m t) -> p m t", m=4)
        ob_tmp = tmp[:, 0:3 * T].rearrange("p (u t) -> p u t", u=3)
        g2, g3 = view("g2"), view("g3")
        xn2 = view("xn2").rearrange("p (t c) -> p t c", t=5)
        xn2T = view("xn2T").rearrange("p (m t) -> p m t", m=8)
        sk = view("sk").rearrange("p (j n) -> p j n", j=16)
        qp = view("qp").rearrange("p (u t) -> p u t", u=2)
        s_all = view("s_all").rearrange("p (t j n) -> p t j n", t=5, j=16)
        v16 = view("v16").rearrange("p (t j n) -> p t j n", t=5, j=16)
        i16 = view("i16").bitcast(U32).rearrange("p (t j n) -> p t j n", t=5, j=16)
        cand = view("cand").rearrange("p (h n) -> p h n", h=PH)
        onehot = view("onehot").rearrange("p (h k j) -> p h k j", h=PH, k=TOPK)
        i16f = view("i16f").rearrange("p (j n) -> p j n", j=16)
        expert = view("expert").bitcast(U32).rearrange("p (t c) -> p t c", t=5)
        gate = view("gate").rearrange("p (t c) -> p t c", t=5)
        top = view("top").rearrange("p (u h k) -> p u h k", u=10, h=PH)
        top_u = view("top").bitcast(U32).rearrange("p (u h k) -> p u h k", u=10, h=PH)
        small = view("small")
        ssq, rstd2, den = small[:, 0:10], small[:, 10:20], small[:, 20:28]
        dot, act_g, coef = small[:, 32:40], small[:, 40:48], small[:, 48:56]
        slot_idx = view("small").bitcast(U32)[:, 56:64]
        idx_guard = view("small").bitcast(U32)[:, 80:82]
        zero_u = cst("zeros")[:, 0:2].bitcast(U32)
        sidx, sgate = view("small").bitcast(U32)[:, 64:72], small[:, 72:80]
        gring = view("gring").rearrange("p (s c) -> p s c", s=RING_G)
        wpg = view("wpg").rearrange("p (k c) -> p k c", k=KD)
        pT = view("pT").rearrange("p (m t) -> p m t", m=2)
        ple_w = view("ple_w").rearrange("p (m c) -> p m c", m=2)
        xn3T = view("xn3T").rearrange("p (k t) -> p k t", k=KD)
        fin, fin_samples = view("fin"), arena[:, maps["fin"][1]:maps["fin"][1] + D]
        assert maps["fin"][1] + D <= maps["cand"][1]
        x3_samples = view("top")[:, 0:KD * NB].rearrange("p (k t) -> p k t", k=KD)

        def end_buffers(t):
            return (fin_samples, x3_samples, (0, 1), (2, 3)) if t == NT else (fin, xn3T, (4, 5), (6, 7))

        diag = view("diag").rearrange("p (s c) -> p s c", s=RING_G)
        sx = view("sx")

        s_list, v_list, i_list = view("s_list"), view("v_list"), view("i_list").bitcast(U32)

        scratch_s = nc.dram_tensor("scratch_scores", (NB, 16 * NKEYS), F32, kind="Internal").ap()
        scratch_v = nc.dram_tensor("scratch_best", (NB, 16 * TOPK), F32, kind="Internal").ap()
        scratch_i = nc.dram_tensor("scratch_places", (NB, 16 * TOPK), U32, kind="Internal").ap()
        scratch_e = nc.dram_tensor("scratch_expert", (NB, SEL), U32, kind="Internal").ap()
        scratch_g = nc.dram_tensor("scratch_gate", (NB, SEL), F32, kind="Internal").ap()
        scratch_x = nc.dram_tensor("scratch_x", (NB, D), F32, kind="Internal").ap()

        items = []
        ends = {}

        def tile_items(s, kind, j):
            for half in range(2):
                items.append((kind, j, half))
            ends[s] = len(items)
        for j in range(8):
            tile_items(S_QA + j, "qk", j)
        AB_ITEM = len(items)
        items += [("ab", 0, 0), ("ab", 0, 1)]
        for j in range(4):
            tile_items(S_QB + j, "qkb", j)
        ALPHA_ITEM = len(items)
        items += [("alpha", m, half) for m in range(2) for half in range(2)]
        for s, kind in ((S_VA, "va"), (S_VB, "vb")):
            items += [(kind, t, 0) for t in range(5)]
            ends[s + 3] = len(items)
        RB_ITEM = len(items)
        for j in range(4):
            tile_items(S_RB + j, "rb", j)
        GATE_ITEM = len(items)
        for j in range(16):
            tile_items(S_GA + j, "gate", j)
        N_ITEMS = len(items)

        w_in_slot = sems("w_landed", RING_W)
        k_landed = sems("k_landed", RING_K)
        v_landed = sems("v_landed", RING_V)
        v_early = sems("v_early", RING_V)
        x_landed = sems("x_landed", 2)
        consts_landed, table_landed = sem("consts_landed"), sem("table_landed")
        wab_landed, state_landed = sem("wab_landed"), sem("state_landed")
        sq_ready, mean1, std1, xn_ready = sem("sq_ready"), sem("mean1"), sem("std1"), sem("xn_ready")
        proj_ready, proj_taken, kstep = sem("proj_ready"), sem("proj_taken"), sem("kstep")
        qksq, qkmean, qkstd, qk_done = sem("qksq"), sem("qkmean"), sem("qkstd"), sem("qk_done")
        qb_ready, qb_taken = sem("qb_ready"), sem("qb_taken")
        k_mul, k_free = sem("k_mul"), sem("k_free")
        act_steps, dve_steps, pool_steps = sem("act_steps"), sem("dve_steps"), sem("pool_steps")
        out_done = sem("out_done")
        v_free = sem("v_free")
        zb_ready, dec_l, dec_sp, dec_z, dec_arg, dec_w = (sem(n) for n in ("zb_ready", "dec_l", "dec_sp", "dec_z", "dec_arg", "dec_w"))
        la_in, la_ready, gla_d, gla_e, gla_in = (sem(n) for n in ("la_in", "la_ready", "gla_d", "gla_e", "gla_in"))
        kd_tr, kd_rows, sc_ready, sc_done, u_ready, states_done, o_ready, o_taken = (
            sem(n) for n in ("kd_tr", "kd_rows", "sc_ready", "sc_done", "u_ready", "states_done", "o_ready", "o_taken"))
        vb_ready, vb_taken, ss_ready, so_ready, ob_sq, ob_mean, ob_std, yb_ready = (
            sem(n) for n in ("vb_ready", "vb_taken", "ss_ready", "so_ready", "ob_sq", "ob_mean", "ob_std", "yb_ready"))
        z_ready, att_l, att_r, att_sp, acc_ready, att_w, y_ready, y_taken = (
            sem(n) for n in ("z_ready", "att_l", "att_r", "att_sp", "acc_ready", "att_w", "y_ready", "y_taken"))
        v_masked, v_done, v_taken = sem("v_masked"), sem("v_done"), sem("v_taken")
        up_ready, up_taken, mix_ready = sem("up_ready"), sem("up_taken"), sem("mix_ready")
        wo_ready, wo_taken = sem("wo_ready"), sem("wo_taken")
        rows_landed = sem("rows_landed")
        h_std, xn2_ready, x2t_ready, x2t_taken = (sem(n) for n in ("h_std", "xn2_ready", "x2t_ready", "x2t_taken"))
        pq_ready, pq_taken, s_ready, s_taken, topk_done = (sem(n) for n in ("pq_ready", "pq_taken", "s_ready", "s_taken", "topk_done"))
        sel_ready, soft_in, soft_e = sem("sel_ready"), sem("soft_in"), sem("soft_e")
        g_landed = sems("g_landed", RING_G)
        dots, gel, gated, diag_ready, g_used = (sem(n) for n in ("dots", "gel", "gated", "diag_ready", "g_used"))
        idx_copied = sem("idx_copied")
        y_sum, h2_ready, h3_std, xn3_ready, x3t_ready, x3t_taken, ple_ready, ple_sig, y_out = (
            sem(n) for n in ("y_sum", "h2_ready", "h3_std", "xn3_ready", "x3t_ready", "x3t_taken", "ple_ready", "ple_sig", "y_out"))
        second_landed, late_landed = sem("second_landed"), sem("late_landed")
        scores_out, scores_in, list_best, best_out, best_in = (
            sem(n) for n in ("scores_out", "scores_in", "list_best", "best_out", "best_in"))
        sample_out, sample_in = sem("sample_out"), sem("sample_in")

        def w_free(s):
            if s < S_UP:
                if s in ends:
                    return proj_ready, ends[s]
                base = {S_VA: 0, S_VB: 3}[S_VA if s < S_VB else S_VB]
                return kstep, base + (s - (S_VA if s < S_VB else S_VB)) + 1
            if s < S_WO:
                return up_ready, 4 * (s - S_UP + 1)
            if s < S_PQ:
                n = s - S_WO
                return (wo_ready, 5 * (n // 4 + 1)) if n % 4 == 3 else (kstep, 6 + 3 * (n // 4) + n % 4 + 1)
            return pq_ready, 2 * (s - S_PQ + 1)

        block = ctx.enter_context(nc.Block())

        @block.sync
        def _(sp):
            for k in range(2):
                sp.dma_start(xT[:, 4 * k:4 * k + 4], A["xT"][:, 4 * k:4 * k + 4]).then_inc(x_landed[k], 16)
            sp.dma_start(view("consts"), A["consts"]).then_inc(consts_landed, 16)
            sp.dma_start(vecs[:, 0:N_VEC], A["vecs"]).then_inc(consts_landed, 16)
            sp.dma_start(abw, A["w_ab"]).then_inc(wab_landed, 16)
            sp.dma_start(alw, A["w_alpha"]).then_inc(wab_landed, 16)
            sp.dma_start(bias_row, A["sb_bias"].partition_broadcast(P)).then_inc(wab_landed, 16)

            def stream(a, b):
                for s in range(a, b):
                    if s >= RING_W:
                        sp.wait_ge(*w_free(s - RING_W))
                    sp.dma_start(wring[:, s % RING_W], A["w_stream"][s]).then_inc(w_in_slot[s % RING_W], 16)

            stream(0, S_RB + RING_W)
            sp.wait_ge(qk_done, 8)
            sp.dma_start(A["new_kT"].rearrange("(m p) t -> p m t", p=P), qk[:, 4:8]).then_inc(out_done, 16)
            sp.wait_ge(proj_taken, ALPHA_ITEM + 4 + 5)
            sp.dma_start(A["new_v"][0:SEQ].rearrange("(t p) c -> p t c", p=P), vab[:, 0:NT, 0:512]).then_inc(out_done, 16)
            sp.dma_start(A["new_v"][SEQ:T], vab[0:NB, NT, 0:512]).then_inc(out_done, 16)
            stream(S_RB + RING_W, S_UP)
            sp.wait_ge(table_landed, 16)
            early_page = lambda n: sp.value_load(page_table[0:1, bass.ds(n, 1)], min_val=0, max_val=A["cache_v"].shape[0] - 1)
            with sp.Fori(0, V_EARLY * PAGES // RING_V) as i:
                pages = [early_page(i * RING_V)]
                for s in range(RING_V):
                    if s + 1 < RING_V:
                        pages.append(early_page(i * RING_V + (s + 1)))
                    sp.wait_ge(v_free, i * RING_V + (s + 1))
                    sp.dma_start(vring[:, s, :], A["cache_v"][bass.ds(pages[s], 1)].rearrange("a p n -> (a p) n")).then_inc(v_early[s], 16)
            sp.wait_ge(k_free, RING_K + NB * PAGES)
            sp.wait_ge(proj_ready, N_ITEMS)
            sp.wait_ge(dec_z, 4)
            sp.dma_start(sstate, A["state"]).then_inc(state_landed, 16)
            stream(S_UP, S_UP + RING_W)
            sp.wait_ge(states_done, 2)
            sp.dma_start(A["gla_prompt"], states[:, NCH]).then_inc(out_done, 16)
            sp.wait_ge(ss_ready, 1)
            sp.dma_start(A["gla_sample"], sstate).then_inc(out_done, 16)
            sp.wait_ge(y_ready, 4)
            sp.wait_ge(out_done, 16 * 5)
            sp.wait_ge(v_done, NB)
            sp.dma_start(h1[:, 0:NT], A["x_rows"][0:SEQ].rearrange("(t p) c -> p t c", p=P)).then_inc(rows_landed, 16)
            sp.dma_start(h1[0:NB, NT], A["x_rows"][SEQ:T]).then_inc(rows_landed, 16)
            stream(S_UP + RING_W, S_WO + RING_W)
            sp.wait_ge(mix_ready, 8)
            sp.dma_start(g2, A["norm2_g"].partition_broadcast(P)).then_inc(second_landed, 16)
            sp.dma_start(sk, A["sub_keysT"]).then_inc(second_landed, 16)
            stream(S_WO + RING_W, S_PQ + RING_W)
            sp.wait_ge(wo_ready, 10)
            sp.dma_start(wpg, A["w_ple_gate"]).then_inc(late_landed, 16)
            stream(S_PQ + RING_W, S_END)
            sp.wait_ge(xn2_ready, 5)
            sp.dma_start(scratch_x, xn2[0:NB, NT]).then_inc(sample_out, 16)
            sp.wait_ge(s_taken, 32)
            sp.dma_start(scratch_s, s_all[0:NB, NT].rearrange("p j n -> p (j n)")).then_inc(scores_out, 16)
            sp.wait_ge(scores_out, 16)
            sp.dma_start(s_list, scratch_s.rearrange("b (j n) -> (b j) n", j=16)).then_inc(scores_in, 16)
            sp.wait_ge(topk_done, 1)
            sp.dma_start(pT, A["pT"]).then_inc(late_landed, 16)
            sp.dma_start(ple_w, A["w_ple"]).then_inc(late_landed, 16)
            sp.dma_start(g3, A["norm3_g"].partition_broadcast(P)).then_inc(late_landed, 16)
            sp.wait_ge(list_best, 1)
            sp.dma_start(scratch_v.rearrange("b (j n) -> (b j) n", j=16), v_list).then_inc(best_out, 16)
            sp.dma_start(scratch_i.rearrange("b (j n) -> (b j) n", j=16), i_list).then_inc(best_out, 16)
            sp.wait_ge(best_out, 32)
            sp.dma_start(v16[0:NB, NT].rearrange("p j n -> p (j n)"), scratch_v).then_inc(best_in, 16)
            sp.dma_start(i16[0:NB, NT].rearrange("p j n -> p (j n)"), scratch_i).then_inc(best_in, 16)
            sp.wait_ge(sel_ready, NT + 1)
            sp.dma_start(scratch_e, expert[0:NB, NT]).then_inc(sample_out, 16)
            sp.dma_start(scratch_g, gate[0:NB, NT]).then_inc(sample_out, 16)
            sp.wait_ge(sample_out, 48)
            for b in range(NB):
                w = P // NB
                sp.dma_start(sx[b * w:(b + 1) * w], scratch_x[b].partition_broadcast(w)).then_inc(sample_in, 16)
            sp.dma_start(sidx, scratch_e.rearrange("b (j r) -> (b j) r", r=8)).then_inc(sample_in, 16)
            sp.dma_start(sgate, scratch_g.rearrange("b (j r) -> (b j) r", r=8)).then_inc(sample_in, 16)
            for t in range(NT + 1):
                sp.wait_ge(y_out, t + 1)
                R = ROWS[t]
                sp.dma_start(A["y"][t * P:t * P + R], h1[0:R, t]).then_inc(out_done, 16)
            sp.wait_ge(out_done, 16 * 10)

        @block.gpsimd
        def _(pool):
            c = Steps(pool, pool_steps)
            pool.dma_start(page_table[0:1, :], A["page_table"]).then_inc(table_landed, 16)
            pool.wait_ge(table_landed, 16)

            def load_page(ring, cache, landed, page, s):
                pool.dma_start(ring[:, s, :], cache[bass.ds(page, 1)].rearrange("a p n -> (a p) n")).then_inc(landed[s], 16)

            page_number = lambda n: pool.value_load(page_table[0:1, bass.ds(n, 1)], min_val=0, max_val=A["cache_k"].shape[0] - 1)

            with pool.Fori(0, NB * PAGES // RING_K) as i:
                pages = [page_number(i * RING_K + s) for s in range(RING_K)]
                for s in range(RING_K):
                    pool.wait_ge(k_free, i * RING_K + (s + 1))
                    load_page(kring, A["cache_k"], k_landed, pages[s], s)
            with pool.Fori(V_EARLY * PAGES // RING_V, NB * PAGES // RING_V) as i:
                pages = [page_number(i * RING_V + s) for s in range(RING_V)]
                for s in range(RING_V):
                    pool.wait_ge(v_free, i * RING_V + (s + 1))
                    load_page(vring, A["cache_v"], v_landed, pages[s], s)
            pool.wait_ge(scores_out, 16)
            for t in range(NT):
                pool.wait_ge(sel_ready, t + 1)
                with pool.Fori(0, SEL // RING_G) as i:
                    for g in range(4):
                        pool.wait_ge(g_used, i * 4 + (t * 64 + g + 1))
                        pair = slot_idx[:, 2 * g:2 * g + 2]
                        rows = expert[:, t, bass.ds(i * 8 + 2 * g, 2)]
                        pool.tensor_tensor(pair, rows, zero_u, ALU.add).then_inc(idx_copied, 1)
                        pool.wait_ge(idx_copied, i * 4 + (t * 64 + g + 1))
                        pool.tensor_tensor(idx_guard, pair, zero_u, ALU.add)
                        for s in (2 * g, 2 * g + 1):
                            pool.indirect_dma_start(gring[:, s, :], None, A["experts"],
                                                    bass.IndirectOffsetOnAxis(ap=slot_idx[:, s:s + 1], axis=0)).then_inc(g_landed[s], 16)
            pool.wait_ge(sample_in, 16 * (NB + 2))
            for r in range(8):
                pool.wait_ge(g_used, NT * 64 + r // 2 + 1)
                pool.indirect_dma_start(gring[:, r, :], None, A["experts"],
                                        bass.IndirectOffsetOnAxis(ap=sidx[:, r:r + 1], axis=0)).then_inc(g_landed[r], 16)

        @block.scalar
        def _(act):
            c = Steps(act, act_steps)
            A_ = nc.scalar.activation
            for k in range(KD):
                act.wait_ge(x_landed[k // 4], 16)
                c.also(A_, qk[:, k], xT[:, k], ACT.Square, signal=sq_ready)
            act.wait_ge(consts_landed, 32)
            std_row = view("zs")[:, 0:T]
            for half, (a, b) in enumerate(HALVES):
                act.wait_ge(mean1, half + 1)
                c.also(A_, std_row[:, a:b], bank[6 + half][:, 0:HALF], ACT.Sqrt, bias=cst("eps"), signal=std1)

            def take(i):
                kind, j, half = items[i]
                act.wait_ge(proj_ready, i + 1)
                a, b = HALVES[half]
                src = bank[i % 6][:, 0:HALF]
                if kind == "qk":
                    c.also(A_, qk[:, j, a:b], src, ACT.Copy, signal=proj_taken)
                elif kind == "ab":
                    c.also(A_, abT[0:RANK, a:b], src[0:RANK], ACT.Copy, signal=proj_taken)
                elif kind == "qkb":
                    c.also(A_, qkb[:, j, a:b], src, ACT.Copy, scale=(GDK ** -0.5 if j < 2 else 1.0), signal=proj_taken)
                elif kind == "alpha":
                    c.also(A_, la[:, j, a:b], src, ACT.Identity, bias=vecs[:, V_BA + j:V_BA + j + 1], signal=proj_taken)
                elif kind in ("va", "vb"):
                    o = 0 if kind == "va" else 512
                    R = ROWS[j]
                    c.also(A_, vab[0:R, j, o:o + 512], bank[i % 6][0:R, :], ACT.Copy, signal=proj_taken)
                elif kind == "rb":
                    c.also(A_, srb[:, j, a:b], src, ACT.Silu, signal=proj_taken)
                else:
                    c.also(A_, gates[:, j, a:b], src, ACT.Sigmoid, bias=vecs[:, V_BG + j:V_BG + j + 1], signal=proj_taken)

            def squares(j):
                if j >= 2:
                    act.wait_ge(qkmean, 2 * (j - 1))
                for half, (a, b) in enumerate(HALVES):
                    if half == 0:
                        c.settle()
                    c.also(A_, qk_sq[:, j % 2, a:b], qk[:, j, a:b], ACT.Square, signal=qksq)

            def roots(j):
                if j in (2, 3, 7):
                    act.wait_ge(qk_done, {2: 1, 3: 2, 7: 3}[j])
                for half, (a, b) in enumerate(HALVES):
                    act.wait_ge(qkmean, 2 * j + half + 1)
                    c.also(A_, qk_std[:, STD_BUF[j], a:b], bank[6 + half][:, 0:HALF], ACT.Sqrt, bias=cst("eps"), signal=qkstd)

            act.wait_ge(xn_ready, KD)
            for j in range(8):
                take(2 * j)
                take(2 * j + 1)
                squares(j)
                if j >= 1:
                    roots(j - 1)
                if j == 5:
                    for b in range(NB):
                        act.wait_ge(qb_ready, b + 1)
                        c.also(A_, qbc[:, b], bank[6 + b % 2][:, :], ACT.Copy, signal=qb_taken)
            take(AB_ITEM)
            take(AB_ITEM + 1)
            roots(7)
            def sample_logs(q):
                act.wait_ge(zb_ready, q + 1)
                c.then(A_, part_l, part_l, ACT.Exp, scale=-1.0)
                c.then(A_, part_l, part_l, ACT.Ln, bias=1.0, signal=dec_l)

            def sample_weights(q):
                act.wait_ge(dec_arg, q + 1)
                c.also(A_, zs[:, 512 * q:512 * q + 512], zs[:, 512 * q:512 * q + 512], ACT.Exp, signal=dec_w)

            for i in range(AB_ITEM + 2, N_ITEMS):
                if i == RB_ITEM:
                    sample_logs(0)
                elif i == GATE_ITEM + 2 * 5:
                    sample_logs(1)
                elif i == GATE_ITEM + 2 * 12:
                    sample_weights(0)
                take(i)
            sample_weights(1)
            sample_logs(2)
            sample_weights(2)
            sample_logs(3)
            sample_weights(3)

            def take_v(b):
                act.wait_ge(v_done, b + 1)
                c.also(A_, v_cols[:, :, b], bank[V_BANK[b]][:, 0:4], ACT.Copy, signal=v_taken)

            act.wait_ge(la_in, 1)
            c.then(A_, tmp[:, 4128:4128 + 2 * T], tmp[:, 4128:4128 + 2 * T], ACT.Exp, scale=-1.0)
            c.then(A_, tmp[:, 4128:4128 + 2 * T], tmp[:, 4128:4128 + 2 * T], ACT.Ln, bias=1.0, signal=la_ready)
            act.wait_ge(gla_d, 1)
            flat = lambda x: x.rearrange("p m t -> p (m t)")
            c.also(A_, flat(qe), flat(cum), ACT.Exp, scale=1.0 / TAU, signal=gla_e)
            c.also(A_, flat(qt), tmp[:, 0:1024], ACT.Exp, scale=1.0 / TAU, signal=gla_e)
            c.also(A_, flat(kt), tmp[:, 0:1024], ACT.Exp, scale=-1.0 / TAU, signal=gla_e)
            c.also(A_, flat(kd), tmp[:, 1024:2048], ACT.Exp, scale=1.0 / TAU, signal=gla_e)
            c.also(A_, sample_decay, la[:, :, SEQ:T], ACT.Exp, scale=1.0 / TAU, signal=gla_e)
            for b in range(3):
                take_v(b)
            for m in range(2):
                act.wait_ge(kd_tr, m + 1)
                c.also(A_, kdr[:, :, m, :], bank[m].rearrange("p (t c) -> p t c", t=NT), ACT.Copy, signal=kd_rows)
            for u in range(2):
                for par in range(2):
                    act.wait_ge(o_ready, 2 * u + par + 1)
                    src = bank[2 + par].rearrange("p (tt m c) -> p m tt c", tt=2, m=2)
                    dst = ob[:, :, 256 * u:256 * u + 256].rearrange("p (m par) (tt c) -> p par m tt c", par=2, tt=2)[:, par]
                    c.also(A_, dst, src, ACT.Copy, signal=o_taken)
            take_v(3)
            for par in range(2):
                act.wait_ge(so_ready, par + 1)
                src = bank[7 if par == 0 else 1][:, 0:16].rearrange("p (m b) -> p m b", m=2)
                dst = ob[:, :, SEQ:T].rearrange("p (m par) b -> p par m b", par=2)[:, par]
                c.also(A_, dst, src, ACT.Copy, signal=o_taken)
            act.wait_ge(ss_ready, 1)
            for h in range(GH):
                c.settle()
                if h >= 2:
                    act.wait_ge(ob_mean, 2 * (h - 1))
                c.also(A_, ob_tmp[:, h % 2], ob[:, h], ACT.Square, signal=ob_sq)
                if h >= 1:
                    act.wait_ge(yb_ready, h)
                for half, (a, b) in enumerate(HALVES):
                    act.wait_ge(ob_mean, 2 * h + half + 1)
                    c.also(A_, ob_tmp[:, 2, a:b], bank[4 + half][:, 0:HALF], ACT.Sqrt, bias=cst("eps"), signal=ob_std)

            act.wait_ge(yb_ready, GH)
            for h in range(H):
                if h in FOLD_AT:
                    take_v(FOLD_AT[h])
                bias_h = bias_row[:, h:h + 1]
                if h >= 1:
                    act.wait_ge(att_sp, h)
                at = 0
                for n in range(NT):
                    w = SEQ - P * n
                    act.wait_ge(z_ready, NT * h + n + 1)
                    c.also(A_, tmp[:, at:at + w], bank[n][:, 0:w], ACT.Identity, bias=bias_h, signal=att_l)
                    at += w
                act.wait_ge(att_r, h + 1)
                c.then(A_, tmp[:, 1280:2560], tmp[:, 1280:2560], ACT.Exp, scale=-1.0)
                c.then(A_, tmp[:, 1280:2560], tmp[:, 1280:2560], ACT.Ln, bias=1.0, signal=att_l)
                at = 0
                for n in range(NT):
                    w = SEQ - P * n
                    act.wait_ge(acc_ready, NT * h + n + 1)
                    c.also(A_, tmp[:, 3840 + at:3840 + at + w], bank[n][:, 0:w], ACT.Exp, bias=bias_h, signal=att_w)
                    at += w
                if h % 2 == 1:
                    act.wait_ge(y_ready, h // 2 + 1)
                    c.also(A_, yaT[:, h // 2, 0:SEQ], bank[4 + h // 2 % 2][:, :], ACT.Copy, signal=y_taken)
            take_v(NB - 1)
            c.settle()
            c.also(A_, yaT[:, :, SEQ:T], v_cols, ACT.Copy, signal=y_taken)

            act.wait_ge(second_landed, 32)
            for t in range(5):
                R = ROWS[t]
                act.wait_ge(wo_taken, 5 + t + 1)
                c.settle()
                c.also(A_, view("onehot")[0:R, 0:D], h1[0:R, t], ACT.Square, accum_out=ssq[0:R, t:t + 1])
                c.then(A_, ssq[0:R, 5 + t:6 + t], ssq[0:R, t:t + 1], ACT.Sqrt, bias=cst("eps")[0:R], scale=1.0 / D, signal=h_std)
            for t in range(5):
                for k2 in range(2 if t < NT else 1):
                    n = 2 * t + k2
                    act.wait_ge(x2t_ready, n + 1)
                    if t < NT:
                        c.also(A_, xn2T[:, 4 * k2:4 * k2 + 4, t * P:t * P + P],
                               bank[2 + n % 6].rearrange("p (k c) -> p k c", k=4), ACT.Copy, signal=x2t_taken)
                    else:
                        c.also(A_, xn2T[:, :, SEQ:T], bank[2 + n % 6][:, 0:64].rearrange("p (k c) -> p k c", k=8),
                               ACT.Copy, signal=x2t_taken)

            def take_scores(j):
                act.wait_ge(s_ready, 2 * j + 1)
                c.also(A_, s_all[:, 0:NT, j, :], bank[4 + j % 2].rearrange("p (t n) -> p t n", t=NT), ACT.Copy, signal=s_taken)
                act.wait_ge(s_ready, 2 * j + 2)
                c.also(A_, s_all[0:NB, NT, j, :], bank[6 + j % 2][0:NB, 0:P], ACT.Copy, signal=s_taken)

            for j in range(16):
                if j >= 2:
                    act.wait_ge(s_ready, 2 * (j - 1))
                for half, (a, b) in enumerate(HALVES):
                    act.wait_ge(pq_ready, 2 * j + half + 1)
                    c.also(A_, qp[:, j % 2, a:b], bank[(2 * j + half) % 4][:, 0:HALF], ACT.Copy, signal=pq_taken)
                if j >= 1:
                    take_scores(j - 1)
            take_scores(15)

            def softmax_exp(t):
                act.wait_ge(soft_in, t + 1)
                c.also(A_, top[0:ROWS[t], 1], top[0:ROWS[t], 1], ACT.Exp, signal=soft_e)

            def h2_root(t):
                R = ROWS[t]
                act.wait_ge(h2_ready, t + 1)
                if 1 <= t < NT:
                    act.wait_ge(y_out, t)
                c.also(A_, end_buffers(t)[0][0:R], h1[0:R, t], ACT.Square, accum_out=ssq[0:R, t:t + 1])
                c.then(A_, ssq[0:R, 5 + t:6 + t], ssq[0:R, t:t + 1], ACT.Sqrt, bias=cst("eps")[0:R], scale=1.0 / D, signal=h3_std)

            def x3_columns(t):
                R = ROWS[t]
                _, columns, banks, _ = end_buffers(t)
                for c2 in range(2):
                    act.wait_ge(x3t_ready, 2 * t + c2 + 1)
                    c.also(A_, columns[:, 4 * c2:4 * c2 + 4, 0:R],
                           bank[banks[c2]][:, 0:4 * R].rearrange("p (k c) -> p k c", k=4), ACT.Copy, signal=x3t_taken)

            def ple_sigmoid(t):
                R = ROWS[t]
                rows, _, _, banks = end_buffers(t)
                c.settle()
                for c2 in range(2):
                    act.wait_ge(ple_ready, 4 * t + c2 + 1)
                    c.also(A_, rows[0:R, 512 * c2:512 * c2 + 512], bank[banks[c2]][0:R, :], ACT.Sigmoid, signal=ple_sig)

            softmax_exp(0)
            for t in range(NT):
                for k in range(SEGMENTS):
                    if t >= 1 and k == 1:
                        h2_root(t - 1)
                    elif t >= 1 and k == 3:
                        x3_columns(t - 1)
                    elif k == 5:
                        softmax_exp(t + 1)
                    elif t >= 1 and k == 6:
                        ple_sigmoid(t - 1)
                    with act.Fori(k * SEG, (k + 1) * SEG) as i:
                        for g in range(4):
                            pair = slice(2 * g, 2 * g + 2)
                            act.wait_ge(dots, i * 4 + (t * 64 + g + 1))
                            A_(act_g[:, pair], dot[:, pair], ACT.Gelu).then_inc(gel, 1)
                            act.wait_ge(gated, i * 4 + (t * 64 + g + 1))
                            act.wait_ge(g_used, i * 4 + (t * 64 + g + 1))
                            A_(diag[:, 2 * g], ident, ACT.Copy, scale=coef[:, 2 * g:2 * g + 1])
                            A_(diag[:, 2 * g + 1], ident, ACT.Copy, scale=coef[:, 2 * g + 1:2 * g + 2]).then_inc(diag_ready, 1)
            h2_root(NT - 1)
            x3_columns(NT - 1)
            act.wait_ge(dots, NT * 64 + 1)
            c.also(A_, act_g, dot, ACT.Gelu, signal=gel)
            act.wait_ge(gated, NT * 64 + 1)
            act.wait_ge(g_used, NT * 64 + 4)
            for r in range(8):
                c.also(A_, diag[:, r, 0:NB], cst("sample_of"), ACT.Copy, scale=coef[:, r:r + 1], signal=diag_ready if r == 7 else None)
            h2_root(NT)
            x3_columns(NT)
            ple_sigmoid(NT - 1)
            ple_sigmoid(NT)

        @block.vector
        def _(dve):
            c = Steps(dve, dve_steps)
            V = nc.vector

            def absolute(out, x):
                return V.scalar_tensor_tensor(out=out, in0=x, scalar=-1.0, in1=x, op0=ALU.mult, op1=ALU.max)

            dve.wait_ge(consts_landed, 32)
            rstd = view("zs")[:, T:2 * T]
            std_row = view("zs")[:, 0:T]
            dve.wait_ge(std1, 2)
            c.also(V.reciprocal, rstd, std_row)
            c.settle()
            for k in range(KD):
                c.also(V.scalar_tensor_tensor, out=xn[:, k], in0=xT[:, k], scalar=vecs[:, V_G1 + k:V_G1 + k + 1], in1=rstd,
                       op0=ALU.mult, op1=ALU.mult, signal=xn_ready)
            c.also(V.tensor_scalar, vecs[:, V_QG:V_QG + 1], vecs[:, V_QG:V_QG + 1], HD ** -0.5, None, ALU.mult)

            def head_norm(j):
                gain = V_QG if j < 4 else V_KG
                dve.wait_ge(qkstd, 2 * (j + 1))
                std = qk_std[:, STD_BUF[j]]
                c.then(V.reciprocal, std, std)
                c.then(V.scalar_tensor_tensor, out=qk[:, j], in0=qk[:, j], scalar=vecs[:, gain:gain + 1], in1=std,
                       op0=ALU.mult, op1=ALU.mult, signal=qk_done)

            for j in range(4):
                head_norm(j)
            dve.wait_ge(qb_taken, NB)
            z4 = zs.rearrange("p (b h g) -> p b g h", b=NB, h=H)
            dve.sem_inc(k_free, RING_K)

            def sum_heads(b, g, s):
                V.tensor_reduce(z4[:, bass.ds(b, 1), bass.ds(g, 1), :].rearrange("p a c h -> p (a c h)"),
                                prod[:, s % PRODS].rearrange("p (h d) -> p h d", h=H), AX.X, ALU.add).then_inc(k_free, 1)

            def k_pages(samples, rounds):
                begin = samples[0] == 0 and rounds[0] == 0
                with dve.Fori(*samples) as b:
                    with dve.Fori(*rounds) as g:
                        for s in range(RING_K):
                            n = b * PAGES + g * RING_K
                            dve.wait_ge(k_landed[s], b * (16 * PAGES // RING_K) + g * 16 + 16)
                            dve.wait_ge(k_free, n + (RING_K if begin and s == 0 else RING_K + s + 1 - PRODS))
                            if s:
                                dve.wait_ge(k_mul, n + s)
                            V.tensor_tensor(prod[:, s % PRODS], kring[:, s], qbc[:, bass.ds(b, 1), :].rearrange("p a n -> p (a n)"),
                                            ALU.mult).then_inc(k_mul, 1)
                            if s:
                                sum_heads(b, g * -RING_K + (PAGES - s), s - 1)
                        dve.wait_ge(k_mul, b * PAGES + g * RING_K + RING_K)
                        sum_heads(b, g * -RING_K + (PAGES - RING_K), RING_K - 1)

            def two_samples(q):
                return zs[:, 512 * q:512 * q + 512]

            def scores_bias(q):
                dve.wait_ge(k_free, RING_K + 2 * (q + 1) * PAGES)
                zb3 = two_samples(q).rearrange("p (b h g) -> p b h g", b=2, h=H)
                brow = bias_row.rearrange("p (b h g) -> p b h g", b=1, g=1).to_broadcast([P, 2, H, PAGES])
                c.also(V.tensor_tensor, zb3, zb3, brow, ALU.add)
                c.then(absolute, part_l, two_samples(q), signal=zb_ready)

            def scores_softplus(q):
                dve.wait_ge(dec_l, q + 1)
                if q >= 1:
                    dve.wait_ge(dec_z, q)
                c.also(V.scalar_tensor_tensor, out=part_sp, in0=two_samples(q), scalar=0.0, in1=part_l, op0=ALU.max, op1=ALU.add)
                c.then(V.tensor_tensor_scan, part_sum, cst("page_reset"), part_sp, 0.0, ALU.mult, ALU.add, signal=dec_sp)

            def scores_argument(q):
                dve.wait_ge(dec_z, q + 1)
                c.also(V.tensor_tensor, two_samples(q), two_samples(q), bank[KEYS_BANK[q]][:, :], ALU.add, signal=dec_arg)

            k_pages((0, 1), (0, 4))
            for j in range(4, 8):
                head_norm(j)
            c.settle()
            dve.sem_inc(v_free, RING_V)
            dve.wait_ge(wab_landed, 48)
            k_pages((1, 2), (0, 4))
            scores_bias(0)
            k_pages((2, 3), (0, 4))
            scores_softplus(0)
            k_pages((3, 4), (0, 4))
            scores_argument(0)
            scores_bias(1)
            k_pages((4, 5), (0, 4))
            scores_softplus(1)
            k_pages((5, 6), (0, 4))
            scores_argument(1)
            scores_bias(2)
            k_pages((6, 7), (0, 4))
            scores_softplus(2)
            k_pages((7, 8), (0, 4))
            scores_argument(2)
            scores_bias(3)
            scores_softplus(3)
            scores_argument(3)
            dve.wait_ge(proj_taken, N_ITEMS)

            def own_heads(b):
                dve.wait_ge(v_free, RING_V + (b + 1) * PAGES)
                if b >= 2:
                    dve.wait_ge(v_done, b - 1)
                own = ident[0:H, 0:H].rearrange("p (h o) -> p h o", o=1).to_broadcast([H, H, HD])
                by_head = lambda x: x.rearrange("p (h d) -> p h d", d=HD)
                c.also(V.tensor_tensor, by_head(v_own[b % 2]), by_head(bank[V_BANK[b]][0:H, :]), own, ALU.mult, signal=v_masked)

            laf = view("la")
            g_tmp = tmp[:, 4128:4128 + 2 * T]
            c.then(absolute, g_tmp, laf, signal=la_in)
            dve.wait_ge(la_ready, 1)
            c.also(V.scalar_tensor_tensor, out=laf, in0=laf, scalar=0.0, in1=g_tmp, op0=ALU.min, op1=ALU.subtract)
            c.settle()
            for m in range(2):
                c.also(V.tensor_tensor_scan, cum[:, m], cst("chunk_reset"), la[:, m, 0:SEQ], 0.0, ALU.mult, ALU.add)
            c.settle()
            ch = view("cum").rearrange("p (c i) -> p c i", i=CHUNK)
            t3 = lambda o: tmp[:, o:o + 1024].rearrange("p (c i) -> p c i", i=CHUNK)
            c.also(V.tensor_tensor, t3(0), ch, ch[:, :, CHUNK // 2 - 1:CHUNK // 2].to_broadcast([P, 2 * NCH, CHUNK]), ALU.subtract)
            c.also(V.tensor_tensor, t3(1024), ch[:, :, CHUNK - 1:CHUNK].to_broadcast([P, 2 * NCH, CHUNK]), ch, ALU.subtract, signal=gla_d)
            dve.wait_ge(gla_e, 5)
            c.also(V.tensor_copy, chunk_decay, view("qe").rearrange("p (c i) -> p c i", i=CHUNK)[:, :, CHUNK - 1])
            c.also(V.tensor_tensor, kd, kd, qkb[:, 2:4, 0:SEQ], ALU.mult, signal=gla_in)
            c.also(V.tensor_tensor, qt, qt, qkb[:, 0:2, 0:SEQ], ALU.mult)
            c.also(V.tensor_tensor, kt, kt, qkb[:, 2:4, 0:SEQ], ALU.mult, signal=gla_in)
            c.then(V.tensor_tensor, qe, qe, qkb[:, 0:2, 0:SEQ], ALU.mult)
            c.also(V.memset, states[:, 0], 0.0, signal=gla_in)
            for b in range(3):
                own_heads(b)
            mask4 = cst("gla_mask").rearrange("p (a c) -> p a c", a=1).to_broadcast([P, 4, P])
            for u in range(2):
                for par in range(2):
                    dve.wait_ge(sc_ready, 2 * u + par + 1)
                    c.also(V.tensor_tensor, sc_v[:, par], bank[2 + par].rearrange("p (a c) -> p a c", a=4), mask4, ALU.mult, signal=sc_done)
                dve.wait_ge(u_ready, u + 1)
                for ch4 in range(4):
                    cc = 4 * u + ch4
                    c.settle()
                    for m in range(2):
                        ub = (4 if u == 0 else 0) + cc % 2
                        ucol = (ch4 // 2 * 2 + m) * P
                        c.also(V.scalar_tensor_tensor, out=states[:, cc + 1, m], in0=states[:, cc, m],
                               scalar=chunk_decay[:, m * NCH + cc:m * NCH + cc + 1], in1=bank[ub][:, ucol:ucol + P],
                               op0=ALU.mult, op1=ALU.add, signal=states_done if (cc in (3, 7) and m == 1) else None)
            own_heads(3)
            dve.wait_ge(state_landed, 16)
            for b in range(NB):
                dve.wait_ge(vb_ready, b + 1)
                for par in range(2):
                    rows = slice(64 * par, 64 * par + 64)
                    v_b = bank[7].rearrange("p (m q e) -> p q m e", m=2, q=2)[rows, par]
                    k_b = qkb[rows, 2:4, SEQ + b:SEQ + b + 1].to_broadcast([64, 2, GDV])
                    c.also(V.tensor_tensor, kv[rows, b], v_b, k_b, ALU.mult, signal=vb_taken if par else None)
            dec = sample_decay.rearrange("p m (b o) -> p b m o", o=1).to_broadcast([P, NB, 2, GDV])
            c.then(V.tensor_tensor, sstate, sstate, dec, ALU.mult)
            c.then(V.tensor_tensor, sstate, sstate, kv, ALU.add, signal=ss_ready)
            for h in range(GH):
                dve.wait_ge(ob_std, 2 * (h + 1))
                c.then(V.reciprocal, ob_tmp[:, 2], ob_tmp[:, 2])
                c.also(V.scalar_tensor_tensor, out=srb[:, h], in0=ob[:, h], scalar=vecs[:, V_OG:V_OG + 1], in1=srb[:, h],
                       op0=ALU.mult, op1=ALU.mult)
                c.then(V.tensor_tensor, srb[:, h], srb[:, h], ob_tmp[:, 2], ALU.mult, signal=yb_ready)

            own_heads(4)
            for h in range(H):
                dve.wait_ge(att_l, 5 * h + 4)
                if h >= 1:
                    dve.wait_ge(acc_ready, NT * h)
                c.also(absolute, tmp[:, 1280:2560], tmp[:, 0:1280], signal=att_r)
                dve.wait_ge(att_l, 5 * h + 5)
                c.also(V.scalar_tensor_tensor, out=tmp[:, 2560:3840], in0=tmp[:, 0:1280], scalar=0.0, in1=tmp[:, 1280:2560],
                       op0=ALU.max, op1=ALU.add)
                at = 2560
                c.settle()
                for n in range(NT):
                    c.also(V.tensor_tensor, tmp[:, at:at + P], tmp[:, at:at + P], cst("keep_mask"), ALU.mult,
                           signal=att_sp if n == NT - 1 else None)
                    at += SEQ - P * n
                if h + 1 in FOLD_AT:
                    own_heads(FOLD_AT[h + 1])
            own_heads(NB - 1)

            for m in range(8):
                for q in range(4):
                    i = 4 * m + q
                    a, b = HALVES[q % 2]
                    dve.wait_ge(up_ready, i + 1)
                    gm = gates[:, (m if q < 2 else 8 + m), a:b]
                    c.also(V.tensor_tensor, gm, gm, bank[i % 8][:, 0:HALF], ALU.mult, signal=up_taken)
                c.then(V.tensor_tensor, gates[:, m], gates[:, m], gates[:, 8 + m], ALU.add, signal=mix_ready)
            dve.wait_ge(rows_landed, 32)
            for i in range(10):
                t, half = i % 5, i // 5
                R = ROWS[t]
                dve.wait_ge(wo_ready, i + 1)
                hh = h1[0:R, t, 512 * half:512 * half + 512]
                c.also(V.tensor_tensor, hh, hh, bank[i % 8][0:R, :], ALU.add, signal=wo_taken)
            dve.wait_ge(second_landed, 32)
            for t in range(5):
                R = ROWS[t]
                dve.wait_ge(h_std, t + 1)
                c.also(V.reciprocal, rstd2[0:R, t:t + 1], ssq[0:R, 5 + t:6 + t])
                c.then(V.scalar_tensor_tensor, out=xn2[0:R, t], in0=h1[0:R, t], scalar=rstd2[0:R, t:t + 1], in1=g2[0:R],
                       op0=ALU.mult, op1=ALU.mult, signal=xn2_ready)

            def two_best(values, best, where, done=None):
                for part in range(2):
                    pick = slice(8 * part, 8 * part + 8)
                    c.settle()
                    for x, v, w in zip(values, best, where):
                        c.also(V.max, v[:, pick], x)
                    c.settle()
                    for n, (x, v, w) in enumerate(zip(values, best, where)):
                        c.also(V.max_index, w[:, pick], v[:, pick], x, signal=done if part and n == len(values) - 1 else None)
                    if part == 0:
                        c.settle()
                        for x, v, w in zip(values, best, where):
                            c.also(V.match_replace, x, v[:, pick], x, LOWEST)

            FIRST_HALF, LAST_HALF, ALL = slice(0, PH // 2), slice(PH // 2, PH), slice(0, PH)

            def select_lists(t, heads):
                R = ROWS[t]
                s4 = v16[0:R, t].rearrange("p (h c) k -> p h c k", c=2)[:, heads]
                c4 = cand[0:R, heads].rearrange("p h (i j) -> p h i j", i=TOPK)
                wide = [R, heads.stop - heads.start, TOPK, TOPK]
                s1 = s4[:, :, 0].rearrange("p h (k o) -> p h k o", o=1).to_broadcast(wide)
                s2 = s4[:, :, 1].rearrange("p h (o k) -> p h o k", o=1).to_broadcast(wide)
                c.then(V.tensor_tensor, c4, s1, s2, ALU.add)

            def select_best(t, heads):
                R = ROWS[t]
                each = range(heads.start, heads.stop)
                two_best([cand[0:R, h] for h in each], [top[0:R, 0, h] for h in each], [top_u[0:R, 2, h] for h in each])
                c.settle()
                best = top[0:R, 0, heads, 0:1].to_broadcast([R, heads.stop - heads.start, TOPK])
                c.also(V.tensor_tensor, top[0:R, 1, heads], top[0:R, 0, heads], best, ALU.subtract, signal=soft_in if heads.stop == PH else None)
                c.also(V.tensor_scalar, top_u[0:R, 3, heads], top_u[0:R, 2, heads], 4, None, ALU.logical_shift_right)
                c.also(V.tensor_scalar, top_u[0:R, 4, heads], top_u[0:R, 2, heads], 15, None, ALU.bitwise_and)
                lists = slice(2 * heads.start, 2 * heads.stop)
                c.also(V.tensor_copy, i16f[0:R, lists], i16[0:R, t, lists])
                c.settle()
                for part in range(2):
                    c.also(V.tensor_copy, top[0:R, 5 + part, heads], top_u[0:R, 3 + part, heads])

            def select_keys(t, part, heads):
                R = ROWS[t]
                wide = [R, heads.stop - heads.start, TOPK, TOPK]
                hot = onehot[0:R, heads]
                iota = cst("iota16")[0:R].rearrange("p (a b j) -> p a b j", a=1, b=1).to_broadcast(wide)
                c.settle()
                place = top[0:R, 5 + part, heads].rearrange("p h (k o) -> p h k o", o=1).to_broadcast(wide)
                keys = i16f[0:R].rearrange("p (h c) (o k) -> p h c o k", c=2, o=1)[:, heads, part].to_broadcast(wide)
                c.also(V.tensor_tensor, hot, place, iota, ALU.is_equal)
                c.then(V.tensor_tensor, hot, hot, keys, ALU.mult)
                c.then(V.tensor_reduce, top[0:R, 7 + part, heads], hot, AX.X, ALU.add)

            def select_end(t):
                R = ROWS[t]
                c.settle()
                flat = lambda x: x.rearrange("p h k -> p (h k)")
                c.also(V.scalar_tensor_tensor, out=expert[0:R, t], in0=flat(top[0:R, 7]), scalar=float(NKEYS), in1=flat(top[0:R, 8]),
                       op0=ALU.mult, op1=ALU.add)
                dve.wait_ge(soft_e, t + 1)
                c.also(V.tensor_reduce, den[0:R], top[0:R, 1], AX.X, ALU.add)
                c.then(V.reciprocal, den[0:R], den[0:R])
                c.then(V.tensor_tensor, gate[0:R, t].rearrange("p (h k) -> p h k", h=PH), top[0:R, 1],
                       den[0:R].rearrange("p (h o) -> p h o", o=1).to_broadcast([R, PH, TOPK]), ALU.mult, signal=sel_ready)

            for j in range(16):
                dve.wait_ge(s_taken, 2 * (j + 1))
                two_best([s_all[:, t, j] for t in range(NT)], [v16[:, t, j] for t in range(NT)], [i16[:, t, j] for t in range(NT)],
                         done=topk_done if j == 15 else None)
                if j in (4, 8, 12, 15):
                    heads = slice((j - 3) // 2 // 2 * 2, (j - 3) // 2 // 2 * 2 + 2)
                    select_lists(0, heads)
                    select_best(0, heads)
                    select_keys(0, 0, heads)
                    select_keys(0, 1, heads)

            def residual(t):
                R = ROWS[t]
                dve.wait_ge(y_sum, t + 1)
                c.settle()
                for c2 in range(2):
                    hh = h1[0:R, t, 512 * c2:512 * c2 + 512]
                    c.also(V.tensor_tensor, hh, hh, bank[Y_BANKS[t % 2][c2]][0:R, :], ALU.add, signal=h2_ready if c2 else None)

            def third_norm(t):
                R = ROWS[t]
                dve.wait_ge(h3_std, t + 1)
                c.also(V.reciprocal, rstd2[0:R, 5:6], ssq[0:R, 5 + t:6 + t])
                c.then(V.scalar_tensor_tensor, out=xn2[0:R, t], in0=h1[0:R, t], scalar=rstd2[0:R, 5:6], in1=g3[0:R],
                       op0=ALU.mult, op1=ALU.mult, signal=xn3_ready)

            def embed(t):
                R = ROWS[t]
                rows, _, banks, _ = end_buffers(t)
                dve.wait_ge(ple_sig, 2 * (t + 1))
                for c2 in range(2):
                    dve.wait_ge(ple_ready, 4 * t + 3 + c2)
                    ff = rows[0:R, 512 * c2:512 * c2 + 512]
                    c.also(V.tensor_tensor, ff, ff, bank[banks[c2]][0:R, :], ALU.mult)
                c.then(V.tensor_tensor, h1[0:R, t], h1[0:R, t], rows[0:R], ALU.add, signal=y_out)

            dve.sem_inc(g_used, 4)
            select_end(0)
            dve.wait_ge(late_landed, 64)
            for t in range(NT):
                for k in range(SEGMENTS):
                    if k == 1 and t == 0:
                        dve.wait_ge(scores_in, 16)
                        two_best([s_list], [v_list], [i_list], done=list_best)
                    elif k == 1:
                        residual(t - 1)
                    elif k == 2:
                        if t >= 1:
                            third_norm(t - 1)
                        if t + 1 == NT:
                            dve.wait_ge(best_in, 32)
                        select_lists(t + 1, ALL)
                    elif k == 3:
                        select_best(t + 1, FIRST_HALF)
                    elif k == 4:
                        select_best(t + 1, LAST_HALF)
                    elif k == 5:
                        select_keys(t + 1, 0, ALL)
                    elif k == 6:
                        select_keys(t + 1, 1, ALL)
                        select_end(t + 1)
                    elif k == 7 and t >= 1:
                        embed(t - 1)
                    c.settle()
                    with dve.Fori(k * SEG, (k + 1) * SEG) as i:
                        for g in range(4):
                            for s in (2 * g, 2 * g + 1):
                                dve.wait_ge(g_landed[s], i * 16 + (t * 256 + 16))
                                last = V.tensor_tensor_reduce(gring[:, s, 0:D], gring[:, s, 0:D], xn2[:, t], 1.0, 0.0,
                                                              ALU.mult, ALU.add, dot[:, s:s + 1])
                            last.then_inc(dots, 1)
                            dve.wait_ge(gel, i * 4 + (t * 64 + g + 1))
                            V.tensor_tensor(coef[:, 2 * g:2 * g + 2], act_g[:, 2 * g:2 * g + 2], gate[:, t, bass.ds(i * 8 + 2 * g, 2)],
                                            ALU.mult).then_inc(gated, 1)
            residual(NT - 1)
            third_norm(NT - 1)
            dve.wait_ge(sample_in, 16 * (NB + 2))
            for r in range(8):
                dve.wait_ge(g_landed[r], 16 * (NT * SEL // RING_G + 1))
                c.also(V.tensor_tensor_reduce, gring[:, r, 0:D], gring[:, r, 0:D], sx, 1.0, 0.0, ALU.mult, ALU.add, dot[:, r:r + 1],
                       signal=dots if r == 7 else None)
            dve.wait_ge(gel, NT * 64 + 1)
            c.also(V.tensor_tensor, coef, act_g, sgate, ALU.mult, signal=gated)
            residual(NT)
            third_norm(NT)
            embed(NT - 1)
            embed(NT)

        @block.tensor
        def _(pe):
            mm, tr = nc.tensor.matmul, nc.tensor.transpose
            pe.wait_ge(consts_landed, 32)
            mean = cst("mean_model")
            for half, (a, b) in enumerate(HALVES):
                for k in range(KD):
                    pe.wait_ge(sq_ready, k + 1)
                    last = mm(bank[6 + half][:, 0:HALF], mean, qk[:, k, a:b], start=(k == 0), stop=(k == KD - 1))
                last.then_inc(mean1, 1)

            def weights(s):
                pe.wait_ge(w_in_slot[s % RING_W], 16 * (s // RING_W + 1))
                return wring[:, s % RING_W]

            def item(i):
                if i >= 6:
                    pe.wait_ge(proj_taken, i - 5)
                return bank[i % 6]

            made_items = [0]

            def project(s):
                w = weights(s).rearrange("p (k c) -> p k c", k=KD)
                for a, b in HALVES:
                    out = item(made_items[0])[:, 0:HALF]
                    made_items[0] += 1
                    for k in range(KD):
                        if s == 0 and a == 0:
                            pe.wait_ge(xn_ready, k + 1)
                        last = mm(out, w[:, k], xn[:, k, a:b], start=(k == 0), stop=(k == KD - 1))
                    last.then_inc(proj_ready, 1)

            def head_means(j):
                pe.wait_ge(qksq, 2 * (j + 1))
                if j >= 1:
                    pe.wait_ge(qkstd, 2 * j)
                for half, (a, b) in enumerate(HALVES):
                    mm(bank[6 + half][:, 0:HALF], cst("mean_head"), qk_sq[:, j % 2, a:b], start=True, stop=True).then_inc(qkmean, 1)

            for j in range(8):
                project(S_QA + j)
                if j >= 1:
                    head_means(j - 1)
                if j == 5:
                    pe.wait_ge(qk_done, 4)
                    pe.wait_ge(qkstd, 10)
                    for b in range(NB):
                        if b >= 2:
                            pe.wait_ge(qb_taken, b - 1)
                        for m in range(4):
                            last = mm(bank[6 + b % 2][:, m * P:m * P + P], qk[:, m, SEQ + b:SEQ + b + 1].to_broadcast([P, P]), ident,
                                      start=True, stop=True)
                        last.then_inc(qb_ready, 1)
                    pe.wait_ge(qb_taken, NB)
            pe.wait_ge(wab_landed, 48)
            for a, b in HALVES:
                out = item(made_items[0])[0:RANK, 0:HALF]
                made_items[0] += 1
                for k in range(KD):
                    last = mm(out, abw[:, k], xn[:, k, a:b], start=(k == 0), stop=(k == KD - 1))
                last.then_inc(proj_ready, 1)
            head_means(7)
            for j in range(4):
                project(S_QB + j)
            pe.wait_ge(proj_taken, AB_ITEM + 2)
            for m in range(2):
                for a, b in HALVES:
                    mm(item(made_items[0])[:, 0:HALF], alw[:, m * P:m * P + P], abT[0:RANK, a:b], start=True, stop=True).then_inc(proj_ready, 1)
                    made_items[0] += 1
            for s0 in (S_VA, S_VB):
                for q in range(4):
                    w = weights(s0 + q).rearrange("p (k c) -> p k c", k=2)
                    for t in range(5):
                        out = (item(made_items[0] + t) if q == 0 else bank[(made_items[0] + t) % 6])[0:ROWS[t], :]
                        for kk in range(2):
                            k = 2 * q + kk
                            last = mm(out, xn[:, k, t * P:t * P + ROWS[t]], w[:, kk], start=(k == 0), stop=(k == KD - 1))
                        if q == 3:
                            last.then_inc(proj_ready, 1)
                    if q < 3:
                        last.then_inc(kstep, 1)
                made_items[0] += 5
            def later_keys(q):
                pe.wait_ge(dec_sp, q + 1)
                late = lambda x: x.rearrange("p (r g) -> p r g", g=PAGES)
                out = bank[KEYS_BANK[q]][:, :]
                mm(out, cst("neg_tri"), part_sp, start=True, stop=True)
                mm(late(out)[:, :, 1:PAGES], cst("neg_ones"), late(part_sum)[:, :, 0:PAGES - 1],
                   start=False, stop=True, skip_group_check=True).then_inc(dec_z, 1)

            for j in range(4):
                project(S_RB + j)
            for j in range(16):
                if j == 1:
                    later_keys(0)
                elif j == 11:
                    later_keys(1)
                project(S_GA + j)

            w4 = zs.rearrange("p (b h g) -> p b g h", b=NB, h=H)
            zrow = cst("zeros")[:, 0:1].to_broadcast([P, 512])
            rounds = PAGES // RING_V

            def v_rounds(b, first, end):
                out = bank[V_BANK[b]][0:H, :]
                if first == 0:
                    if b >= 4:
                        pe.wait_ge(v_taken, max(b - 1, 4))
                    mm(out, cst("zeros"), zrow, start=True, stop=True)
                for g in range(first, end):
                    for s in range(RING_V):
                        if b < V_EARLY:
                            pe.wait_ge(v_early[s], 16 * (b * rounds + g + 1))
                        else:
                            pe.wait_ge(v_landed[s], 16 * ((b - V_EARLY) * rounds + g + 1))
                        mm(out, w4[:, b, PAGES - 1 - g * RING_V - s], vring[:, s],
                           start=False, stop=True, skip_group_check=True).then_inc(v_free, 1)

            def v_fold(b):
                pe.wait_ge(v_masked, b + 1)
                for m in range(4):
                    last = mm(bank[V_BANK[b]][:, m:m + 1], v_own[b % 2][:, m * P:m * P + P], cst("one")[0:H], start=True, stop=True)
                last.then_inc(v_done, 1)

            pe.wait_ge(proj_taken, N_ITEMS)
            pe.wait_ge(dec_w, 1)
            v_rounds(0, 0, 4)
            later_keys(2)
            v_rounds(1, 0, 4)
            pe.wait_ge(dec_w, 2)
            v_rounds(2, 0, 2)
            later_keys(3)
            v_rounds(2, 2, 4)
            pe.wait_ge(dec_arg, 4)
            pe.wait_ge(gla_in, 1)
            for m in range(2):
                for t in range(NT):
                    last = tr(bank[m][:, t * P:t * P + P], kd[:, m, t * P:t * P + P], ident)
                last.then_inc(kd_tr, 1)
            for b in range(3):
                v_fold(b)
            v_rounds(3, 0, 1)
            pe.wait_ge(v_taken, 3)
            pe.wait_ge(gla_in, 3)
            qrow = lambda par: slice(64 * par, 64 * par + 64)
            for u in range(2):
                if u == 1:
                    pe.wait_ge(o_taken, 2)
                for par in range(2):
                    for tt in range(2):
                        for m in range(2):
                            t = slice((2 * u + tt) * P, (2 * u + tt) * P + P)
                            last = mm(bank[2 + par][:, (2 * tt + m) * P:(2 * tt + m) * P + P], kt[qrow(par), m, t], qt[qrow(par), m, t],
                                      start=True, stop=True)
                    last.then_inc(sc_ready, 1)
                if u == 0:
                    v_rounds(3, 1, 2)
                pe.wait_ge(kd_rows, 2)
                for c2 in range(2):
                    for tt in range(2):
                        for m in range(2):
                            for par in range(2):
                                t = 2 * u + tt
                                h = 2 * m + par
                                rows = qrow(c2)
                                last = mm(bank[(4 if u == 0 else 0) + c2][qrow(par), (2 * tt + m) * P:(2 * tt + m) * P + P],
                                          kdr[rows, t, m, 64 * par:64 * par + 64], vab[rows, t, 512 + h * P:512 + h * P + P],
                                          start=True, stop=True)
                last.then_inc(u_ready, 1)
                v_rounds(3, u + 2, u + 3)
                pe.wait_ge(sc_done, 2 * u + 2)
                pe.wait_ge(states_done, u + 1)
                for par in range(2):
                    for tt in range(2):
                        for m in range(2):
                            t, h, col = 2 * u + tt, 2 * m + par, (2 * tt + m) * P
                            mm(bank[2 + par][:, col:col + P], vab[:, t, 512 + h * P:512 + h * P + P], sc_v[:, par, 2 * tt + m],
                               start=True, stop=True)
                            for c2 in range(2):
                                last = mm(bank[2 + par][:, col + 64 * c2:col + 64 * c2 + 64], states[qrow(par), 2 * t + c2, m],
                                          qe[qrow(par), m, t * P + 64 * c2:t * P + 64 * c2 + 64], start=False, stop=True,
                                          skip_group_check=True)
                    last.then_inc(o_ready, 1)
            for b in range(NB):
                if b >= 1:
                    pe.wait_ge(vb_taken, b)
                mm(bank[7][:, :], ident[0:NB, b:b + 1].to_broadcast([NB, P]), vab[0:NB, NT, 512:1024], start=True, stop=True).then_inc(vb_ready, 1)
            v_fold(3)
            pe.wait_ge(dec_w, 4)
            v_rounds(4, 0, 1)
            pe.wait_ge(ss_ready, 1)
            for par in range(2):
                for m in range(2):
                    for b in range(NB):
                        last = mm(bank[7 if par == 0 else 1][:, m * NB + b:m * NB + b + 1], sstate[qrow(par), b, m],
                                  qkb[qrow(par), m, SEQ + b:SEQ + b + 1], start=True, stop=True)
                last.then_inc(so_ready, 1)
            for h in range(GH):
                pe.wait_ge(ob_sq, h + 1)
                if h >= 1:
                    pe.wait_ge(ob_std, 2 * h)
                for half, (a, b) in enumerate(HALVES):
                    mm(bank[4 + half][:, 0:HALF], cst("mean_gdv"), ob_tmp[:, h % 2, a:b], start=True, stop=True).then_inc(ob_mean, 1)
                if h < GH - 1:
                    v_rounds(4, h + 1, h + 2)

            def v_round(r):
                v_rounds(5 + r // rounds, r % rounds, r % rounds + 1)

            pe.wait_ge(yb_ready, GH)
            for h in range(H):
                m, rows = h // 2, qrow(h % 2)
                if h >= 1:
                    pe.wait_ge(att_w, NT * h)
                if h in FOLD_AT:
                    v_fold(FOLD_AT[h])
                for n in range(NT):
                    mm(bank[n][:, 0:SEQ - P * n], qk[rows, 4 + m, n * P:n * P + P], qk[rows, m, n * P:SEQ],
                       start=True, stop=True).then_inc(z_ready, 1)
                v_round(h + h // 2)
                pe.wait_ge(att_sp, h + 1)
                at = [2560, 3072, 3456, 3712]
                for n in range(NT):
                    w = SEQ - P * n
                    mm(bank[n][:, 0:w], cst("neg_tri"), tmp[:, at[n]:at[n] + w], start=False, stop=True, skip_group_check=True)
                    for k2 in range(n + 1, NT):
                        mm(bank[n][:, P * (k2 - n):w], cst("neg_ones"), tmp[:, at[k2]:at[k2] + SEQ - P * k2],
                           start=False, stop=True, skip_group_check=True)
                    mm(bank[n][:, 0:P], ident, cst("neg_mask"), start=False, stop=True, skip_group_check=True).then_inc(acc_ready, 1)
                if h % 2 == 1:
                    v_round(h + h // 2 + 1)
                if m >= 2:
                    pe.wait_ge(y_taken, m - 1)
                for n in range(NT):
                    pe.wait_ge(att_w, NT * h + n + 1)
                    last = mm(bank[4 + m % 2][rows, P * n:SEQ], vab[:, n, h * HD:h * HD + HD], tmp[:, at[n] + 1280:at[n] + 1280 + SEQ - P * n],
                              start=(n == 0), stop=(n == NT - 1), skip_group_check=True)
                if h % 2 == 1:
                    last.then_inc(y_ready, 1)
            v_fold(NB - 1)

            pe.wait_ge(y_taken, 5)
            for m in range(8):
                w = weights(S_UP + m).rearrange("p (u k c) -> p u k c", u=2, k=4)
                for q in range(4):
                    i = 4 * m + q
                    a, b = HALVES[q % 2]
                    if i >= 8:
                        pe.wait_ge(up_taken, i - 7)
                    src = yaT if q < 2 else srb
                    for k in range(4):
                        last = mm(bank[i % 8][:, 0:HALF], w[:, q // 2, k], src[:, k, a:b], start=(k == 0), stop=(k == 3))
                    last.then_inc(up_ready, 1)
            pe.wait_ge(mix_ready, 8)
            for half in range(2):
                for q in range(4):
                    w = weights(S_WO + 4 * half + q).rearrange("p (k c) -> p k c", k=2)
                    for t in range(5):
                        i = 5 * half + t
                        if q == 0 and i >= 8:
                            pe.wait_ge(wo_taken, i - 7)
                        for kk in range(2):
                            k = 2 * q + kk
                            last = mm(bank[i % 8][0:ROWS[t], :], mixT[:, k, t * P:t * P + ROWS[t]], w[:, kk], start=(k == 0), stop=(k == KD - 1))
                        if q == 3:
                            last.then_inc(wo_ready, 1)
                    if q < 3:
                        last.then_inc(kstep, 1)

            pe.wait_ge(wo_taken, 10)
            for t in range(5):
                R = ROWS[t]
                pe.wait_ge(xn2_ready, t + 1)
                for k in range(KD):
                    n = 2 * t + (k // 4 if t < NT else 0)
                    if k % 4 == 0 and n >= 6:
                        pe.wait_ge(x2t_taken, n - 5)
                    col = (k % 4) * P if t < NT else k * NB
                    last = tr(bank[2 + n % 6][:, col:col + R], xn2[0:R, t, k * P:k * P + P], ident[0:R, 0:R])
                    if k == KD - 1 or (k == 3 and t < NT):
                        last.then_inc(x2t_ready, 1)

            def scores(j):
                pe.wait_ge(pq_taken, 2 * (j + 1))
                if j >= 2:
                    pe.wait_ge(s_taken, 2 * (j - 1))
                for t in range(NT):
                    last = mm(bank[4 + j % 2][:, t * P:t * P + P], qp[:, j % 2, t * P:t * P + P], sk[:, j], start=True, stop=True)
                last.then_inc(s_ready, 1)
                mm(bank[6 + j % 2][0:NB, 0:P], qp[:, j % 2, SEQ:T], sk[:, j], start=True, stop=True).then_inc(s_ready, 1)

            pe.wait_ge(x2t_taken, 9)
            for j in range(16):
                w = weights(S_PQ + j).rearrange("p (k c) -> p k c", k=KD)
                for half, (a, b) in enumerate(HALVES):
                    i = 2 * j + half
                    if i >= 4:
                        pe.wait_ge(pq_taken, i - 3)
                    for k in range(KD):
                        last = mm(bank[i % 4][:, 0:HALF], w[:, k], xn2T[:, k, a:b], start=(k == 0), stop=(k == KD - 1))
                    last.then_inc(pq_ready, 1)
                if j >= 1:
                    scores(j - 1)
            scores(15)

            pe.wait_ge(s_taken, 32)
            pe.wait_ge(late_landed, 64)

            def x3_columns(t):
                R = ROWS[t]
                banks = end_buffers(t)[2]
                pe.wait_ge(xn3_ready, t + 1)
                if 1 <= t < NT:
                    pe.wait_ge(y_out, t)
                for k in range(KD):
                    last = tr(bank[banks[k // 4]][:, (k % 4) * R:(k % 4) * R + R], xn2[0:R, t, k * P:k * P + P], ident[0:R, 0:R])
                    if k % 4 == 3:
                        last.then_inc(x3t_ready, 1)

            def ple_gate(t, c2):
                R = ROWS[t]
                _, columns, _, banks = end_buffers(t)
                pe.wait_ge(x3t_taken, 2 * (t + 1))
                for k in range(KD):
                    last = mm(bank[banks[c2]][0:R, :], columns[:, k, 0:R], wpg[:, k, 512 * c2:512 * c2 + 512], start=(k == 0), stop=(k == KD - 1))
                last.then_inc(ple_ready, 1)

            def ple_embedding(t):
                R = ROWS[t]
                banks = end_buffers(t)[2]
                for c2 in range(2):
                    for k in range(2):
                        last = mm(bank[banks[c2]][0:R, :], pT[:, k, t * P:t * P + R], ple_w[:, k, 512 * c2:512 * c2 + 512], start=(k == 0), stop=(k == 1))
                    last.then_inc(ple_ready, 1)

            for t in range(NT):
                yb = Y_BANKS[t % 2]
                if t >= 2:
                    pe.wait_ge(h2_ready, t - 1)
                for c2 in range(2):
                    mm(bank[yb[c2]][:, :], ident, zrow, start=True, stop=True, skip_group_check=True)
                for k in range(SEGMENTS):
                    if t >= 1 and k == 3:
                        x3_columns(t - 1)
                    elif t >= 1 and k == 4:
                        ple_gate(t - 1, 0)
                    elif t >= 1 and k == 5:
                        ple_gate(t - 1, 1)
                    elif t >= 1 and k == 6:
                        ple_embedding(t - 1)
                    with pe.Fori(k * SEG, (k + 1) * SEG) as i:
                        for g in range(4):
                            pe.wait_ge(diag_ready, i * 4 + (t * 64 + g + 1))
                            for s in (2 * g, 2 * g + 1):
                                for c2 in range(2):
                                    last = mm(bank[yb[c2]][:, :], diag[:, s], gring[:, s, D + 512 * c2:D + 512 * c2 + 512],
                                              start=False, stop=True, skip_group_check=True)
                            last.then_inc(g_used, 1)
                for c2 in range(2):
                    last = mm(bank[yb[c2]][:, :], ident, zrow, start=False, stop=True, skip_group_check=True)
                last.then_inc(y_sum, 1)
            x3_columns(NT - 1)
            ple_gate(NT - 1, 0)
            yb = Y_BANKS[NT % 2]
            pe.wait_ge(diag_ready, NT * 64 + 1)
            for r in range(8):
                for c2 in range(2):
                    last = mm(bank[yb[c2]][0:NB, :], diag[:, r, 0:NB], gring[:, r, D + 512 * c2:D + 512 * c2 + 512],
                              start=(r == 0), stop=(r == 7), skip_group_check=True)
            mm(bank[yb[1]][0:NB, :], ident[:, 0:NB], zrow, start=False, stop=True, skip_group_check=True).then_inc(y_sum, 1)
            ple_gate(NT - 1, 1)
            x3_columns(NT)
            ple_embedding(NT - 1)
            ple_gate(NT, 0)
            ple_gate(NT, 1)
            ple_embedding(NT)


def kernel(x_prompt, x_sample, p_prompt, p_sample, cache_k, cache_v, state_gla, page_table, norm1_g, w_in, b_gate,
           qa_norm_g, ka_norm_g, sb_bias, w_alpha, b_alpha, ob_norm_g, w_up_a, w_up_b, w_o, norm2_g, w_peer_q,
           peer_sub_keys, expert_u, expert_v, norm3_g, w_ple, w_ple_gate):
    import concourse.bacc as bacc
    from concourse.bass_utils import run_bass_kernel_spmd

    n = np.asarray

    def tiles(w):
        k, m = w.shape[0] // P, w.shape[1] // P
        return w.reshape(k, P, m, P).transpose(2, 1, 0, 3).reshape(m, P, k * P)

    def by_pairs(w):
        j = w.shape[1] // 512
        return w.reshape(4, 2, P, j, 512).transpose(3, 0, 2, 1, 4).reshape(4 * j, P, 1024)

    def by_feature(a):
        return a.reshape(a.shape[0], -1, P).transpose(2, 1, 0)

    wi = n(w_in)[0]
    cut = np.cumsum([512, 512, 512, 256, 256, 512, 512, 16, 1024, 1024])
    qa, ka, va, qb, kb, vb, rb, ab, gza, gzb = np.split(wi, cut[:-1], axis=1)
    up = np.stack([tiles(n(w_up_a)[0]), tiles(n(w_up_b)[0])], axis=2)
    w_stream = np.concatenate([
        tiles(qa), tiles(ka), tiles(qb), tiles(kb), by_pairs(va), by_pairs(vb), tiles(rb), tiles(gza), tiles(gzb),
        up.reshape(8, P, 1024), by_pairs(n(w_o)[0]), tiles(n(w_peer_q)[0])])
    col = lambda a: a.reshape(-1, P).T
    vecs = np.concatenate([
        col(n(norm1_g)[0]), np.tile(n(qa_norm_g)[0], 2)[:, None], np.tile(n(ka_norm_g)[0], 2)[:, None],
        col(n(b_alpha)[0]), col(n(b_gate)[0].reshape(-1)), n(ob_norm_g)[0][:, None]], axis=1)
    x = np.concatenate([n(x_prompt)[0], n(x_sample)[:, 0]])
    p = np.concatenate([n(p_prompt)[0, 0], n(p_sample)[0, :, 0]])
    feeds = {
        "consts": _consts(),
        "vecs": vecs,
        "xT": by_feature(x),
        "x_rows": x,
        "w_ab": ab.reshape(KD, P, RANK).transpose(1, 0, 2),
        "w_alpha": n(w_alpha)[0],
        "sb_bias": n(sb_bias)[0],
        "w_stream": w_stream,
        "cache_k": n(cache_k)[0].reshape(-1, P, PAGE_ROW),
        "cache_v": n(cache_v)[0].reshape(-1, P, PAGE_ROW),
        "page_table": n(page_table).reshape(1, -1),
        "state": n(state_gla)[0].reshape(NB, 2, 2 * GDK, GDV).transpose(2, 0, 1, 3),
        "norm2_g": n(norm2_g)[0],
        "norm3_g": n(norm3_g)[0],
        "sub_keysT": n(peer_sub_keys)[0].reshape(16, NKEYS, P).transpose(2, 0, 1),
        "experts": np.concatenate([n(expert_u)[0], n(expert_v)[0]], axis=1),
        "pT": by_feature(p),
        "w_ple": n(w_ple)[0].reshape(2, P, D).transpose(1, 0, 2),
        "w_ple_gate": n(w_ple_gate)[0].reshape(KD, P, D).transpose(1, 0, 2),
    }
    outs = {"y": (T, D), "new_kT": (512, T), "new_v": (T, 512), "gla_prompt": (P, 2, GDV), "gla_sample": (P, NB, 2, GDV)}
    nc = bacc.Bacc("TRN2", target_bir_lowering=False, num_devices=1)
    aps, arrays = {}, {}
    for name, a in feeds.items():
        arrays[name + "_in"] = np.ascontiguousarray(a)
        aps[name] = nc.dram_tensor(name + "_in", a.shape, mybir.dt.from_np(a.dtype), kind="ExternalInput").ap()
    for name, shape in outs.items():
        aps[name] = nc.dram_tensor(name + "_out", shape, F32, kind="ExternalOutput").ap()
    build(nc, aps)
    r = run_bass_kernel_spmd(nc, [arrays], core_ids=[0]).results[0]
    y, kT, v = r["y_out"], r["new_kT_out"], r["new_v_out"]
    k = kT.T.reshape(T, H, HD)
    v = v.reshape(T, H, HD)
    sp = r["gla_prompt_out"].reshape(2, GDK, 2, GDV).transpose(2, 0, 1, 3).reshape(1, 1, GH, GDK, GDV)
    ss = r["gla_sample_out"].reshape(2, GDK, NB, 2, GDV).transpose(2, 3, 0, 1, 4).reshape(1, NB, GH, GDK, GDV)
    return (y[None, :SEQ], y[SEQ:, None], k[None, None, :SEQ], v[None, None, :SEQ], sp,
            k[None, SEQ:, None], v[None, SEQ:, None], ss)
```
